# Optimizing a Trainium2 kernel written in Bass

```python
import jax, jax.numpy as jnp
from jax import lax
import numpy as np

D_MODEL = 1024
BATCH = 1
SEQ = 1024
DEPTH = 1
DEC_BATCH = 8
DEC_SEQ = 4
PAST_LEN = 4096
PAGE_SIZE = 128

N_META = 16
N_HEADS = 8
QK_NOPE = 64
QK_ROPE = 32
V_HEAD = 64
QK_HEAD = QK_NOPE + QK_ROPE
Q_LORA = 384
KV_LORA = 256
ATTN_WIDTH = N_HEADS * V_HEAD
CONV_CH = D_MODEL - ATTN_WIDTH
CONV_GROUPS = 8
CONV_W = 3
D_FF = 4 * D_MODEL
IN_WIDTH = Q_LORA + KV_LORA + QK_ROPE + 3 * CONV_CH
ROPE_THETA = 10000.0
EPS = 1e-6
Q_BLOCK = 128
ATTN_SCALE = QK_HEAD ** -0.5

kernel_name = "hymba_mla_shortconv_decode_step"

def _rmsnorm(x, g):
    xf = x.astype(jnp.float32)
    y = xf * lax.rsqrt(jnp.mean(xf * xf, axis=-1, keepdims=True) + EPS)
    return (y * g.astype(jnp.float32)).astype(x.dtype)

def _rope_tables(pos):
    inv_freq = ROPE_THETA ** (-(jnp.arange(0, QK_ROPE, 2, dtype=jnp.float32) / QK_ROPE))
    ang = pos.astype(jnp.float32)[:, None] * inv_freq[None, :]
    return jnp.cos(ang), jnp.sin(ang)

def _apply_rope(x, cos, sin):
    xf = x.astype(jnp.float32)
    x1, x2 = xf[..., : QK_ROPE // 2], xf[..., QK_ROPE // 2:]
    out = jnp.concatenate([x1 * cos - x2 * sin, x2 * cos + x1 * sin], axis=-1)
    return out.astype(x.dtype)

def _mixer_inputs(h, w_in, q_lora_g, kv_lora_g, w_uq, q_norm_g, cos, sin):
    B, T = h.shape[0], h.shape[1]
    z = h @ w_in
    o1 = Q_LORA
    o2 = o1 + KV_LORA
    o3 = o2 + QK_ROPE
    o4 = o3 + CONV_CH
    o5 = o4 + CONV_CH
    cq, ckv, kpe = z[..., :o1], z[..., o1:o2], z[..., o2:o3]
    gb, gc, hc = z[..., o3:o4], z[..., o4:o5], z[..., o5:]
    q = (_rmsnorm(cq, q_lora_g) @ w_uq).reshape(B, T, N_HEADS, QK_HEAD)
    q_pe = _apply_rope(q[..., QK_NOPE:], cos[:, None, :], sin[:, None, :])
    q = _rmsnorm(jnp.concatenate([q[..., :QK_NOPE], q_pe], axis=-1), q_norm_g)
    lat = _rmsnorm(ckv, kv_lora_g)
    k_pe = _apply_rope(kpe, cos, sin)
    u = gc * hc
    return q, lat, k_pe, gb, u

def _expand_kv(lat, k_pe, w_ukv, k_norm_g):
    kv = (lat @ w_ukv).reshape(lat.shape[:-1] + (N_HEADS, QK_NOPE + V_HEAD))
    k_nope, v = kv[..., :QK_NOPE], kv[..., QK_NOPE:]
    k_rot = jnp.broadcast_to(k_pe[..., None, :], k_nope.shape[:-1] + (QK_ROPE,))
    k = _rmsnorm(jnp.concatenate([k_nope, k_rot], axis=-1), k_norm_g)
    return k, v

def _prompt_attention(q, k, v):
    B, T = q.shape[0], q.shape[1]
    nb = -(-T // Q_BLOCK)
    Tp = nb * Q_BLOCK
    pad = ((0, 0), (0, Tp - T), (0, 0), (0, 0))
    q, k, v = jnp.pad(q, pad), jnp.pad(k, pad), jnp.pad(v, pad)
    qb = q.reshape(B, nb, Q_BLOCK, N_HEADS, QK_HEAD).transpose(1, 0, 2, 3, 4)
    kpos = jnp.arange(Tp)

    def block(args):
        qblk, i = args
        qpos = i * Q_BLOCK + jnp.arange(Q_BLOCK)
        s = jnp.einsum('bqhd,bkhd->bhqk', qblk, k).astype(jnp.float32) * ATTN_SCALE
        s = jnp.where(kpos[None, :] <= qpos[:, None], s, -jnp.inf)
        p = jax.nn.softmax(s, axis=-1).astype(v.dtype)
        return jnp.einsum('bhqk,bkhd->bqhd', p, v)

    out = lax.map(block, (qb, jnp.arange(nb)))
    out = out.transpose(1, 0, 2, 3, 4).reshape(B, Tp, N_HEADS, V_HEAD)
    return out[:, :T]

def _sample_attention(q, lat_new, kpe_new, page_table, cache_lat, cache_kpe, w_ukv, k_norm_g):
    S = q.shape[1]
    past = page_table.shape[1] * PAGE_SIZE
    L = past + S
    kidx = jnp.arange(L)
    qidx = past + jnp.arange(S)
    mask = kidx[None, :] <= qidx[:, None]

    def one(args):
        pages, qs, lat, kp = args
        lat_all = jnp.concatenate([cache_lat[pages].reshape(past, KV_LORA), lat], axis=0)
        kp_all = jnp.concatenate([cache_kpe[pages].reshape(past, QK_ROPE), kp], axis=0)
        k, v = _expand_kv(lat_all, kp_all, w_ukv, k_norm_g)
        s = jnp.einsum('qhd,khd->hqk', qs, k).astype(jnp.float32) * ATTN_SCALE
        s = jnp.where(mask[None], s, -jnp.inf)
        p = jax.nn.softmax(s, axis=-1).astype(v.dtype)
        return jnp.einsum('hqk,khd->qhd', p, v)

    return lax.map(one, (page_table, q, lat_new, kpe_new))

def _short_conv(u_padded, gb, conv_w, conv_b):
    T = gb.shape[1]
    y = conv_b
    for j in range(CONV_W):
        y = y + u_padded[:, j:j + T] * conv_w[j]
    return gb * y

def _merge_and_ffn(x, attn, conv, attn_out_g, conv_out_g, w_o, norm_ffn_g, w_up, w_down):
    B, T = x.shape[0], x.shape[1]
    mix = jnp.concatenate([_rmsnorm(attn.reshape(B, T, ATTN_WIDTH), attn_out_g),
                           _rmsnorm(conv, conv_out_g)], axis=-1)
    x = x + mix @ w_o
    hf = _rmsnorm(x, norm_ffn_g)
    return x + jnp.square(jax.nn.relu(hf @ w_up)) @ w_down

def setup_inputs(seed: int = 0) -> dict:
    key = jax.random.key(seed)
    ks = jax.random.split(key, 24)
    n_pages = PAST_LEN // PAGE_SIZE
    n_pool = (DEC_BATCH * n_pages * 5) // 4
    f32 = jnp.float32

    def nrm(k, shape, scale):
        return jax.random.normal(k, shape, f32) * scale

    def gain(k, shape):
        return 1.0 + 0.02 * jax.random.normal(k, shape, f32)

    page_table = jax.random.permutation(ks[5], n_pool)[: DEC_BATCH * n_pages]
    page_table = page_table.reshape(DEC_BATCH, n_pages).astype(jnp.int32)
    return {
        "x_prompt": nrm(ks[0], (BATCH, SEQ, D_MODEL), 1.0),
        "x_sample": nrm(ks[1], (DEC_BATCH, DEC_SEQ, D_MODEL), 1.0),
        "cache_kv_latent": nrm(ks[2], (DEPTH, n_pool, PAGE_SIZE, KV_LORA), 1.0),
        "cache_k_rope": nrm(ks[3], (DEPTH, n_pool, PAGE_SIZE, QK_ROPE), 1.0),
        "state_conv": nrm(ks[4], (DEPTH, DEC_BATCH, CONV_W - 1, CONV_CH), 1.0),
        "page_table": page_table,
        "meta_tokens": nrm(ks[6], (N_META, D_MODEL), 1.0),
        "norm_mix_g": gain(ks[7], (DEPTH, D_MODEL)),
        "w_in": nrm(ks[8], (DEPTH, D_MODEL, IN_WIDTH), D_MODEL ** -0.5),
        "q_lora_g": gain(ks[9], (DEPTH, Q_LORA)),
        "kv_lora_g": gain(ks[10], (DEPTH, KV_LORA)),
        "w_uq": nrm(ks[11], (DEPTH, Q_LORA, N_HEADS * QK_HEAD), Q_LORA ** -0.5),
        "w_ukv": nrm(ks[12], (DEPTH, KV_LORA, N_HEADS * (QK_NOPE + V_HEAD)), KV_LORA ** -0.5),
        "q_norm_g": gain(ks[13], (DEPTH, QK_HEAD)),
        "k_norm_g": gain(ks[14], (DEPTH, QK_HEAD)),
        "conv_w": nrm(ks[15], (DEPTH, CONV_W, CONV_CH), CONV_W ** -0.5),
        "conv_b": nrm(ks[16], (DEPTH, CONV_CH), 0.01),
        "attn_out_g": gain(ks[17], (DEPTH, ATTN_WIDTH)),
        "conv_out_g": gain(ks[18], (DEPTH, CONV_CH)),
        "w_o": nrm(ks[19], (DEPTH, D_MODEL, D_MODEL), D_MODEL ** -0.5),
        "norm_ffn_g": gain(ks[20], (DEPTH, D_MODEL)),
        "w_up": nrm(ks[21], (DEPTH, D_MODEL, D_FF), D_MODEL ** -0.5),
        "w_down": nrm(ks[22], (DEPTH, D_FF, D_MODEL), D_FF ** -0.5),
    }

def reference(x_prompt, x_sample, cache_kv_latent, cache_k_rope, state_conv, page_table, meta_tokens,
              norm_mix_g, w_in, q_lora_g, kv_lora_g, w_uq, w_ukv, q_norm_g, k_norm_g, conv_w, conv_b,
              attn_out_g, conv_out_g, w_o, norm_ffn_g, w_up, w_down):
    B = x_prompt.shape[0]
    meta = jnp.broadcast_to(meta_tokens[None].astype(x_prompt.dtype), (B, N_META, D_MODEL))
    xp = jnp.concatenate([meta, x_prompt], axis=1)
    xs = x_sample
    Tp = xp.shape[1]
    S = xs.shape[1]
    past = page_table.shape[1] * PAGE_SIZE
    cos_p, sin_p = _rope_tables(jnp.arange(Tp))
    cos_s, sin_s = _rope_tables(past + jnp.arange(S))

    lat_p_all, kpe_p_all, conv_p_all = [], [], []
    lat_s_all, kpe_s_all, conv_s_all = [], [], []
    for l in range(DEPTH):
        hp = _rmsnorm(xp, norm_mix_g[l])
        q, lat, kpe, gb, u = _mixer_inputs(hp, w_in[l], q_lora_g[l], kv_lora_g[l], w_uq[l],
                                           q_norm_g[l], cos_p, sin_p)
        k, v = _expand_kv(lat, kpe, w_ukv[l], k_norm_g[l])
        attn = _prompt_attention(q, k, v)
        up = jnp.concatenate([jnp.zeros((B, CONV_W - 1, CONV_CH), u.dtype), u], axis=1)
        conv = _short_conv(up, gb, conv_w[l], conv_b[l])
        xp = _merge_and_ffn(xp, attn, conv, attn_out_g[l], conv_out_g[l], w_o[l],
                            norm_ffn_g[l], w_up[l], w_down[l])
        lat_p_all.append(lat)
        kpe_p_all.append(kpe)
        conv_p_all.append(up[:, -(CONV_W - 1):])

        hs = _rmsnorm(xs, norm_mix_g[l])
        q, lat, kpe, gb, u = _mixer_inputs(hs, w_in[l], q_lora_g[l], kv_lora_g[l], w_uq[l],
                                           q_norm_g[l], cos_s, sin_s)
        attn = _sample_attention(q, lat, kpe, page_table, cache_kv_latent[l], cache_k_rope[l],
                                 w_ukv[l], k_norm_g[l])
        us = jnp.concatenate([state_conv[l].astype(u.dtype), u], axis=1)
        conv = _short_conv(us, gb, conv_w[l], conv_b[l])
        xs = _merge_and_ffn(xs, attn, conv, attn_out_g[l], conv_out_g[l], w_o[l],
                            norm_ffn_g[l], w_up[l], w_down[l])
        lat_s_all.append(lat)
        kpe_s_all.append(kpe)
        conv_s_all.append(us[:, -(CONV_W - 1):])

    y_prompt = xp[:, N_META:]
    y_sample = xs
    return (y_prompt, y_sample,
            jnp.stack(lat_p_all), jnp.stack(kpe_p_all), jnp.stack(conv_p_all),
            jnp.stack(lat_s_all), jnp.stack(kpe_s_all), jnp.stack(conv_s_all))


_drawn_inputs = setup_inputs


def setup_inputs(seed=0):
    import zlib

    import numpy as np

    out = dict(_drawn_inputs(seed))
    spreads = {}
    factors = {'q_lora_g': 5.518,
     'kv_lora_g': 2.743,
     'q_norm_g': 5.0,
     'k_norm_g': 5.673,
     'conv_b': 8.0,
     'attn_out_g': 5.557,
     'conv_out_g': 5.442,
     'norm_ffn_g': 3.902}
    for name, (base, spread) in spreads.items():
        noise = np.random.default_rng([zlib.crc32(name.encode()), seed]).standard_normal(out[name].shape)
        drawn = base * np.exp(spread * noise) if base else spread * noise
        out[name] = __import__('jax').numpy.asarray(drawn.astype(out[name].dtype))
    for name, factor in factors.items():
        out[name] = (out[name] * factor).astype(out[name].dtype)
    return out
```

```python
from contextlib import ExitStack

import concourse.bass as bass
from concourse import mybir

F32 = mybir.dt.float32
F32R = mybir.dt.float32r
I32 = mybir.dt.int32
ALU = mybir.AluOpType
ACT = mybir.ActivationFunctionType
AX_X = mybir.AxisListType.X
ds = bass.ds

P = 128
D = 1024
KD = D // P
META, SEQ = 16, 1024
TP = META + SEQ
NSEQ, SDEC = 8, 4
NS = NSEQ * SDEC
T = TP + NS
NBLK = 3
TB = 2 * -(-T // (2 * NBLK))
TT = NBLK * TB
PAGE, NPAGES, PAST = 128, 32, 4096
H, NOPE, ROPE, VH = 8, 64, 32, 64
QK = NOPE + ROPE
QL, KVL = 384, 256
KQ, KL = QL // P, KVL // P
AW = H * VH
CW = D - AW
KC = CW // P
DFF = 4 * D
EPS = 1e-6
SCALE = QK ** -0.5
NT = -(-T // P)
TQ = NT * P
BANK = 512
MASKED = -1.0e30

G_MIX, G_QL, G_KVL = 0, 8, 11
G_ATT, G_CONV, G_FFN = 13, 17, 21
G_CW, G_CB = 29, 41
G_QN, G_KN = 45, 46
G_ROWS = 47

Z_CQ, Z_CKV, Z_KPE, Z_GB, Z_GC, Z_HC = 0, 3, 5, 6, 10, 14
NZ = 18


class Shared:

    def __init__(self, nc, arrays, banks):
        self.nc, self.A, self.banks = nc, arrays, banks


class Arena:

    def __init__(self, nc, start, end):
        self.nc, self.at, self.end = nc, start, end

    def take(self, name, shape, dtype):
        size = 4
        for n in shape[1:]:
            size *= n
        t = self.nc.alloc_sbuf_tensor_at(name, shape, dtype, offset=self.at)
        self.at += -(-size // 32) * 32
        assert self.at <= self.end, (name, self.at, self.end)
        return t

    def skip(self, size):
        a = self.at
        self.at += -(-size // 32) * 32
        assert self.at <= self.end
        return a


def norm_scratch(name, arena):
    return (arena.take(f"{name}_sq", [P, 2, TT], F32), arena.take(f"{name}_ms", [P, TT], F32),
            arena.take(f"{name}_scaled", [P, 2, TT], F32))


class Norm:

    def __init__(self, nc, sem, name, scratch, src, K, width, gain, hi, lo, ss, ones, full=None):
        self.nc, self.src, self.K, self.width, self.gain = nc, src, K, width, gain
        self.hi, self.lo, self.ss, self.ones, self.full = hi, lo, ss, ones, full
        self.sq, self.ms, self.scaled = scratch
        self.squared = sem(f"{name}_squared")
        self.summed = sem(f"{name}_summed")
        self.mean = sem(f"{name}_mean")
        self.root = sem(f"{name}_root")
        self.inv = sem(f"{name}_inv")
        self.norm = sem(f"{name}_norm")
        self.hi_done = sem(f"{name}_hi_done")
        self.lo_done = sem(f"{name}_lo_done")

    def act(self, act):
        for c in range(self.K):
            if c >= 2:
                act.wait_ge(self.summed, c - 1)
            act.activation(self.sq[:, c % 2, :], self.src(c), ACT.Square).then_inc(self.squared, 1)
        act.wait_ge(self.mean, 1)
        act.activation(self.ms[:, :], self.ms[:, :], ACT.Sqrt).then_inc(self.root, 1)
        for c in range(self.K):
            act.wait_ge(self.norm, c + 1)
            act.copy(self.hi(c), self.buf(c)).then_inc(self.hi_done, 1)

    def pe(self, pe):
        for c in range(self.K):
            pe.wait_ge(self.squared, c + 1)
            for b in range(NBLK):
                mm = pe.matmul(self.ss[:, b, 0:TB], self.ones[:, :], self.sq[:, c % 2, b * TB:(b + 1) * TB],
                               start=c == 0, stop=c == self.K - 1)
            mm.then_inc(self.summed, 1)

    def buf(self, c):
        return self.full(c) if self.full else self.scaled[:, c % 2, :]

    def dve(self, v):
        nc = self.nc
        v.wait_ge(self.summed, self.K)
        nc.vector.tensor_scalar(self.ms[:, :].rearrange("p (b t) -> p b t", b=NBLK), self.ss[:, :, 0:TB],
                                1.0 / self.width, EPS, ALU.mult, ALU.add).then_inc(self.mean, 1)
        v.wait_ge(self.root, 1)
        nc.vector.reciprocal(self.ms[:, :], self.ms[:, :]).then_inc(self.inv, 1)
        v.wait_ge(self.inv, 1)
        for c in range(self.K):
            if c >= 2 and not self.full:
                v.wait_ge(self.lo_done, c - 1)
            nc.vector.scalar_tensor_tensor(self.buf(c), self.src(c), self.gain(c), self.ms[:, :],
                                           ALU.mult, ALU.mult).then_inc(self.norm, 1)

    def pool(self, pool):
        for c in range(self.K):
            pool.wait_ge(self.hi_done, c + 1)
            self.nc.gpsimd.tensor_sub(self.lo(c), self.buf(c), self.hi(c).bitcast(F32)).then_inc(self.lo_done, 1)


class Ring:

    def __init__(self, sem, name, arena, K, slots=2):
        self.K = K
        self.raw = [arena.take(f"{name}_raw{s}", [P, K, P], F32) for s in range(slots)]
        self.hi = [arena.take(f"{name}_hi{s}", [P, K, P], F32R) for s in range(slots)]
        self.lo = [arena.take(f"{name}_lo{s}", [P, K, P], F32R) for s in range(slots)]
        self.loaded = [sem(f"{name}_loaded{s}") for s in range(slots)]
        self.hi_done = [sem(f"{name}_hi_done{s}") for s in range(slots)]
        self.lo_done = [sem(f"{name}_lo_done{s}") for s in range(slots)]
        self.used = [sem(f"{name}_used{s}") for s in range(slots)]
        self.evacuated = [sem(f"{name}_evacuated{s}") for s in range(slots)]

    def open(self, engine, semaphores):
        for x in semaphores:
            engine.sem_inc(x, 1)

    def split_hi(self, act, s, n, loads=1):
        act.wait_ge(self.loaded[s], (n + 1) * (16 * loads))
        act.wait_ge(self.used[s], n + 1)
        act.copy(self.hi[s][:, :, :], self.raw[s][:, :, :]).then_inc(self.hi_done[s], 1)

    def split_lo(self, nc, pool, s, n):
        pool.wait_ge(self.hi_done[s], n + 1)
        nc.gpsimd.tensor_sub(self.lo[s][:, :, :], self.raw[s][:, :, :],
                             self.hi[s][:, :, :].bitcast(F32)).then_inc(self.lo_done[s], 1)

    def products(self, pe, s, n, out, xhi, xlo, first=None):
        pe.wait_ge(self.lo_done[s], n + 2)
        for k in range(self.K):
            if first is not None:
                first(k)
            for w, x, a in ((self.hi, xhi, 0), (self.hi, xlo, 1), (self.lo, xhi, 2)):
                for b in range(NBLK):
                    mm = pe.matmul(out[:, b, 0:TB], w[s][:, k, :], x(k)[:, b * TB:(b + 1) * TB],
                                   start=k == 0 and a == 0, stop=k == self.K - 1 and a == 2)
        mm.then_inc(self.used[s], 1)


def program(nc, A):
    ctx = ExitStack()
    with ctx:
        def sem(name):
            return ctx.enter_context(nc.semaphore(name))

        banks = ctx.enter_context(nc.psum_tensor("banks", [P, 8, BANK], F32))
        g = Shared(nc, A, banks)
        g.done = sem("stores_done")
        low = -(-nc.sbuf_base // 32) * 32
        top = nc.sbuf_usable_end // 32 * 32
        fixed = Arena(nc, low, top)
        g.ident = fixed.take("ident", [P, P], F32)
        g.ones = fixed.take("ones", [P, P], F32)
        g.gcol = fixed.take("gain_columns", [P, G_ROWS], F32)
        g.cs = fixed.take("cos_sin", [P, TT], F32)
        g.xT = fixed.take("xT", [P, KD, TT], F32)
        g.start, g.top = fixed.at, top
        U = TT * 4
        g.h_at = top - 16 * U
        g.z_at = g.start
        for phase in (load_inputs, project_inputs, norms_and_conv, prompt_attention, sample_attention,
                      output_projection, mlp, store_outputs):
            own = []

            def own_semaphore(name):
                own.append(nc.alloc_semaphore(f"{phase.__name__}_{name}"))
                return own[-1]

            g.sem = own_semaphore
            phase(g)
            nc.clear_and_free_semaphores(own)
            nc.all_engine_barrier()


def load_inputs(g):
    nc, A, sem = g.nc, g.A, g.sem
    ar = Arena(nc, g.start, g.h_at)
    top = Arena(nc, g.h_at, g.top)
    g.h_hi = top.take("h_hi", [P, KD, TT], F32R)
    g.h_lo = top.take("h_lo", [P, KD, TT], F32R)
    xt = [ar.take(f"x_tile{i}", [P, D], F32) for i in range(3)]
    grow = ar.take("gain_rows", [G_ROWS, P], F32)
    x_loaded = [sem(f"x_loaded{i}") for i in range(3)]
    gains_loaded, table_loaded = sem("gains_loaded"), sem("table_loaded")
    gains_zeroed, consts = sem("gains_zeroed"), sem("consts")
    x_transposed = sem("x_transposed")
    low_copied, high_copied = sem("low_chunks_copied"), sem("high_chunks_copied")
    g_transposed, g_copied = sem("g_transposed"), sem("g_copied")
    xT, ident, banks = g.xT, g.ident, g.banks
    gbank = banks[:, 7, 0:G_ROWS]
    norm = Norm(nc, sem, "mixnorm", norm_scratch("mixnorm", ar), lambda c: xT[:, c, :], KD, D, lambda c: g.gcol[:, G_MIX + c:G_MIX + c + 1],
                lambda c: g.h_hi[:, c, :], lambda c: g.h_lo[:, c, :], banks[:, 4:7, :], g.ones)
    parts = []
    for t in range(NT):
        at, rows = t * P, min(P, T - t * P)
        p = []
        for name, first, n in (("meta_tokens", 0, META), ("x_prompt", META, SEQ), ("x_sample", TP, NS)):
            a, b = max(at, first), min(at + rows, first + n)
            if a < b:
                p.append((a - at, b - at, A[name][a - first:b - first, :]))
        parts.append((rows, p))
    ends = [0, 0, 0]
    loaded_at = []
    for t, (_, p) in enumerate(parts):
        ends[t % 3] += 16 * len(p)
        loaded_at.append(ends[t % 3])

    with nc.Block() as block:
        @block.sync
        def _(sp):
            for t, (_, p) in enumerate(parts):
                if t >= 3:
                    sp.wait_ge(x_transposed, t - 2)
                for a, b, src in p:
                    sp.dma_start(xt[t % 3][a:b, :], src).then_inc(x_loaded[t % 3], 16)

        @block.gpsimd
        def _(pool):
            nc.gpsimd.memset(ident[:, :], 0.0).then_inc(consts, 1)
            nc.gpsimd.memset(g.ones[:, :], 1.0).then_inc(consts, 1)
            nc.gpsimd.memset(xT[:, :, T:TT], 0.0).then_inc(consts, 1)
            pool.wait_ge(consts, 3)
            nc.gpsimd.affine_select(out=ident[:, :], in_=ident[:, :], compare_op=ALU.not_equal, fill=1.0, base=0,
                                    pattern=[[-1, P]], channel_multiplier=1).then_inc(consts, 1)
            norm.pool(pool)

        @block.scalar
        def _(act):
            act.wait_ge(gains_zeroed, 1)
            for name, row in (("norm_mix_g", G_MIX), ("q_lora_g", G_QL), ("kv_lora_g", G_KVL), ("attn_out_g", G_ATT),
                              ("conv_out_g", G_CONV), ("norm_ffn_g", G_FFN), ("conv_w", G_CW), ("conv_b", G_CB)):
                v = A[name].rearrange("(k p) -> k p", p=P)
                act.dma_start(grow[row:row + v.shape[0], :], v).then_inc(gains_loaded, 16)
            for name, row in (("q_norm_g", G_QN), ("k_norm_g", G_KN)):
                act.dma_start(grow[row:row + 1, 0:QK], A[name].rearrange("(o n) -> o n", o=1)).then_inc(gains_loaded, 16)
            act.dma_start(g.cs[NOPE:P, :], A["rope_table"]).then_inc(table_loaded, 16)
            for t in range(NT):
                rows = parts[t][0]
                act.wait_ge(x_transposed, t + 1)
                act.copy(xT[:, 0:KD // 2, t * P:t * P + rows],
                         banks[:, 2 * (t % 2), :].rearrange("p (k t) -> p k t", t=P)[:, :, 0:rows]).then_inc(low_copied, 1)
            act.wait_ge(low_copied, NT)
            act.wait_ge(high_copied, NT)
            act.wait_ge(consts, 3)
            norm.act(act)
            act.wait_ge(table_loaded, 16)

        @block.vector
        def _(v):
            nc.vector.memset(grow[:, :], 0.0).then_inc(gains_zeroed, 1)
            for t in range(NT):
                rows = parts[t][0]
                v.wait_ge(x_transposed, t + 1)
                nc.vector.tensor_copy(xT[:, KD // 2:KD, t * P:t * P + rows],
                                      banks[:, 2 * (t % 2) + 1, :].rearrange("p (k t) -> p k t", t=P)[:, :, 0:rows])\
                    .then_inc(high_copied, 1)
            v.wait_ge(g_transposed, 1)
            nc.vector.tensor_copy(g.gcol[:, :], gbank).then_inc(g_copied, 1)
            v.wait_ge(g_copied, 1)
            norm.dve(v)

        @block.tensor
        def _(pe):
            pe.wait_ge(consts, 4)
            for t in range(NT):
                rows = parts[t][0]
                pe.wait_ge(x_loaded[t % 3], loaded_at[t])
                if t >= 2:
                    pe.wait_ge(low_copied, t - 1)
                    pe.wait_ge(high_copied, t - 1)
                for k in range(KD):
                    mm = pe.transpose(banks[:, 2 * (t % 2) + k // 4, (k % 4) * P:(k % 4) * P + rows],
                                      xt[t % 3][0:rows, k * P:(k + 1) * P], ident[0:rows, 0:rows])
                mm.then_inc(x_transposed, 1)
            pe.wait_ge(gains_loaded, 16 * 10)
            pe.transpose(gbank, grow[:, :], ident[0:G_ROWS, 0:G_ROWS]).then_inc(g_transposed, 1)
            norm.pe(pe)


def project_inputs(g):
    nc, A, sem = g.nc, g.A, g.sem
    ar = Arena(nc, g.z_at, g.h_at)
    g.zT = ar.take("zT", [P, NZ, TT], F32)
    g.z_end = ar.at
    g.conv_at = g.z_at + Z_GB * TT * 4
    g.z_hc_at = g.z_at + -(-Z_GC * TT * 4 // 32) * 32
    ring = Ring(sem, "w_in", ar, KD)
    zT, banks = g.zT, g.banks
    w = A["w_in"].rearrange("(k p) n -> p k n", p=P)
    kpe0 = QL + KVL
    half = ROPE // 2

    with nc.Block() as block:
        @block.sync
        def _(sp):
            def free(s, n):
                sp.wait_ge(ring.lo_done[s], n + 1)

            for n in range(2):
                for s in range(2):
                    free(s, n)
                    c = 2 * n + s
                    sp.dma_start(ring.raw[s][:, :, :], w[:, :, c * P:(c + 1) * P]).then_inc(ring.loaded[s], 16)
            free(0, 2)
            sp.dma_start(ring.raw[0][:, :, :], w[:, :, 4 * P:5 * P]).then_inc(ring.loaded[0], 16)
            free(1, 2)
            for at in (0, 2 * ROPE):
                sp.dma_start(ring.raw[1][:, :, at:at + ROPE], w[:, :, kpe0:kpe0 + ROPE]).then_inc(ring.loaded[1], 16)
                sp.dma_start(ring.raw[1][:, :, at + ROPE:at + ROPE + half],
                             w[:, :, kpe0 + half:kpe0 + ROPE]).then_inc(ring.loaded[1], 16)
                sp.dma_start(ring.raw[1][:, :, at + ROPE + half:at + 2 * ROPE],
                             w[:, :, kpe0:kpe0 + half]).then_inc(ring.loaded[1], 16)
            with sp.Fori(3, NZ // 2) as i:
                for s in range(2):
                    free(s, i)
                    sp.dma_start(ring.raw[s][:, :, :],
                                 w[:, :, ds(i * (2 * P) + (kpe0 + ROPE - 6 * P + s * P), P)])\
                        .then_inc(ring.loaded[s], 16)

        @block.scalar
        def _(act):
            def split(s, n, extra=0):
                act.wait_ge(ring.loaded[s], n * 16 + (16 + extra))
                act.wait_ge(ring.used[s], n + 1)
                act.copy(ring.hi[s][:, :, :], ring.raw[s][:, :, :]).then_inc(ring.hi_done[s], 1)

            for n in range(2):
                split(0, n)
                split(1, n)
            split(0, 2)
            split(1, 2, 5 * 16)
            with act.Fori(3, NZ // 2) as i:
                split(0, i)
                split(1, i, 5 * 16)

        @block.gpsimd
        def _(pool):
            ring.open(pool, ring.lo_done)
            with pool.Fori(0, NZ // 2) as i:
                for s in range(2):
                    ring.split_lo(nc, pool, s, i)

        @block.tensor
        def _(pe):
            ring.open(pe, ring.used)
            with pe.Fori(0, NZ // 2) as i:
                for s in range(2):
                    pe.wait_ge(ring.evacuated[s], i + 1)
                    ring.products(pe, s, i, banks[:, 3 * s:3 * s + 3, :],
                                  lambda k: g.h_hi[:, k, :], lambda k: g.h_lo[:, k, :])

        @block.vector
        def _(v):
            ring.open(v, ring.evacuated)
            with v.Fori(0, NZ // 2) as i:
                for s in range(2):
                    v.wait_ge(ring.used[s], i + 2)
                    nc.vector.tensor_copy(
                        zT[:, ds(i * 2 + s, 1), :].rearrange("p o (b t) -> p (o b) t", b=NBLK),
                        banks[:, 3 * s:3 * s + 3, 0:TB]).then_inc(ring.evacuated[s], 1)


def norms_and_conv(g):
    nc, A, sem, zT, banks, ident = g.nc, g.A, g.sem, g.zT, g.banks, g.ident
    keep = Arena(nc, g.h_at, g.top)
    g.cq_hi, g.cq_lo = keep.take("cq_hi", [P, KQ, TT], F32R), keep.take("cq_lo", [P, KQ, TT], F32R)
    g.lat_hi, g.lat_lo = keep.take("lat_hi", [P, KL, TT], F32R), keep.take("lat_lo", [P, KL, TT], F32R)
    g.lora_end = keep.at
    g.kpe = keep.take("key_rope", [P, TT], F32)
    g.new_latT = keep.take("new_latT", [P, KL, NS], F32)
    g.new_page = keep.take("new_page", [NS, KVL + ROPE], F32)
    g.qs = keep.take("q_sampled", [P, H, NS], F32)
    g.gg = keep.take("qk_gain", [P, 1], F32)
    g.p4_at = keep.at
    lat = keep.take("lat", [P, KL, TT], F32)
    rows = [keep.take(f"new_rows{i}", [P, KVL + ROPE], F32) for i in range(2)]
    ar = Arena(nc, g.z_end, g.h_at)
    scr = norm_scratch("lora_norms", ar)
    us = keep.take("u_sampled", [P, KC, NSEQ, SDEC + 2], F32)
    ends = keep.take("conv_ends", [P, KC, 2 * NSEQ + 2], F32)
    state = keep.take("state_rows", [2 * NSEQ, CW], F32)
    crows = keep.take("conv_rows", [2 * NSEQ + 2, CW], F32)

    kv = Norm(nc, sem, "kvnorm", scr, lambda c: zT[:, Z_CKV + c, :], KL, KVL,
              lambda c: g.gcol[:, G_KVL + c:G_KVL + c + 1], lambda c: g.lat_hi[:, c, :], lambda c: g.lat_lo[:, c, :],
              banks[:, 0:3, :], g.ones, full=lambda c: lat[:, c, :])
    cq = Norm(nc, sem, "cqnorm", scr, lambda c: zT[:, Z_CQ + c, :], KQ, QL,
              lambda c: g.gcol[:, G_QL + c:G_QL + c + 1], lambda c: g.cq_hi[:, c, :], lambda c: g.cq_lo[:, c, :],
              banks[:, 3:6, :], g.ones)
    state_loaded, state_transposed, state_copied = sem("state_loaded"), sem("state_transposed"), sem("state_copied")
    rope_cos, rope_sin, rope_done = sem("rope_cos"), sem("rope_sin"), sem("rope_done")
    gated, u_sampled, ends_done = sem("gated"), sem("u_sampled"), sem("ends_done")
    taps, conv_done = sem("taps"), sem("conv_done")
    ends_transposed, conv_rows_done = sem("ends_transposed"), sem("conv_rows_done")
    tile_transposed, tile_copied = sem("tile_transposed"), sem("tile_copied")
    new_copied, latT_copied = sem("new_page_copied"), sem("new_latT_copied")
    stored = [sem(f"tile_stored{i}") for i in range(2)]
    sb = banks[:, 6, :]
    tiles = [(t * P, min(P, TP - t * P)) for t in range(NT)] + [(TP, NS)]
    tsb = TT - 2
    cwc = lambda j, c: g.gcol[:, G_CW + KC * j + c:G_CW + KC * j + c + 1]
    scratch = zT[:, Z_KPE, :]

    with nc.Block() as block:
        @block.sync
        def _(sp):
            sp.dma_start(state[:, :], A["state_conv"]).then_inc(state_loaded, 16)
            for t, (at, n) in enumerate(tiles):
                src = rows[t % 2] if t < NT else g.new_page
                sp.wait_ge(tile_copied, t + 1)
                out, o = ("prompt", at) if t < NT else ("sample", 0)
                done = stored[t % 2]
                sp.dma_start(A[f"out_new_lat_{out}"][o:o + n, :], src[0:n, 0:KVL]).then_inc(done, 16)
                sp.dma_start(A[f"out_new_kpe_{out}"][o:o + n, :], src[0:n, KVL:KVL + ROPE]).then_inc(done, 16)
            sp.wait_ge(conv_rows_done, 1)
            sp.dma_start(A["out_new_conv_sample"].rearrange("b j c -> (b j) c"), crows[0:2 * NSEQ, :]).then_inc(g.done, 16)
            sp.dma_start(A["out_new_conv_prompt"], crows[2 * NSEQ:2 * NSEQ + 2, :]).then_inc(g.done, 16)
            sp.wait_ge(stored[0], 32 * ((NT + 2) // 2))
            sp.wait_ge(stored[1], 32 * ((NT + 1) // 2))
            sp.wait_ge(g.done, 32)

        @block.scalar
        def _(act):
            kv.act(act)
            cq.act(act)
            for t, (at, n) in enumerate(tiles):
                dst = rows[t % 2] if t < NT else g.new_page
                act.wait_ge(tile_transposed, t + 1)
                if t >= 2:
                    act.wait_ge(stored[t % 2], 32 * (t // 2))
                act.copy(dst[0:n, :], banks[0:n, t % 2, 0:KVL + ROPE]).then_inc(tile_copied, 1)
            act.wait_ge(ends_transposed, 1)
            act.copy(crows[:, :], banks[0:2 * NSEQ + 2, 7, :]).then_inc(conv_rows_done, 1)

        @block.gpsimd
        def _(pool):
            for c in range(KC):
                nc.gpsimd.tensor_mul(zT[:, Z_GC + c, :], zT[:, Z_GC + c, :], zT[:, Z_HC + c, :]).then_inc(gated, 1)
            kv.pool(pool)
            cq.pool(pool)

        @block.vector
        def _(v):
            nc.vector.tensor_mul(g.kpe[NOPE:QK, :], zT[NOPE:QK, Z_KPE, :], g.cs[NOPE:QK, :]).then_inc(rope_cos, 1)
            v.wait_ge(rope_cos, 1)
            nc.vector.tensor_mul(scratch[NOPE:QK, :], zT[QK:P, Z_KPE, :], g.cs[QK:P, :]).then_inc(rope_sin, 1)
            v.wait_ge(rope_sin, 1)
            nc.vector.tensor_add(g.kpe[NOPE:QK, :], g.kpe[NOPE:QK, :], scratch[NOPE:QK, :]).then_inc(rope_done, 1)
            kv.dve(v)
            v.wait_ge(kv.norm, KL)
            nc.vector.tensor_copy(g.new_latT[:, :, :], lat[:, :, TP:T]).then_inc(latT_copied, 1)
            cq.dve(v)
            v.wait_ge(gated, KC)
            v.wait_ge(state_transposed, 1)
            nc.vector.tensor_copy(us[:, :, :, 2:], zT[:, Z_GC:Z_GC + KC, TP:T].rearrange("p c (b s) -> p c b s", b=NSEQ))\
                .then_inc(u_sampled, 1)
            nc.vector.tensor_copy(us[:, :, :, 0:2], banks[:, 6, 0:KC * 2 * NSEQ]
                                  .rearrange("p (c b j) -> p c b j", c=KC, j=2)).then_inc(u_sampled, 1)
            v.wait_ge(u_sampled, 2)
            nc.vector.tensor_copy(ends[:, :, 0:2 * NSEQ].rearrange("p c (b j) -> p c b j", j=2), us[:, :, :, SDEC:])\
                .then_inc(ends_done, 1)
            nc.vector.tensor_copy(ends[:, :, 2 * NSEQ:], zT[:, Z_GC:Z_GC + KC, TP - 2:TP]).then_inc(ends_done, 1)
            n = 0
            for c in range(KC):
                y, u = zT[:, Z_HC + c, :], zT[:, Z_GC + c, :]
                yp, ys = y[:, 0:TP], y[:, TP:T].rearrange("p (b s) -> p b s", b=NSEQ)
                b = g.gcol[:, G_CB + c:G_CB + c + 1]
                nc.vector.tensor_scalar(y[:, 0:TP], u[:, 0:TP], cwc(2, c), b, ALU.mult, ALU.add).then_inc(taps, 1)
                nc.vector.tensor_scalar(ys, us[:, c, :, 2:2 + SDEC], cwc(2, c), b, ALU.mult, ALU.add).then_inc(taps, 1)
                n += 2
                for j in (1, 0):
                    sh = 2 - j
                    v.wait_ge(taps, n)
                    nc.vector.scalar_tensor_tensor(yp[:, sh:], u[:, 0:TP - sh], cwc(j, c), yp[:, sh:],
                                                   ALU.mult, ALU.add).then_inc(taps, 1)
                    nc.vector.scalar_tensor_tensor(ys, us[:, c, :, j:j + SDEC], cwc(j, c), ys,
                                                   ALU.mult, ALU.add).then_inc(taps, 1)
                    n += 2
                v.wait_ge(taps, n)
                nc.vector.tensor_mul(zT[:, Z_GB + c, 0:T], zT[:, Z_GB + c, 0:T], y[:, 0:T]).then_inc(conv_done, 1)
            v.wait_ge(conv_done, KC)

        @block.tensor
        def _(pe):
            pe.wait_ge(state_loaded, 16)
            for c in range(KC):
                mm = pe.transpose(banks[:, 6, c * 2 * NSEQ:(c + 1) * 2 * NSEQ], state[:, c * P:(c + 1) * P],
                                  ident[0:2 * NSEQ, 0:2 * NSEQ])
            mm.then_inc(state_transposed, 1)
            kv.pe(pe)
            cq.pe(pe)
            pe.wait_ge(rope_done, 1)
            pe.wait_ge(kv.norm, KL)
            pe.wait_ge(kv.mean, 1)
            for t, (at, n) in enumerate(tiles):
                if t >= 2:
                    pe.wait_ge(tile_copied, t - 1)
                for c in range(KL):
                    pe.transpose(banks[0:n, t % 2, c * P:(c + 1) * P], lat[:, c, at:at + n], ident[:, :])
                pe.transpose(banks[0:n, t % 2, KVL:KVL + ROPE], g.kpe[NOPE:QK, at:at + n], ident[NOPE:QK, NOPE:QK])\
                    .then_inc(tile_transposed, 1)
            pe.wait_ge(ends_done, 2)
            for c in range(KC):
                mm = pe.transpose(banks[0:2 * NSEQ + 2, 7, c * P:(c + 1) * P], ends[:, c, :], ident[:, :])
            mm.then_inc(ends_transposed, 1)


def prompt_attention(g):
    nc, A, sem, banks, ident = g.nc, g.A, g.sem, g.banks, g.ident
    low = Arena(nc, g.z_at, g.top)
    g.attnT = low.take("attnT", [P, AW // P, TT], F32)
    ar = Arena(nc, g.z_hc_at, g.h_at)
    qf, kf, part = (ar.take(n, [P, TT], F32) for n in ("q_raw", "k_raw", "rope_part"))
    sq_k, ms = ar.take("k_squares", [P, TT], F32), ar.take("k_inv", [P, TT], F32)
    sq_q = ar.take("q_squares", [P, TQ], F32)
    q_hi, q_lo = ar.take("q_hi", [P, TQ], F32R), ar.take("q_lo", [P, TQ], F32R)
    k_hi, k_lo = ar.take("k_hi", [P, TQ], F32R), ar.take("k_lo", [P, TQ], F32R)
    probs = [ar.take(f"probs{i}", [P, TQ], F32) for i in range(2)]
    vh = ar.take("v_head", [P, NT, VH], F32)
    tail = Arena(nc, g.p4_at, g.top)
    NW = KQ + KL
    w_raw = tail.take("w_head_raw", [P, NW, P], F32)
    w_hi, w_lo = tail.take("w_head_hi", [P, NW, P], F32R), tail.take("w_head_lo", [P, NW, P], F32R)
    vT = tail.take("vT", [P, TQ], F32)
    mask = tail.take("causal_mask", [P, P], F32)
    gg = g.gg
    rq, mx, nb, rs, ri = (tail.take(n, [P, NT], F32) for n in ("rq", "row_max", "neg_max", "row_sum", "row_inv"))
    pt = [Arena(nc, low.at + i * 2048 + 32, g.top).take(f"probsT{i}", [P, 4, P], F32) for i in range(2)]

    names = ("w_loaded w_hi_done w_lo_done ready masked qk_gain_done q_projected kv_projected q_nope k_nope q_cos q_sin "
             "q_roped v_copied q_squared k_squared k_summed rq_summed rq_mean rq_root rq_done k_mean k_root k_inv "
             "k_scaled q_hi_done q_lo_done k_hi_done k_lo_done v_transposed vh_copied q_kept scored s_masked maxed "
             "biased exped inverted normed p_transposed p_copied pv_done out_copied padded").split()
    s = {n: sem(n) for n in names}
    def chunks(i):
        return [(j, min(4, i + 1 - j)) for j in range(0, i + 1, 4)]

    NCH = sum(len(chunks(i)) for i in range(NT))

    def score_shape(i):
        pieces = -(-(i + 1) * P // BANK)
        return pieces, (i + 1) * P // pieces

    def scores(i):
        pieces, n = score_shape(i)
        return banks[:, 3 * (i % 2):3 * (i % 2) + pieces, 0:n]

    w_uq = A["w_uq"].rearrange("(k p) n -> p k n", p=P)
    w_ukv = A["w_ukv"].rearrange("(k p) n -> p k n", p=P)
    half = ROPE // 2
    blocks = lambda ap: ap.rearrange("p (b t) -> p b t", b=NBLK)

    with nc.Block() as block:
        @block.sync
        def _(sp):
            with sp.Fori(0, H // 2) as i:
                for hh in range(2):
                    sp.wait_ge(s["w_lo_done"], i * 2 + hh + 1)
                    q0, kv0 = i * (2 * QK) + hh * QK, i * (2 * P) + hh * P
                    sp.dma_start(w_raw[:, 0:KQ, 0:QK], w_uq[:, :, ds(q0, QK)]).then_inc(s["w_loaded"], 16)
                    sp.dma_start(w_raw[:, 0:KQ, QK:QK + half], w_uq[:, :, ds(q0 + (NOPE + half), half)])\
                        .then_inc(s["w_loaded"], 16)
                    sp.dma_start(w_raw[:, 0:KQ, QK + half:P], w_uq[:, :, ds(q0 + NOPE, half)]).then_inc(s["w_loaded"], 16)
                    sp.dma_start(w_raw[:, KQ:NW, :], w_ukv[:, :, ds(kv0, P)]).then_inc(s["w_loaded"], 16)

        @block.gpsimd
        def _(pool):
            for opening in (s["w_lo_done"], s["k_lo_done"]):
                pool.sem_inc(opening, 1)
            nc.gpsimd.memset(mask[:, :], 0.0).then_inc(s["ready"], 1)
            pool.wait_ge(s["ready"], 1)
            nc.gpsimd.affine_select(out=mask[:, :], in_=mask[:, :], compare_op=ALU.is_ge, fill=MASKED, base=0,
                                    pattern=[[-1, P]], channel_multiplier=1).then_inc(s["ready"], 1)
            nc.gpsimd.memset(vT[:, TT:TQ], 0.0).then_inc(s["padded"], 1)
            nc.gpsimd.memset(sq_q[:, TT:TQ], 0.0).then_inc(s["padded"], 1)
            for t in (q_hi, q_lo, k_hi, k_lo):
                nc.gpsimd.memset(t[:, TT:TQ].bitcast(F32), 0.0).then_inc(s["padded"], 1)
            with pool.Fori(0, H // 2) as i:
                for hh in range(2):
                    n = i * 2 + hh
                    pool.wait_ge(s["w_hi_done"], n + 1)
                    nc.gpsimd.tensor_sub(w_lo[:, :, :], w_raw[:, :, :], w_hi[:, :, :].bitcast(F32)).then_inc(s["w_lo_done"], 1)
                    pool.wait_ge(s["k_hi_done"], n + 1)
                    nc.gpsimd.tensor_sub(k_lo[0:QK, 0:TT], sq_k[0:QK, :], k_hi[0:QK, 0:TT].bitcast(F32))\
                        .then_inc(s["k_lo_done"], 1)

        @block.scalar
        def _(act):
            for opening in (s["exped"],):
                act.sem_inc(opening, 1)
            act.copy(kf[NOPE:QK, :], g.kpe[NOPE:QK, :]).then_inc(s["masked"], 1)
            with act.Fori(0, H // 2) as i:
                for hh in range(2):
                    n = i * 2 + hh
                    act.wait_ge(s["w_loaded"], n * 64 + 64)
                    act.wait_ge(s["kv_projected"], n + 1)
                    act.copy(w_hi[:, :, :], w_raw[:, :, :]).then_inc(s["w_hi_done"], 1)
                    act.wait_ge(s["q_projected"], n + 1)
                    act.wait_ge(s["q_lo_done"], n + 1)
                    act.wait_ge(s["q_kept"], n + 1)
                    act.copy(blocks(qf[0:NOPE, :]), banks[0:NOPE, 0:3, 0:TB]).then_inc(s["q_nope"], 1)
                    act.wait_ge(s["kv_projected"], n + 2)
                    act.copy(blocks(kf[0:NOPE, :]), banks[0:NOPE, 3:6, 0:TB]).then_inc(s["k_nope"], 1)
                    act.wait_ge(s["k_nope"], n + 1)
                    act.wait_ge(s["masked"], 1)
                    act.wait_ge(s["k_lo_done"], n + 1)
                    act.activation(sq_k[0:QK, :], kf[0:QK, :], ACT.Square).then_inc(s["k_squared"], 1)
                    act.wait_ge(s["q_roped"], n + 1)
                    act.wait_ge(s["q_nope"], n + 1)
                    act.activation(sq_q[0:QK, 0:TT], qf[0:QK, :], ACT.Square).then_inc(s["q_squared"], 1)
                    act.wait_ge(s["qk_gain_done"], 1)
                    act.activation(q_hi[0:QK, 0:TT], qf[0:QK, :], ACT.Copy, scale=gg[0:QK, :]).then_inc(s["q_hi_done"], 1)
                    act.wait_ge(s["v_transposed"], n + 2)
                    act.copy(vh[:, 0:8, :], banks[:, 6, :].rearrange("p (t d) -> p t d", d=VH)).then_inc(s["vh_copied"], 1)
                    act.copy(vh[:, 8, :], banks[:, 7, 0:VH]).then_inc(s["vh_copied"], 1)
                    act.wait_ge(s["rq_mean"], n + 1)
                    act.activation(rq[:, :], rq[:, :], ACT.Sqrt).then_inc(s["rq_root"], 1)
                    act.wait_ge(s["k_mean"], n + 1)
                    act.activation(ms[0:QK, :], ms[0:QK, :], ACT.Sqrt).then_inc(s["k_root"], 1)
                    act.wait_ge(s["k_scaled"], n + 1)
                    act.copy(k_hi[0:QK, 0:TT], sq_k[0:QK, :]).then_inc(s["k_hi_done"], 1)

                    def probabilities(t):
                        m = (t + 1) * P
                        pieces, L = score_shape(t)
                        act.wait_ge(s["biased"], n * NT + (t + 1))
                        if t < 2:
                            act.wait_ge(s["p_transposed"], n * NCH + 1)
                        else:
                            act.wait_ge(s["p_transposed"], n * NCH + sum(len(chunks(x)) for x in range(t - 1)) + 1)
                        act.activation(probs[t % 2][:, 0:m].rearrange("p (a b) -> p a b", a=pieces), scores(t), ACT.Exp,
                                       bias=nb[:, t:t + 1], scale=rq[:, t:t + 1], accum_out=rs[:, t:t + 1])\
                            .then_inc(s["exped"], 1)

                    probabilities(0)
                    c = 0
                    for t in range(NT):
                        if t + 1 < NT:
                            probabilities(t + 1)
                        for j, m in chunks(t):
                            act.wait_ge(s["p_transposed"], n * NCH + (c + 1 + 1))
                            if c >= 2:
                                act.wait_ge(s["pv_done"], n * NCH + (c - 1))
                            act.copy(pt[c % 2][:, 0:m, :], banks[:, 6, 0:m * P].rearrange("p (j q) -> p j q", q=P))\
                                .then_inc(s["p_copied"], 1)
                            c += 1

        @block.vector
        def _(v):
            for opening in (s["q_kept"], s["q_lo_done"], s["out_copied"]):
                v.sem_inc(opening, 1)
            nc.vector.tensor_mul(gg[:, :], g.gcol[:, G_QN:G_QN + 1], g.gcol[:, G_KN:G_KN + 1]).then_inc(s["qk_gain_done"], 1)
            v.wait_ge(s["padded"], 6)
            with v.Fori(0, H // 2) as i:
                for hh in range(2):
                    n = i * 2 + hh
                    v.wait_ge(s["q_projected"], n + 1)
                    v.wait_ge(s["rq_summed"], n + 1)
                    nc.vector.tensor_mul(blocks(qf[NOPE:QK, :]), banks[NOPE:QK, 0:3, 0:TB], blocks(g.cs[NOPE:QK, :]))\
                        .then_inc(s["q_cos"], 1)
                    nc.vector.tensor_mul(blocks(part[NOPE:QK, :]), banks[QK:P, 0:3, 0:TB], blocks(g.cs[QK:P, :]))\
                        .then_inc(s["q_sin"], 1)
                    v.wait_ge(s["q_cos"], n + 1)
                    v.wait_ge(s["q_sin"], n + 1)
                    nc.vector.tensor_add(qf[NOPE:QK, :], qf[NOPE:QK, :], part[NOPE:QK, :]).then_inc(s["q_roped"], 1)
                    v.wait_ge(s["kv_projected"], n + 2)
                    v.wait_ge(s["v_transposed"], n + 1)
                    nc.vector.tensor_copy(blocks(vT[NOPE:P, 0:TT]), banks[NOPE:P, 3:6, 0:TB]).then_inc(s["v_copied"], 1)
                    v.wait_ge(s["q_roped"], n + 1)
                    v.wait_ge(s["q_hi_done"], n + 1)
                    nc.vector.scalar_tensor_tensor(q_lo[0:QK, 0:TT], qf[0:QK, :], gg[0:QK, :],
                                                   q_hi[0:QK, 0:TT].bitcast(F32), ALU.mult, ALU.subtract)\
                        .then_inc(s["q_lo_done"], 1)
                    nc.vector.tensor_copy(g.qs[0:QK, ds(n, 1), :].rearrange("p o t -> p (o t)"), qf[0:QK, TP:T])\
                        .then_inc(s["q_kept"], 1)
                    v.wait_ge(s["k_summed"], n + 1)
                    nc.vector.tensor_scalar(blocks(ms[0:QK, :]), banks[0:QK, 3:6, 0:TB], 1.0 / QK, EPS,
                                            ALU.mult, ALU.add).then_inc(s["k_mean"], 1)
                    v.wait_ge(s["rq_summed"], n + 2)
                    nc.vector.tensor_scalar(rq[:, :], banks[:, 7, 256:256 + NT], 1.0 / QK, EPS, ALU.mult, ALU.add)\
                        .then_inc(s["rq_mean"], 1)
                    v.wait_ge(s["k_root"], n + 1)
                    nc.vector.reciprocal(ms[0:QK, :], ms[0:QK, :]).then_inc(s["k_inv"], 1)
                    v.wait_ge(s["rq_root"], n + 1)
                    nc.vector.reciprocal(rq[:, :], rq[:, :]).then_inc(s["rq_done"], 1)
                    v.wait_ge(s["k_inv"], n + 1)
                    nc.vector.tensor_mul(sq_k[0:QK, :], kf[0:QK, :], ms[0:QK, :]).then_inc(s["k_scaled"], 1)
                    v.wait_ge(s["rq_done"], n * 2 + 1)
                    nc.vector.tensor_scalar(rq[:, :], rq[:, :], SCALE, None, ALU.mult).then_inc(s["rq_done"], 1)

                    def maxima(t):
                        pieces, L = score_shape(t)
                        v.wait_ge(s["scored"], n * NT + (t + 1))
                        diag = banks[:, 3 * (t % 2) + pieces - 1, L - P:L]
                        nc.vector.tensor_add(diag, diag, mask[:, :]).then_inc(s["s_masked"], 1)
                        v.wait_ge(s["s_masked"], n * NT + (t + 1))
                        nc.vector.tensor_reduce(mx[:, t:t + 1], scores(t), mybir.AxisListType.XY, ALU.max)\
                            .then_inc(s["maxed"], 1)
                        v.wait_ge(s["maxed"], n * NT + (t + 1))
                        nc.vector.scalar_tensor_tensor(nb[:, t:t + 1], mx[:, t:t + 1], -1.0, rq[:, t:t + 1],
                                                       ALU.mult, ALU.mult).then_inc(s["biased"], 1)

                    v.wait_ge(s["ready"], 2)
                    v.wait_ge(s["rq_done"], n * 2 + 2)

                    def keep_output(t):
                        v.wait_ge(s["pv_done"], n * NCH + sum(len(chunks(x)) for x in range(t + 1)))
                        w = min(P, TP - t * P)
                        nc.vector.tensor_copy(g.attnT[VH * hh:VH * hh + VH, ds(i, 1), t * P:t * P + w]
                                              .rearrange("p o t -> p (o t)"), banks[0:VH, 7, 0:w]).then_inc(s["out_copied"], 1)

                    maxima(0)
                    for t in range(NT):
                        if t + 1 < NT:
                            maxima(t + 1)
                        v.wait_ge(s["exped"], n * NT + (t + 1 + 1))
                        nc.vector.reciprocal(ri[:, t:t + 1], rs[:, t:t + 1]).then_inc(s["inverted"], 1)
                        v.wait_ge(s["inverted"], n * NT + (t + 1))
                        pr = probs[t % 2][:, 0:(t + 1) * P]
                        nc.vector.tensor_scalar(pr, pr, ri[:, t:t + 1], None, ALU.mult).then_inc(s["normed"], 1)
                        if t >= 1:
                            keep_output(t - 1)
                    keep_output(NT - 1)

        @block.tensor
        def _(pe):
            for opening in (s["kv_projected"], s["p_transposed"], s["rq_summed"], s["v_transposed"]):
                pe.sem_inc(opening, 1)
            pe.wait_ge(s["padded"], 6)
            with pe.Fori(0, H // 2) as i:
                for hh in range(2):
                    n = i * 2 + hh
                    pe.wait_ge(s["w_lo_done"], n + 2)
                    pe.wait_ge(s["exped"], n * NT + 1)
                    for out, k0, K, xhi, xlo, done in ((0, 0, KQ, g.cq_hi, g.cq_lo, s["q_projected"]),
                                                       (3, KQ, KL, g.lat_hi, g.lat_lo, s["kv_projected"])):
                        for k in range(K):
                            for w, x, a in ((w_hi, xhi, 0), (w_hi, xlo, 1), (w_lo, xhi, 2)):
                                for b in range(NBLK):
                                    mm = pe.matmul(banks[:, out + b, 0:TB], w[:, k0 + k, :], x[:, k, b * TB:(b + 1) * TB],
                                                   start=k == 0 and a == 0, stop=k == K - 1 and a == 2)
                        mm.then_inc(done, 1)
                    pe.wait_ge(s["k_squared"], n + 1)
                    pe.wait_ge(s["v_copied"], n + 1)
                    pe.wait_ge(s["out_copied"], n * NT + 1)
                    for b in range(NBLK):
                        mm = pe.matmul(banks[:, 3 + b, 0:TB], g.ones[0:QK, :], sq_k[0:QK, b * TB:(b + 1) * TB],
                                       start=True, stop=True)
                    mm.then_inc(s["k_summed"], 1)
                    for t in range(NT):
                        mm = pe.transpose(banks[:, 6 + t // 8, (t % 8) * VH:(t % 8 + 1) * VH], vT[NOPE:P, t * P:(t + 1) * P],
                                          ident[NOPE:P, NOPE:P])
                    mm.then_inc(s["v_transposed"], 1)
                    pe.wait_ge(s["q_squared"], n + 1)
                    pe.wait_ge(s["vh_copied"], n * 2 + 2)
                    for t in range(NT):
                        mm = pe.matmul(banks[:, 7, 256 + t:257 + t], sq_q[0:QK, t * P:(t + 1) * P], g.ones[0:QK, 0:1],
                                       start=True, stop=True)
                    mm.then_inc(s["rq_summed"], 1)
                    pe.wait_ge(s["q_lo_done"], n + 2)
                    pe.wait_ge(s["k_lo_done"], n + 2)
                    pe.wait_ge(s["rq_mean"], n + 1)
                    pe.wait_ge(s["k_mean"], n + 1)

                    def score(t):
                        pieces, L = score_shape(t)
                        if t >= 2:
                            pe.wait_ge(s["exped"], n * NT + (t - 1 + 1))
                        for b in range(pieces):
                            for q, k, a in ((q_hi, k_hi, 0), (q_hi, k_lo, 1), (q_lo, k_hi, 2)):
                                mm = pe.matmul(banks[:, 3 * (t % 2) + b, 0:L], q[0:QK, t * P:(t + 1) * P],
                                               k[0:QK, b * L:(b + 1) * L], start=a == 0, stop=a == 2)
                        mm.then_inc(s["scored"], 1)

                    def values(t, c, j, m):
                        pe.wait_ge(s["p_copied"], n * NCH + (c + 1))
                        if j == 0:
                            pe.wait_ge(s["out_copied"], n * NT + t + 1)
                        for x in range(m):
                            mm = pe.matmul(banks[0:VH, 7, 0:P], vh[:, j + x, :], pt[c % 2][:, x, :],
                                           start=j + x == 0, stop=j + x == t)
                        mm.then_inc(s["pv_done"], 1)

                    score(0)
                    c, last = 0, None
                    for t in range(NT):
                        if t + 1 < NT:
                            score(t + 1)
                        pe.wait_ge(s["normed"], n * NT + (t + 1))
                        for j, m in chunks(t):
                            if c >= 1:
                                pe.wait_ge(s["p_copied"], n * NCH + c)
                            for x in range(m):
                                mm = pe.transpose(banks[:, 6, x * P:(x + 1) * P],
                                                  probs[t % 2][:, (j + x) * P:(j + x + 1) * P], ident[:, :])
                            mm.then_inc(s["p_transposed"], 1)
                            if last:
                                values(*last)
                            last = (t, c, j, m)
                            c += 1
                    values(*last)


def sample_attention(g):
    nc, A, sem, banks, ident = g.nc, g.A, g.sem, g.banks, g.ident
    G = 8
    SETS = 4
    AHEAD = 4
    GROUPS = NSEQ * NPAGES // G
    PER_SEQ = NPAGES // G
    HS = H * SDEC
    HC = H // 2
    WK = HC * NOPE
    WC = WK + HC * SDEC
    KW = NOPE + VH
    ar = Arena(nc, g.z_hc_at, g.h_at)
    comb_hi = [ar.take(f"comb_hi{i}", [P, KL, 2, WC], F32R) for i in range(2)]
    comb_lo = [ar.take(f"comb_lo{i}", [P, KL, 2, WC], F32R) for i in range(2)]
    lora = Arena(nc, g.h_at, g.lora_end)
    X = [a.take(f"page_latents{i}", [P, G, KVL + 2], F32) for i, a in enumerate((ar, ar, lora, lora))]
    R = [a.take(f"page_ropes{i}", [P, G * ROPE], F32) for i, a in enumerate((ar, ar, lora, lora))]
    xT_hi = [lora.take(f"pageT_hi{i}", [P, KL, P], F32R) for i in range(AHEAD)]
    xT_lo = [lora.take(f"pageT_lo{i}", [P, KL, P], F32R) for i in range(AHEAD)]
    sq = [ar.take(f"k_sq{i}", [P, H * NOPE], F32) for i in range(2)]
    ctxs = ar.take("context", [HS, NSEQ, KVL + 1], F32)
    tail = Arena(nc, g.p4_at, g.top)
    wkv = ar.take("w_ukv", [P, KL, H * KW], F32)
    qab = tail.take("q_latent", [P, NSEQ, KL, HS], F32)
    qab_hi, qab_lo = (tail.take(n, [P, NSEQ, KL, HS], F32R) for n in ("q_latent_hi", "q_latent_lo"))
    rT = tail.take("ropesT", [P, 2 * P], F32)
    rsq = tail.take("rope_sq", [P, G, ROPE], F32)
    qr4 = tail.take("q_rope4", [P, NSEQ, HS], F32)
    own = tail.take("own_block", [P, 4, HS], F32)
    qbd = [tail.take(f"q_rope_blocks{i}", [P, 4, HS], F32) for i in range(2)]
    sc = [tail.take(f"scores{i}", [P, G, HS], F32) for i in range(2)]
    st = tail.take("scaled_scores", [P, G, HS], F32)
    pr = tail.take("probabilities", [P, G, HS], F32)
    ksum = [tail.take(f"k_sums{i}", [P, G, H], F32) for i in range(2)]
    rk, rsum = tail.take("k_inv_root", [P, G * H], F32), tail.take("rope_sums", [P, G], F32)
    mx, diag = tail.take("maxima", [P, HS], F32), tail.take("max_diagonal", [HS, HS], F32)
    gmax, mnew, dmax, alpha = (tail.take(n, [HS, 1], F32) for n in ("group_max", "new_max", "max_fall", "alpha"))
    mrun = tail.take("running_max", [HS, NSEQ], F32)
    linv = tail.take("sum_inv", [HS, NSEQ], F32)
    pages = tail.take("page_table", [1, NSEQ * NPAGES], I32)
    mask0 = tail.take("new_mask", [NS, NSEQ, SDEC], F32)
    wukT = Arena(nc, g.z_at + -(-KC * TT * 4 // 32) * 32, g.conv_at).take("w_ukT", [P, H * KL, P], F32)

    names = ("w_loaded table_loaded constants memsets q_squared q_sum q_mean q_root q_inv q_normed wT_done wT_copied qab_done "
             "qab_copied qab_split qab_lo_done comb_w_hi comb_w_lo kn0_done sq0_done k0_parts k0_mean k0_root k0_inv s0_done "
             "s0_steps s0_transposed m0_done s0_shifted p0_done l0_done p0_transposed p0_copied ctx0_done ctx0_copied "
             "x_transposed hi_done lo_done kn_done sq_done sc_copied summed r_transposed r_copied rp_done ropes_squared "
             "comb_ready qbd_ready s_added k_tot k_mean k_root k_inv s_steps maxed max_transposed max_steps diag_done "
             "alpha_done max_spread shifted exped ctx_done final_inv final_scaled ctxT_done ctxT_copied "
             "out_done out_copied qr_copied").split()
    s = {n: sem(n) for n in names}
    loaded = [sem(f"pages_loaded{i}") for i in range(SETS)]
    ropes_loaded = [sem(f"ropes_loaded{i}") for i in range(SETS)]
    s["pages_free"] = [sem(f"pages_free{i}") for i in range(SETS)]
    B0 = lambda n, a, b: banks[0:n, 0, a:b]

    def ge(engine, semaphore, value):
        if not isinstance(value, int) or value > 0:
            engine.wait_ge(semaphore, value)

    nope = wkv[:, :, :].rearrange("p k (h c) -> p (k h) c", c=KW)
    lat_cache, rope_cache = A["cache_kv_latent"], A["cache_k_rope"]
    n_pool = lat_cache.shape[0]
    m7 = lambda a, b: banks[:, 7, a:b]
    pageT = lambda j: banks[:, 4 + j % 2, 0:KVL]
    MT, MB, CT = 0, P, P + HS

    with nc.Block() as block:
        @block.sync
        def _(sp):
            sp.dma_start(pages[:, :], A["page_table"]).then_inc(s["table_loaded"], 16)
            sp.dma_start(wkv[:, :, :], A["w_ukv"].rearrange("(k p) n -> p k n", p=P)).then_inc(s["w_loaded"], 16)
            sp.wait_ge(s["table_loaded"], 16)
            with sp.Fori(0, GROUPS // SETS) as i:
                for q in range(SETS):
                    for j in range(G):
                        page = sp.value_load(pages[0:1, ds(i * (SETS * G) + (q * G + j), 1)], min_val=0,
                                             max_val=n_pool - 1)
                        if j == 0:
                            sp.wait_ge(s["pages_free"][q], i + 1)
                        sp.dma_start(X[q][:, j, 0:KVL], lat_cache[ds(page, 1), :, :].rearrange("o p n -> p (o n)"))\
                            .then_inc(loaded[q], 16)
                        sp.dma_start(R[q][:, j * ROPE:(j + 1) * ROPE],
                                     rope_cache[ds(page, 1), :, :].rearrange("o p n -> p (o n)")).then_inc(ropes_loaded[q], 16)

        def groups(engine, step, last):
            at = lambda n: (n, n % SETS, n // SETS)
            step(at(0), None, None)
            step(at(1), at(0), None)
            with engine.Fori(0, (GROUPS - SETS) // SETS) as i:
                inside = lambda c: (i * SETS + c, c % SETS, i + c // SETS)
                for c in range(2, 2 + SETS):
                    step(inside(c), inside(c - 1), inside(c - 2))
            step(at(GROUPS - 2), at(GROUPS - 3), at(GROUPS - 4))
            step(at(GROUPS - 1), at(GROUPS - 2), at(GROUPS - 3))
            last(at(GROUPS - 1), at(GROUPS - 2))

        def following(group, j):
            n, q, fill = group
            if j < G:
                return q, fill, j
            if isinstance(n, int) and n == GROUPS - 1:
                return None
            return (q + 1) % SETS, fill + (q + 1) // SETS, j - G

        @block.gpsimd
        def _(pool):
            nc.gpsimd.memset(mask0[:, :, :], 0.0).then_inc(s["memsets"], 1)
            nc.gpsimd.memset(own[:, :, :], 1.0).then_inc(s["memsets"], 1)
            for q in range(SETS):
                nc.gpsimd.memset(X[q][:, :, KVL:KVL + 1], 1.0).then_inc(s["memsets"], 1)
            nc.gpsimd.memset(g.attnT[:, :, T:TT], 0.0).then_inc(s["memsets"], 1)
            pool.wait_ge(s["memsets"], 3 + SETS)
            nc.gpsimd.affine_select(out=mask0[:, :, :], in_=mask0[:, :, :], compare_op=ALU.is_ge, fill=MASKED, base=0,
                                    pattern=[[-SDEC, NSEQ], [0, SDEC]], channel_multiplier=1).then_inc(s["constants"], 1)
            nc.gpsimd.affine_select(out=own[:, :, :], in_=own[:, :, :], compare_op=ALU.is_ge, fill=0.0, base=0,
                                    pattern=[[-ROPE, 4], [0, HS]], channel_multiplier=1).then_inc(s["constants"], 1)
            pool.wait_ge(s["constants"], 2)
            nc.gpsimd.affine_select(out=mask0[:, :, :], in_=mask0[:, :, :], compare_op=ALU.is_ge, fill=MASKED, base=0,
                                    pattern=[[SDEC, NSEQ], [1, SDEC]], channel_multiplier=-1).then_inc(s["constants"], 1)
            nc.gpsimd.affine_select(out=own[:, :, :], in_=own[:, :, :], compare_op=ALU.is_ge, fill=0.0, base=ROPE - 1,
                                    pattern=[[ROPE, 4], [0, HS]], channel_multiplier=-1).then_inc(s["constants"], 1)
            pool.wait_ge(s["constants"], 4)
            pool.wait_ge(s["qab_lo_done"], 1)
            pool.wait_ge(s["qr_copied"], 4)
            pool.wait_ge(s["comb_w_lo"], 2)

            def step(group, *_):
                n, q, fill = group
                b, par = n // PER_SEQ, q % 2
                ge(pool, s["kn_done"], n * G - G + 1)
                for t, src in ((comb_hi, qab_hi), (comb_lo, qab_lo)):
                    nc.gpsimd.tensor_copy(t[par][:, :, :, WK:WC],
                                          src[:, ds(b, 1), :, :].bitcast(F32).rearrange("p o k (a q) -> p (o k) a q", a=2))\
                        .then_inc(s["comb_ready"], 1)
                ge(pool, s["rp_done"], n)
                nc.gpsimd.tensor_mul(qbd[par][:, :, :], own[:, :, :],
                                     qr4[:, ds(b, 1), :].broadcast_to([P, 4, HS])).then_inc(s["qbd_ready"], 1)
                pool.wait_ge(ropes_loaded[q], fill * (16 * G) + 16 * G)
                ge(pool, s["k_tot"], n * 2)
                nc.gpsimd.tensor_mul(rsq[:, :, :].rearrange("p j r -> p (j r)"), R[q][:, :], R[q][:, :])\
                    .then_inc(s["ropes_squared"], 1)

            groups(pool, step, lambda *_: None)

        @block.scalar
        def _(act):
            qs = g.qs[0:QK, :, :].rearrange("p h t -> p (h t)")
            act.activation(st[0:QK, :, :].rearrange("p a b -> p (a b)"), qs, ACT.Square).then_inc(s["q_squared"], 1)
            act.wait_ge(s["q_mean"], 1)
            act.activation(pr[0:QK, :, :], pr[0:QK, :, :], ACT.Sqrt).then_inc(s["q_root"], 1)
            act.wait_ge(s["wT_done"], 1)
            act.copy(wukT[0:NOPE, :, :].rearrange("p (a b) c -> p a (b c)", a=4), banks[0:NOPE, 2:6, :])\
                .then_inc(s["wT_copied"], 1)
            for p in range(2):
                act.copy(comb_hi[p][:, :, :, 0:WK].rearrange("p k a (h c) -> p (k a) h c", c=NOPE),
                         nope[:, :, 0:NOPE].rearrange("p (a h) c -> p a h c", h=HC)).then_inc(s["comb_w_hi"], 1)
            act.wait_ge(s["kn0_done"], 1)
            act.activation(sq[0][0:NS, :], banks[0:NS, 1, :], ACT.Square).then_inc(s["sq0_done"], 1)
            act.wait_ge(s["qab_copied"], KL)
            act.copy(qab_hi[:, :, :, :], qab[:, :, :, :]).then_inc(s["qab_split"], 1)
            act.wait_ge(s["q_normed"], 1)
            for quad in range(4):
                act.wait_ge(s["q_normed"], 1)
                act.copy(qr4[quad * ROPE:(quad + 1) * ROPE, :, :].rearrange("p b (h s) -> p b h s", h=H),
                         g.qs[NOPE:QK, :, :].rearrange("p h (b s) -> p b h s", s=SDEC)).then_inc(s["qr_copied"], 1)
            act.wait_ge(s["k0_mean"], 1)
            act.activation(rk[0:NS, 0:H], rk[0:NS, 0:H], ACT.Sqrt).then_inc(s["k0_root"], 1)
            act.wait_ge(s["s0_shifted"], 1)
            act.activation(sc[0][0:HS, :, :], sc[0][0:HS, :, :], ACT.Exp, scale=SCALE).then_inc(s["p0_done"], 1)
            act.wait_ge(s["p0_transposed"], 1)
            act.wait_ge(s["q_inv"], 1)
            act.copy(pr[0:NS, :, :].rearrange("p a b -> p (a b)"), banks[0:NS, 7, 0:NSEQ * HS]).then_inc(s["p0_copied"], 1)
            act.wait_ge(s["ctx0_done"], 1)
            act.copy(ctxs[:, :, 0:KVL].rearrange("p (a b) c -> p a b c", a=4),
                     banks[0:HS, 2:6, :].rearrange("p a (b c) -> p a b c", b=2)).then_inc(s["ctx0_copied"], 1)

            def sqrt_step(n):
                act.wait_ge(s["k_mean"], n + 1)
                act.activation(rk[:, :], rk[:, :], ACT.Sqrt).then_inc(s["k_root"], 1)

            def alpha_step(n):
                act.wait_ge(s["max_steps"], n * 3 + 3)
                act.activation(alpha[:, :], dmax[:, :], ACT.Exp, scale=SCALE).then_inc(s["alpha_done"], 1)

            def exp_step(n):
                act.wait_ge(s["shifted"], n + 1)
                act.activation(pr[:, :, :], st[:, :, :], ACT.Exp, scale=SCALE).then_inc(s["exped"], 1)

            def step(group, soft, _):
                n, q, fill = group
                base, par = n * G, q % 2

                def hi(j):
                    if following(group, j):
                        act.wait_ge(s["x_transposed"], base + (j + 1))
                        ge(act, s["kn_done"], base + (j - AHEAD + 1 + 1))
                        act.copy(xT_hi[j % AHEAD][:, :, :].rearrange("p k t -> p (k t)"), pageT(j)).then_inc(s["hi_done"], 1)

                if soft is None:
                    hi(0)
                    hi(1)
                for j in range(G):
                    hi(j + 2)
                    if soft is not None:
                        if j == 2:
                            sqrt_step(soft[0])
                        if j == 6:
                            alpha_step(soft[0])
                        if j == 7:
                            exp_step(soft[0])
                    act.wait_ge(s["kn_done"], base + (j + 1 + 1))
                    ge(act, s["summed"], base + (j - 1))
                    kn = banks[:, 2 * (j % 2):2 * (j % 2) + 2, :]
                    act.activation(sq[j % 2][:, :].rearrange("p (a c) -> p a c", a=2), kn[:, :, 0:WK], ACT.Square)\
                        .then_inc(s["sq_done"], 1)
                    if j == 0:
                        ge(act, s["s_added"], n)
                    act.copy(sc[par][:, j, :].rearrange("p (a q) -> p a q", a=2), kn[:, :, WK:WC]).then_inc(s["sc_copied"], 1)
                    if j == 3:
                        act.wait_ge(s["r_transposed"], n + 1)
                        ge(act, s["rp_done"], n + 1)
                        act.copy(rT[:, :], banks[:, 6, 0:2 * P]).then_inc(s["r_copied"], 1)

            def last(soft, _):
                sqrt_step(soft[0])
                alpha_step(soft[0])
                exp_step(soft[0])

            groups(act, step, last)
            act.wait_ge(s["ctxT_done"], 1)
            act.copy(wukT[:, 0:2 * NSEQ * HS // P, :].rearrange("p a b -> p (a b)"), banks[:, 0, :]).then_inc(s["ctxT_copied"], 1)

        @block.vector
        def _(v):
            for opening in (s["s_added"], s["k_tot"], s["ctx_done"]):
                v.sem_inc(opening, 1)
            f8 = lambda t, n: t[0:n, :, :].rearrange("p a b -> p (a b)")
            v.wait_ge(s["q_sum"], 1)
            nc.vector.tensor_scalar(f8(pr, QK), B0(QK, 0, H * NS), 1.0 / QK, EPS, ALU.mult, ALU.add).then_inc(s["q_mean"], 1)
            v.wait_ge(s["q_root"], 1)
            nc.vector.reciprocal(pr[0:QK, :, :], pr[0:QK, :, :]).then_inc(s["q_inv"], 1)
            v.wait_ge(s["q_inv"], 1)
            qs = g.qs[0:QK, :, :].rearrange("p h t -> p (h t)")
            nc.vector.scalar_tensor_tensor(qs, qs, g.gg[0:QK, :], f8(pr, QK), ALU.mult, ALU.mult).then_inc(s["q_normed"], 1)
            v.wait_ge(s["qab_done"], 1)
            for k in range(KL):
                nc.vector.tensor_copy(qab[:, :, k, :].rearrange("p b (h s) -> p b h s", h=H),
                                      banks[:, 0, k * H * NS:(k + 1) * H * NS].rearrange("p (h b s) -> p b h s", b=NSEQ, s=SDEC))\
                    .then_inc(s["qab_copied"], 1)
            v.wait_ge(s["qab_copied"], KL)
            v.wait_ge(s["qab_split"], 1)
            nc.vector.tensor_sub(qab_lo[:, :, :, :].rearrange("p b k q -> p (b k q)"), qab[:, :, :, :].rearrange("p b k q -> p (b k q)"),
                                 qab_hi[:, :, :, :].bitcast(F32).rearrange("p b k q -> p (b k q)")).then_inc(s["qab_lo_done"], 1)
            for p in range(2):
                v.wait_ge(s["comb_w_hi"], p + 1)
                nc.vector.tensor_sub(comb_lo[p][:, :, :, 0:WK].rearrange("p k a (h c) -> p (k a) h c", c=NOPE),
                                     nope[:, :, 0:NOPE].rearrange("p (a h) c -> p a h c", h=HC),
                                     comb_hi[p][:, :, :, 0:WK].bitcast(F32).rearrange("p k a (h c) -> p (k a) h c", c=NOPE))\
                    .then_inc(s["comb_w_lo"], 1)
            v.wait_ge(s["sq0_done"], 1)
            nc.vector.tensor_reduce(ksum[0][0:NS, 0, :], sq[0][0:NS, :].rearrange("p (h c) -> p h c", h=H), AX_X, ALU.add)\
                .then_inc(s["k0_parts"], 1)
            rope = g.new_page[:, KVL:KVL + ROPE]
            nc.vector.tensor_mul(diag[:, :], rope, rope).then_inc(s["k0_parts"], 1)
            v.wait_ge(s["k0_parts"], 2)
            nc.vector.reduce_sum(rsum[0:NS, 0:1], diag[:, :], AX_X).then_inc(s["k0_parts"], 1)
            v.wait_ge(s["k0_parts"], 3)
            nc.vector.tensor_scalar(rk[0:NS, 0:H], ksum[0][0:NS, 0, :], rsum[0:NS, 0:1], 1.0 / QK, ALU.add, ALU.mult)\
                .then_inc(s["k0_parts"], 1)
            v.wait_ge(s["k0_parts"], 4)
            nc.vector.tensor_scalar(rk[0:NS, 0:H], rk[0:NS, 0:H], EPS, None, ALU.add).then_inc(s["k0_mean"], 1)
            v.wait_ge(s["k0_root"], 1)
            nc.vector.reciprocal(rk[0:NS, 0:H], rk[0:NS, 0:H]).then_inc(s["k0_inv"], 1)
            v.wait_ge(s["s0_done"], 1)
            s0 = f8(st, NS)
            s04 = st[0:NS, :, :].rearrange("p b (h s) -> p b h s", h=H)
            nc.vector.tensor_copy(s0, banks[0:NS, 6, 0:NSEQ * HS]).then_inc(s["s0_steps"], 1)
            v.wait_ge(s["s0_steps"], 1)
            nc.vector.tensor_add(s0, s0, banks[0:NS, 7, 0:NSEQ * HS]).then_inc(s["s0_steps"], 1)
            v.wait_ge(s["s0_steps"], 2)
            v.wait_ge(s["k0_inv"], 1)
            nc.vector.tensor_mul(s04, s04, rk[0:NS, 0:H].unsqueeze(1).unsqueeze(3).broadcast_to([NS, NSEQ, H, SDEC]))\
                .then_inc(s["s0_steps"], 1)
            v.wait_ge(s["s0_steps"], 3)
            v.wait_ge(s["constants"], 4)
            nc.vector.tensor_add(s04, s04, mask0[:, :, :].unsqueeze(2).broadcast_to([NS, NSEQ, H, SDEC])).then_inc(s["s0_steps"], 1)
            v.wait_ge(s["s0_transposed"], 1)
            s0T = banks[0:HS, 6, 0:NSEQ * NS].rearrange("p (b t) -> p b t", b=NSEQ)
            nc.vector.tensor_reduce(mrun[:, :], s0T, AX_X, ALU.max).then_inc(s["m0_done"], 1)
            v.wait_ge(s["m0_done"], 1)
            nc.vector.tensor_sub(sc[0][0:HS, :, :], s0T, mrun[:, :].unsqueeze(2).broadcast_to([HS, NSEQ, NS])).then_inc(s["s0_shifted"], 1)
            v.wait_ge(s["p0_done"], 1)
            nc.vector.tensor_reduce(ctxs[:, :, KVL:KVL + 1].rearrange("p b o -> p (b o)"), sc[0][0:HS, :, :], AX_X, ALU.add)\
                .then_inc(s["l0_done"], 1)
            v.wait_ge(s["l0_done"], 1)
            v.wait_ge(s["ctx0_copied"], 1)

            def soft_mean(n, par):
                v.wait_ge(s["ropes_squared"], n + 1)
                nc.vector.tensor_reduce(rsum[:, :], rsq[:, :, :], AX_X, ALU.add).then_inc(s["k_tot"], 1)
                v.wait_ge(s["k_tot"], n * 2 + 2)
                v.wait_ge(s["summed"], n * G + G)
                nc.vector.tensor_add(rk[:, :].rearrange("p (j h) -> p j h", h=H), ksum[par][:, :, :],
                                     rsum[:, :].unsqueeze(2).broadcast_to([P, G, H])).then_inc(s["k_tot"], 1)
                v.wait_ge(s["k_tot"], n * 2 + 3)
                nc.vector.tensor_scalar(rk[:, :], rk[:, :], 1.0 / QK, EPS, ALU.mult, ALU.add).then_inc(s["k_mean"], 1)
                v.wait_ge(s["rp_done"], n + 2)
                v.wait_ge(s["sc_copied"], n * G + G)
                nc.vector.tensor_add(f8(st, P), f8(sc[par], P), banks[:, 6, 2 * P:4 * P]).then_inc(s["s_added"], 1)

            def soft_scores(n):
                v.wait_ge(s["k_root"], n + 1)
                nc.vector.reciprocal(rk[:, :], rk[:, :]).then_inc(s["k_inv"], 1)
                v.wait_ge(s["k_inv"], n + 1)
                v.wait_ge(s["s_added"], n + 2)
                sv = f8(st, P).rearrange("p (a s) -> p a s", s=SDEC)
                nc.vector.tensor_mul(sv, sv, rk[:, :].unsqueeze(2).broadcast_to([P, G * H, SDEC])).then_inc(s["s_steps"], 1)

            def soft_maxima(n):
                v.wait_ge(s["s_steps"], n + 1)
                nc.vector.tensor_reduce(mx[:, :], st[:, :, :].rearrange("p j q -> p q j"), AX_X, ALU.max).then_inc(s["maxed"], 1)

            def soft_max(n, b):
                v.wait_ge(s["max_transposed"], n + 1)
                nc.vector.reduce_max(gmax[:, :], banks[0:HS, 7, MT:MT + P], AX_X).then_inc(s["max_steps"], 1)
                v.wait_ge(s["max_steps"], n * 3 + 1)
                nc.vector.tensor_max(mnew[:, :], gmax[:, :], mrun[:, ds(b, 1)]).then_inc(s["max_steps"], 1)
                v.wait_ge(s["max_steps"], n * 3 + 2)
                nc.vector.tensor_scalar(diag[:, :], ident[0:HS, 0:HS], mnew[:, :], None, ALU.mult).then_inc(s["diag_done"], 1)
                nc.vector.tensor_sub(dmax[:, :], mrun[:, ds(b, 1)], mnew[:, :]).then_inc(s["max_steps"], 1)
                v.wait_ge(s["max_steps"], n * 3 + 3)
                nc.vector.tensor_scalar(mrun[:, ds(b, 1)], mnew[:, :], 1.0, None, ALU.mult).then_inc(s["m0_done"], 1)

            def soft_shift(n):
                v.wait_ge(s["max_spread"], n + 1)
                nc.vector.tensor_sub(st[:, :, :], st[:, :, :], banks[:, 7, MB:MB + HS].unsqueeze(1).broadcast_to([P, G, HS]))\
                    .then_inc(s["shifted"], 1)

            def soft_context(group):
                n, q, fill = group
                b = n // PER_SEQ
                v.wait_ge(s["pages_free"][q], fill + 2)
                v.wait_ge(s["alpha_done"], n + 1)
                v.wait_ge(s["m0_done"], n + 2)
                ge(v, s["ctx_done"], n + 1)
                c = ctxs[:, ds(b, 1), :].rearrange("p o c -> p (o c)")
                nc.vector.scalar_tensor_tensor(c, c, alpha[:, :], banks[0:HS, 7, CT:CT + KVL + 1], ALU.mult, ALU.add)\
                    .then_inc(s["ctx_done"], 1)

            def step(group, soft, added):
                n, q, fill = group
                base, par = n * G, q % 2

                def lo(j):
                    if following(group, j):
                        v.wait_ge(s["hi_done"], base + (j + 1))
                        nc.vector.tensor_sub(xT_lo[j % AHEAD][:, :, :].rearrange("p k t -> p (k t)"), pageT(j),
                                             xT_hi[j % AHEAD][:, :, :].bitcast(F32).rearrange("p k t -> p (k t)"))\
                            .then_inc(s["lo_done"], 1)

                if soft is None:
                    lo(0)
                    lo(1)
                for j in range(G):
                    lo(j + 2)
                    if added is not None and j == 0:
                        soft_context(added)
                    if soft is not None:
                        if j == 1:
                            soft_mean(soft[0], 1 - par)
                        if j == 3:
                            soft_scores(soft[0])
                        if j == 4:
                            soft_maxima(soft[0])
                        if j == 5:
                            soft_max(soft[0], soft[0] // PER_SEQ)
                        if j == 6:
                            soft_shift(soft[0])
                    v.wait_ge(s["sq_done"], base + (j + 1))
                    if j == 0:
                        ge(v, s["k_tot"], n * 2 - 1)
                    nc.vector.tensor_reduce(ksum[par][:, j, :], sq[j % 2][:, :].rearrange("p (h c) -> p h c", h=H), AX_X, ALU.add)\
                        .then_inc(s["summed"], 1)

            def last(soft, added):
                n = soft[0]
                soft_context(added)
                soft_mean(n, n % 2)
                soft_scores(n)
                soft_maxima(n)
                soft_max(n, n // PER_SEQ)
                soft_shift(n)
                soft_context(soft)

            groups(v, step, last)
            v.wait_ge(s["ctx_done"], GROUPS + 1)
            nc.vector.reciprocal(linv[:, :], ctxs[:, :, KVL:KVL + 1].rearrange("p b o -> p (b o)")).then_inc(s["final_inv"], 1)
            v.wait_ge(s["final_inv"], 1)
            nc.vector.tensor_mul(ctxs[:, :, 0:KVL], ctxs[:, :, 0:KVL], linv[:, :].unsqueeze(2).broadcast_to([HS, NSEQ, KVL]))\
                .then_inc(s["final_scaled"], 1)
            v.wait_ge(s["out_done"], 1)
            o = banks[0:VH, 1, 0:H * NS].rearrange("p (c a t) -> p c a t", a=2, t=NS)
            for a in range(2):
                nc.vector.tensor_copy(g.attnT[VH * a:VH * a + VH, :, TP:T], o[:, :, a, :]).then_inc(s["out_copied"], 1)
            v.wait_ge(s["out_copied"], 2)

        @block.tensor
        def _(pe):
            for opening in (*s["pages_free"], s["kn_done"], s["rp_done"]):
                pe.sem_inc(opening, 1)
            pe.wait_ge(s["q_squared"], 1)
            pe.matmul(banks[:, 0, 0:H * NS], g.ones[0:QK, :], st[0:QK, :, :].rearrange("p a b -> p (a b)"),
                      start=True, stop=True).then_inc(s["q_sum"], 1)
            pe.wait_ge(s["w_loaded"], 16)
            for x in range(H * KL):
                h, k = x // KL, x % KL
                mm = pe.transpose(banks[0:NOPE, 2 + x // 4, (x % 4) * P:(x % 4 + 1) * P], wkv[:, k, h * KW:h * KW + NOPE],
                                  ident[:, :])
            mm.then_inc(s["wT_done"], 1)
            pe.wait_ge(s["q_normed"], 1)
            pe.wait_ge(s["wT_copied"], 1)
            for h in range(H):
                for k in range(KL):
                    at = k * H * NS + h * NS
                    mm = pe.matmul(banks[:, 0, at:at + NS], wukT[0:NOPE, h * KL + k, :], g.qs[0:NOPE, h, :], start=True, stop=True)
            mm.then_inc(s["qab_done"], 1)
            for k in range(KL):
                mm = pe.matmul(banks[0:NS, 1, :], g.new_latT[:, k, :], nope[:, k * H:(k + 1) * H, 0:NOPE],
                               start=k == 0, stop=k == KL - 1)
            mm.then_inc(s["kn0_done"], 1)
            pe.wait_ge(s["qab_copied"], KL)
            for k in range(KL):
                pe.matmul(banks[0:NS, 6, 0:NSEQ * HS], g.new_latT[:, k, :], qab[:, :, k, :], start=k == 0, stop=k == KL - 1)
            pe.matmul(banks[0:NS, 7, 0:NSEQ * HS], g.kpe[NOPE:QK, TP:T],
                      g.qs[NOPE:QK, :, :].rearrange("p h (b s) -> p b h s", s=SDEC), start=True, stop=True).then_inc(s["s0_done"], 1)
            pe.wait_ge(s["s0_steps"], 4)
            for b in range(NSEQ):
                mm = pe.transpose(banks[0:HS, 6, b * NS:(b + 1) * NS], st[0:NS, b, :], ident[0:NS, 0:NS])
            mm.then_inc(s["s0_transposed"], 1)
            pe.wait_ge(s["p0_done"], 1)
            for b in range(NSEQ):
                mm = pe.transpose(banks[0:NS, 7, b * HS:(b + 1) * HS], sc[0][0:HS, b, :], ident[0:HS, 0:HS])
            mm.then_inc(s["p0_transposed"], 1)
            pe.wait_ge(s["p0_copied"], 1)
            for b in range(NSEQ):
                mm = pe.matmul(banks[0:HS, 2 + b // 2, (b % 2) * KVL:(b % 2 + 1) * KVL], pr[0:NS, b, :], g.new_page[:, 0:KVL],
                               start=True, stop=True)
            mm.then_inc(s["ctx0_done"], 1)
            pe.wait_ge(s["ctx0_copied"], 1)

            def spread_max(n):
                pe.wait_ge(s["diag_done"], n + 1)
                pe.matmul(banks[:, 7, MB:MB + HS], g.ones[0:HS, :], diag[:, :], start=True, stop=True).then_inc(s["max_spread"], 1)

            def transpose_max(n):
                pe.wait_ge(s["maxed"], n + 1)
                ge(pe, s["ctx_done"], n + 1)
                pe.transpose(banks[0:HS, 7, MT:MT + P], mx[:, :], ident[:, :]).then_inc(s["max_transposed"], 1)

            def context(group):
                n, q, _ = group
                pe.wait_ge(s["exped"], n + 1)
                for j in range(G):
                    mm = pe.matmul(banks[0:HS, 7, CT:CT + KVL + 1], pr[:, j, :], X[q][:, j, 0:KVL + 1],
                                   start=j == 0, stop=j == G - 1)
                mm.then_inc(s["pages_free"][q], 1)

            def step(group, soft, _):
                n, q, fill = group
                base, par = n * G, q % 2

                def transposes(j):
                    page = following(group, j)
                    if page:
                        at, turn, place = page
                        if place == 0:
                            pe.wait_ge(loaded[at], turn * (16 * G) + 16 * G)
                        ge(pe, s["lo_done"], base + (j - 1))
                        for k in range(KL):
                            mm = pe.transpose(pageT(j)[:, k * P:(k + 1) * P], X[at][:, place, k * P:(k + 1) * P], ident[:, :])
                        mm.then_inc(s["x_transposed"], 1)

                def expand(j):
                    pe.wait_ge(s["lo_done"], base + (j + 1))
                    ge(pe, s["sq_done"], base + (j - 1))
                    ge(pe, s["sc_copied"], base + (j - 1))
                    for k in range(KL):
                        for x, w, a in ((xT_hi, comb_hi, 0), (xT_hi, comb_lo, 1), (xT_lo, comb_hi, 2)):
                            for half in range(2):
                                mm = pe.matmul(banks[:, 2 * (j % 2) + half, 0:WC], x[j % AHEAD][:, k, :], w[par][:, k, half, :],
                                               start=k == 0 and a == 0, stop=k == KL - 1 and a == 2)
                    mm.then_inc(s["kn_done"], 1)

                if soft is None:
                    transposes(0)
                    transposes(1)
                for j in range(G):
                    transposes(j + 2)
                    if j == 0:
                        pe.wait_ge(s["comb_ready"], n * 2 + 2)
                    if soft is not None:
                        if j == 5:
                            transpose_max(soft[0])
                        if j == 6:
                            spread_max(soft[0])
                    expand(j)
                    if j == 3:
                        pe.wait_ge(ropes_loaded[q], fill * (16 * G) + 16 * G)
                        ge(pe, s["s_added"], n + 1)
                        for x in range(2):
                            mm = pe.transpose(banks[:, 6, x * P:(x + 1) * P], R[q][:, x * P:(x + 1) * P], ident[:, :])
                        mm.then_inc(s["r_transposed"], 1)
                    if j == 6:
                        pe.wait_ge(s["r_copied"], n + 1)
                        pe.wait_ge(s["qbd_ready"], n + 1)
                        for x in range(2):
                            mm = pe.matmul(banks[:, 6, (2 + x) * P:(3 + x) * P], rT[:, x * P:(x + 1) * P],
                                           qbd[par][:, :, :].rearrange("p a b -> p (a b)"), start=True, stop=True)
                        mm.then_inc(s["rp_done"], 1)
                if soft is not None:
                    context(soft)

            def last(soft, _):
                transpose_max(soft[0])
                spread_max(soft[0])
                context(soft)

            groups(pe, step, last)
            pe.wait_ge(s["final_scaled"], 1)
            for k in range(KL):
                for b in range(NSEQ):
                    at = (k * NSEQ + b) * HS
                    mm = pe.transpose(banks[:, 0, at:at + HS], ctxs[:, b, k * P:(k + 1) * P], ident[0:HS, 0:HS])
            mm.then_inc(s["ctxT_done"], 1)
            pe.wait_ge(s["ctxT_copied"], 1)
            cT = wukT[:, 0:2 * NSEQ * HS // P, :].rearrange("p a b -> p (a b)")\
                .rearrange("p (k b h s) -> p k b h s", k=KL, b=NSEQ, h=H)
            for h in range(H):
                for k in range(KL):
                    mm = pe.matmul(banks[0:VH, 1, h * NS:(h + 1) * NS], wkv[:, k, h * KW + NOPE:(h + 1) * KW], cT[:, k, :, h, :],
                                   start=k == 0, stop=k == KL - 1)
            mm.then_inc(s["out_done"], 1)


def output_projection(g):
    nc, A, sem, zT, banks = g.nc, g.A, g.sem, g.zT, g.banks
    top = Arena(nc, g.h_at, g.top)
    mix_hi, mix_lo = top.take("mix_hi", [P, KD, TT], F32R), top.take("mix_lo", [P, KD, TT], F32R)
    ar = Arena(nc, g.z_hc_at, g.h_at)
    scr = norm_scratch("mix_norms", ar)
    ring = Ring(sem, "w_o", ar, KD)
    conv = Norm(nc, sem, "convnorm", scr, lambda c: zT[:, Z_GB + c, :], KC, CW,
                lambda c: g.gcol[:, G_CONV + c:G_CONV + c + 1], lambda c: mix_hi[:, KC + c, :],
                lambda c: mix_lo[:, KC + c, :], banks[:, 0:3, :], g.ones)
    att = Norm(nc, sem, "attnorm", scr, lambda c: g.attnT[:, c, :], KC, AW,
               lambda c: g.gcol[:, G_ATT + c:G_ATT + c + 1], lambda c: mix_hi[:, c, :],
               lambda c: mix_lo[:, c, :], banks[:, 3:6, :], g.ones)
    w = A["w_o"].rearrange("(k p) n -> p k n", p=P)

    with nc.Block() as block:
        @block.sync
        def _(sp):
            with sp.Fori(0, KD // 2) as i:
                for s in range(2):
                    sp.wait_ge(ring.lo_done[s], i + 1)
                    sp.dma_start(ring.raw[s][:, :, :], w[:, :, ds(i * (2 * P) + s * P, P)]).then_inc(ring.loaded[s], 16)

        @block.scalar
        def _(act):
            conv.act(act)
            att.act(act)
            with act.Fori(0, KD // 2) as i:
                for s in range(2):
                    ring.split_hi(act, s, i)

        @block.gpsimd
        def _(pool):
            ring.open(pool, ring.lo_done)
            conv.pool(pool)
            att.pool(pool)
            with pool.Fori(0, KD // 2) as i:
                for s in range(2):
                    ring.split_lo(nc, pool, s, i)

        @block.tensor
        def _(pe):
            ring.open(pe, ring.used)
            conv.pe(pe)
            att.pe(pe)
            pe.wait_ge(att.lo_done, KC)
            pe.wait_ge(conv.lo_done, KC)
            pe.wait_ge(conv.mean, 1)
            pe.wait_ge(att.mean, 1)
            with pe.Fori(0, KD // 2) as i:
                for s in range(2):
                    pe.wait_ge(ring.evacuated[s], i + 1)
                    ring.products(pe, s, i, banks[:, 3 * s:3 * s + 3, :],
                                  lambda k: mix_hi[:, k, :], lambda k: mix_lo[:, k, :])

        @block.vector
        def _(v):
            ring.open(v, ring.evacuated)
            conv.dve(v)
            v.wait_ge(conv.lo_done, KC)
            v.wait_ge(conv.norm, KC)
            att.dve(v)
            with v.Fori(0, KD // 2) as i:
                for s in range(2):
                    v.wait_ge(ring.used[s], i + 2)
                    x = g.xT[:, ds(i * 2 + s, 1), :].rearrange("p o (b t) -> p (o b) t", b=NBLK)
                    nc.vector.tensor_add(x, x, banks[:, 3 * s:3 * s + 3, 0:TB]).then_inc(ring.evacuated[s], 1)


def mlp(g):
    nc, A, sem, banks, xT = g.nc, g.A, g.sem, g.banks, g.xT
    FC = 4
    GROUPS = DFF // (FC * P)
    top = Arena(nc, g.h_at, g.top)
    hf_hi, hf_lo = top.take("hf_hi", [P, KD, TT], F32R), top.take("hf_lo", [P, KD, TT], F32R)
    ar = Arena(nc, g.start, g.h_at)
    a_hi, a_lo = ar.take("a_hi", [P, FC, TT], F32R), ar.take("a_lo", [P, FC, TT], F32R)
    up = Ring(sem, "w_up", ar, KD)
    down = Ring(sem, "w_down", ar, FC)
    scr = norm_scratch("ffn_norm", ar)
    norm = Norm(nc, sem, "ffnnorm", scr, lambda c: xT[:, c, :], KD, D, lambda c: g.gcol[:, G_FFN + c:G_FFN + c + 1],
                lambda c: hf_hi[:, c, :], lambda c: hf_lo[:, c, :], banks[:, 0:3, :], g.ones)
    relu, full = scr[0], scr[2]
    relu_done = sem("relu_done")
    hi_done, sq_done, act_ready = sem("a_hi_done"), sem("a_squared"), sem("a_ready")
    w_up = A["w_up"].rearrange("(k p) n -> p k n", p=P)
    w_down = A["w_down"].rearrange("(g k p) n -> p g k n", k=FC, p=P)
    per = KD // 2

    with nc.Block() as block:
        @block.sync
        def _(sp):
            with sp.Fori(0, GROUPS) as i:
                for f in range(FC):
                    s = f % 2
                    sp.wait_ge(up.lo_done[s], i * (FC // 2) + (f // 2 + 1))
                    sp.dma_start(up.raw[s][:, :, :], w_up[:, :, ds(i * (FC * P) + f * P, P)])\
                        .then_inc(up.loaded[s], 16)
                for m in range(KD):
                    s = m % 2
                    sp.wait_ge(down.lo_done[s], i * per + (m // 2 + 1))
                    sp.dma_start(down.raw[s][:, :, :],
                                 w_down[:, ds(i, 1), :, m * P:(m + 1) * P].rearrange("p o k n -> p (o k) n"))\
                        .then_inc(down.loaded[s], 16)

        @block.scalar
        def _(act):
            norm.act(act)
            act.wait_ge(norm.lo_done, KD)
            with act.Fori(0, GROUPS) as i:
                up.split_hi(act, 0, i * 2)
                for f in range(FC):
                    if f + 1 < FC:
                        up.split_hi(act, (f + 1) % 2, i * 2 + (f + 1) // 2)
                    else:
                        down.split_hi(act, 0, i * per)
                    act.wait_ge(up.used[f % 2], i * 2 + (f // 2 + 2))
                    act.wait_ge(act_ready, i * FC + max(f, 1))
                    act.activation(relu[:, f % 2, :].rearrange("p (b t) -> p b t", b=NBLK),
                                   banks[:, 3 * (f % 2):3 * (f % 2) + 3, 0:TB], ACT.Relu)\
                        .then_inc(up.evacuated[f % 2], 1)
                    act.wait_ge(up.evacuated[f % 2], i * 2 + (f // 2 + 1))
                    act.activation(a_hi[:, f, :], relu[:, f % 2, :], ACT.Square).then_inc(hi_done, 1)
                for m in range(1, KD):
                    down.split_hi(act, m % 2, i * per + m // 2)

        @block.gpsimd
        def _(pool):
            up.open(pool, up.lo_done)
            down.open(pool, down.lo_done)
            norm.pool(pool)
            with pool.Fori(0, GROUPS) as i:
                for f in range(FC):
                    up.split_lo(nc, pool, f % 2, i * 2 + f // 2)
                for m in range(KD):
                    down.split_lo(nc, pool, m % 2, i * per + m // 2)

        @block.tensor
        def _(pe):
            up.open(pe, up.used)
            down.open(pe, down.used)
            norm.pe(pe)
            pe.wait_ge(norm.lo_done, KD)
            pe.wait_ge(norm.mean, 1)
            with pe.Fori(0, GROUPS) as i:
                for f in range(FC):
                    s = f % 2
                    if f < 2:
                        pe.wait_ge(down.evacuated[s], i * per + 1)
                    else:
                        pe.wait_ge(up.evacuated[s], i * 2 + 1)
                    up.products(pe, s, i * 2 + f // 2, banks[:, 3 * s:3 * s + 3, :],
                                lambda k: hf_hi[:, k, :], lambda k: hf_lo[:, k, :])
                for m in range(KD):
                    s = m % 2
                    if m < 2:
                        pe.wait_ge(up.evacuated[s], i * 2 + 2)
                    else:
                        pe.wait_ge(down.evacuated[s], i * per + (m // 2 + 1))

                    def hidden(k, m=m):
                        if m == 0:
                            pe.wait_ge(act_ready, i * FC + (k + 2))
                    down.products(pe, s, i * per + m // 2, banks[:, 3 * s:3 * s + 3, :],
                                  lambda k: a_hi[:, k, :], lambda k: a_lo[:, k, :], first=hidden)

        @block.vector
        def _(v):
            down.open(v, down.evacuated)
            down.open(v, [act_ready])
            norm.dve(v)
            v.wait_ge(norm.lo_done, KD)
            v.wait_ge(norm.norm, KD)
            with v.Fori(0, GROUPS) as i:
                for f in range(FC):
                    s = f % 2
                    v.wait_ge(up.evacuated[s], i * 2 + (f // 2 + 1))
                    v.wait_ge(act_ready, i * FC + max(f, 1))
                    nc.vector.tensor_mul(full[:, s, :], relu[:, s, :], relu[:, s, :]).then_inc(sq_done, 1)
                    v.wait_ge(sq_done, i * FC + (f + 1))
                    v.wait_ge(hi_done, i * FC + (f + 1))
                    nc.vector.tensor_sub(a_lo[:, f, :], full[:, s, :], a_hi[:, f, :].bitcast(F32))\
                        .then_inc(act_ready, 1)
                for m in range(KD):
                    s = m % 2
                    v.wait_ge(down.used[s], i * per + (m // 2 + 2))
                    v.wait_ge(down.evacuated[s], i * per + (m // 2 + 1))
                    x = xT[:, m, :].rearrange("p (b t) -> p b t", b=NBLK)
                    nc.vector.tensor_add(x, x, banks[:, 3 * s:3 * s + 3, 0:TB]).then_inc(down.evacuated[s], 1)


def store_outputs(g):
    nc, A, sem, banks, xT = g.nc, g.A, g.sem, g.banks, g.xT
    ar = Arena(nc, g.start, g.top)
    y = [ar.take(f"y_tile{i}", [P, D], F32) for i in range(3)]
    tiles = [(META + t * P, P, A["out_y_prompt"][t * P:(t + 1) * P, :]) for t in range(SEQ // P)]
    tiles.append((TP, NS, A["out_y_sample"]))
    transposed, low_copied, high_copied = sem("y_transposed"), sem("y_low_copied"), sem("y_high_copied")
    stored = [sem(f"y_stored{i}") for i in range(3)]

    with nc.Block() as block:
        @block.tensor
        def _(pe):
            for t, (at, n, _) in enumerate(tiles):
                if t >= 4:
                    pe.wait_ge(low_copied, t - 3)
                    pe.wait_ge(high_copied, t - 3)
                for k in range(KD):
                    mm = pe.transpose(banks[0:n, 2 * (t % 4) + k // 4, (k % 4) * P:(k % 4 + 1) * P],
                                      xT[:, k, at:at + n], g.ident[:, :])
                mm.then_inc(transposed, 1)

        @block.scalar
        def _(act):
            for t, (at, n, _) in enumerate(tiles):
                act.wait_ge(transposed, t + 1)
                if t >= 3:
                    act.wait_ge(stored[t % 3], 16 * (t // 3))
                act.copy(y[t % 3][0:n, 0:BANK], banks[0:n, 2 * (t % 4), :]).then_inc(low_copied, 1)

        @block.vector
        def _(v):
            for t, (at, n, _) in enumerate(tiles):
                v.wait_ge(transposed, t + 1)
                if t >= 3:
                    v.wait_ge(stored[t % 3], 16 * (t // 3))
                nc.vector.tensor_copy(y[t % 3][0:n, BANK:D], banks[0:n, 2 * (t % 4) + 1, :]).then_inc(high_copied, 1)

        @block.sync
        def _(sp):
            for t, (at, n, out) in enumerate(tiles):
                sp.wait_ge(low_copied, t + 1)
                sp.wait_ge(high_copied, t + 1)
                sp.dma_start(out, y[t % 3][0:n, :]).then_inc(stored[t % 3], 16)
            for i in range(3):
                sp.wait_ge(stored[i], 16 * len(tiles[i::3]))


_OUTS = [("y_prompt", (SEQ, D)), ("y_sample", (NS, D)), ("new_lat_prompt", (TP, KVL)), ("new_kpe_prompt", (TP, ROPE)),
         ("new_conv_prompt", (2, CW)), ("new_lat_sample", (NS, KVL)), ("new_kpe_sample", (NS, ROPE)),
         ("new_conv_sample", (NSEQ, 2, CW))]


def rope_table():
    import numpy as np
    inv = (np.float32(10000.0) ** (-(np.arange(0, ROPE, 2, dtype=np.float32) / np.float32(ROPE)))).astype(np.float32)
    pos = np.concatenate([np.arange(TP), np.tile(PAST + np.arange(SDEC), NSEQ)]).astype(np.float32)
    ang = pos[None, :] * inv[:, None]
    out = np.zeros((2 * ROPE, TT), np.float32)
    c, s = np.cos(ang), np.sin(ang)
    out[:, :T] = np.concatenate([c, c, -s, s], axis=0)
    return out


def kernel(x_prompt, x_sample, cache_kv_latent, cache_k_rope, state_conv, page_table, meta_tokens,
           norm_mix_g, w_in, q_lora_g, kv_lora_g, w_uq, w_ukv, q_norm_g, k_norm_g, conv_w, conv_b,
           attn_out_g, conv_out_g, w_o, norm_ffn_g, w_up, w_down):
    import numpy as np
    from concourse import bacc
    from concourse.bass_utils import run_bass_kernel_spmd

    nc = bacc.Bacc("TRN2", target_bir_lowering=False, num_devices=1)
    given = dict(x_prompt=x_prompt, x_sample=x_sample, cache_kv_latent=cache_kv_latent, cache_k_rope=cache_k_rope,
                 state_conv=state_conv, page_table=page_table, meta_tokens=meta_tokens, norm_mix_g=norm_mix_g,
                 w_in=w_in, q_lora_g=q_lora_g, kv_lora_g=kv_lora_g, w_uq=w_uq, w_ukv=w_ukv, q_norm_g=q_norm_g,
                 k_norm_g=k_norm_g, conv_w=conv_w, conv_b=conv_b, attn_out_g=attn_out_g, conv_out_g=conv_out_g,
                 w_o=w_o, norm_ffn_g=norm_ffn_g, w_up=w_up, w_down=w_down)
    npool = cache_kv_latent.shape[1]
    shapes = dict(x_prompt=(SEQ, D), x_sample=(NS, D), cache_kv_latent=(npool, PAGE, KVL),
                  cache_k_rope=(npool, PAGE, ROPE), state_conv=(NSEQ * 2, CW), page_table=(1, NSEQ * NPAGES),
                  norm_mix_g=(D,), w_in=w_in.shape[1:], q_lora_g=(QL,), kv_lora_g=(KVL,), w_uq=w_uq.shape[1:],
                  w_ukv=w_ukv.shape[1:], q_norm_g=(QK,), k_norm_g=(QK,), conv_w=(3 * CW,), conv_b=(CW,),
                  attn_out_g=(AW,), conv_out_g=(CW,), w_o=(D, D), norm_ffn_g=(D,), w_up=(D, DFF), w_down=(DFF, D))
    arrays, A = {}, {}
    given["rope_table"] = rope_table()
    for name, a in given.items():
        a = np.ascontiguousarray(np.asarray(a)).reshape(shapes.get(name, np.shape(a)))
        arrays[f"in_{name}"] = a
        A[name] = nc.dram_tensor(f"in_{name}", a.shape, mybir.dt.from_np(a.dtype), kind="ExternalInput").ap()
    for name, shape in _OUTS:
        A["out_" + name] = nc.dram_tensor(f"out_{name}", shape, F32, kind="ExternalOutput").ap()
    program(nc, A)
    r = run_bass_kernel_spmd(nc, [arrays], core_ids=[0])
    o = r.results[0]
    return (o["out_y_prompt"].reshape(1, SEQ, D), o["out_y_sample"].reshape(NSEQ, SDEC, D),
            o["out_new_lat_prompt"].reshape(1, 1, TP, KVL), o["out_new_kpe_prompt"].reshape(1, 1, TP, ROPE),
            o["out_new_conv_prompt"].reshape(1, 1, 2, CW), o["out_new_lat_sample"].reshape(1, NSEQ, SDEC, KVL),
            o["out_new_kpe_sample"].reshape(1, NSEQ, SDEC, ROPE), o["out_new_conv_sample"].reshape(1, NSEQ, 2, CW))
```

```python
from contextlib import ExitStack

import concourse.bass as bass
from concourse import mybir

F32 = mybir.dt.float32
F32R = mybir.dt.float32r
I32 = mybir.dt.int32
BF16 = mybir.dt.bfloat16
ALU = mybir.AluOpType
ACT = mybir.ActivationFunctionType
AX_X = mybir.AxisListType.X
ds = bass.ds

P = 128
D = 1024
KD = D // P
META, SEQ = 16, 1024
TP = META + SEQ
NSEQ, SDEC = 8, 4
NS = NSEQ * SDEC
T = TP + NS
NBLK = 3
TB = 2 * -(-T // (2 * NBLK))
TT = NBLK * TB
PAGE, NPAGES, PAST = 128, 32, 4096
H, NOPE, ROPE, VH = 8, 64, 32, 64
QK = NOPE + ROPE
QL, KVL = 384, 256
KQ, KL = QL // P, KVL // P
AW = H * VH
CW = D - AW
KC = CW // P
DFF = 4 * D
EPS = 1e-6
SCALE = QK ** -0.5
NT = -(-T // P)
TQ = NT * P
BANK = 512
MASKED = -1.0e30

G_MIX, G_QL, G_KVL = 0, 8, 11
G_ATT, G_CONV, G_FFN = 13, 17, 21
G_CW, G_CB = 29, 41
G_QN, G_KN = 45, 46
G_ROWS = 47

Z_CQ, Z_CKV, Z_KPE, Z_GB, Z_GC, Z_HC = 0, 3, 5, 6, 10, 14
NZ = 18


class Shared:

    def __init__(self, nc, arrays, banks):
        self.nc, self.A, self.banks = nc, arrays, banks


class Arena:

    def __init__(self, nc, start, end):
        self.nc, self.at, self.end = nc, start, end

    def take(self, name, shape, dtype):
        size = 2 if dtype == BF16 else 4
        for n in shape[1:]:
            size *= n
        t = self.nc.alloc_sbuf_tensor_at(name, shape, dtype, offset=self.at)
        self.at += -(-size // 32) * 32
        assert self.at <= self.end, (name, self.at, self.end)
        return t

    def skip(self, size):
        a = self.at
        self.at += -(-size // 32) * 32
        assert self.at <= self.end
        return a


def norm_scratch(name, arena):
    return (arena.take(f"{name}_sq", [P, 2, TT], F32), arena.take(f"{name}_ms", [P, TT], F32),
            arena.take(f"{name}_scaled", [P, 2, TT], F32))


class Norm:

    def __init__(self, nc, sem, name, scratch, src, K, width, gain, hi, lo, ss, ones, full=None):
        self.nc, self.src, self.K, self.width, self.gain = nc, src, K, width, gain
        self.hi, self.lo, self.ss, self.ones, self.full = hi, lo, ss, ones, full
        self.sq, self.ms, self.scaled = scratch
        self.squared = sem(f"{name}_squared")
        self.summed = sem(f"{name}_summed")
        self.mean = sem(f"{name}_mean")
        self.root = sem(f"{name}_root")
        self.inv = sem(f"{name}_inv")
        self.norm = sem(f"{name}_norm")
        self.hi_done = sem(f"{name}_hi_done")
        self.lo_done = sem(f"{name}_lo_done")

    def act(self, act):
        for c in range(self.K):
            if c >= 2:
                act.wait_ge(self.summed, c - 1)
            act.activation(self.sq[:, c % 2, :], self.src(c), ACT.Square).then_inc(self.squared, 1)
        act.wait_ge(self.mean, 1)
        act.activation(self.ms[:, :], self.ms[:, :], ACT.Sqrt).then_inc(self.root, 1)
        for c in range(self.K):
            act.wait_ge(self.norm, c + 1)
            act.copy(self.hi(c), self.buf(c)).then_inc(self.hi_done, 1)

    def pe(self, pe):
        for c in range(self.K):
            pe.wait_ge(self.squared, c + 1)
            for b in range(NBLK):
                mm = pe.matmul(self.ss[:, b, 0:TB], self.ones[:, :], self.sq[:, c % 2, b * TB:(b + 1) * TB],
                               start=c == 0, stop=c == self.K - 1)
            mm.then_inc(self.summed, 1)

    def buf(self, c):
        return self.full(c) if self.full else self.scaled[:, c % 2, :]

    def dve(self, v):
        nc = self.nc
        v.wait_ge(self.summed, self.K)
        nc.vector.tensor_scalar(self.ms[:, :].rearrange("p (b t) -> p b t", b=NBLK), self.ss[:, :, 0:TB],
                                1.0 / self.width, EPS, ALU.mult, ALU.add).then_inc(self.mean, 1)
        v.wait_ge(self.root, 1)
        nc.vector.reciprocal(self.ms[:, :], self.ms[:, :]).then_inc(self.inv, 1)
        v.wait_ge(self.inv, 1)
        for c in range(self.K):
            if c >= 2 and not self.full:
                v.wait_ge(self.lo_done, c - 1)
            nc.vector.scalar_tensor_tensor(self.buf(c), self.src(c), self.gain(c), self.ms[:, :],
                                           ALU.mult, ALU.mult).then_inc(self.norm, 1)

    def pool(self, pool):
        for c in range(self.K):
            pool.wait_ge(self.hi_done, c + 1)
            self.nc.gpsimd.tensor_sub(self.lo(c), self.buf(c), self.hi(c).bitcast(F32)).then_inc(self.lo_done, 1)


class Ring:

    def __init__(self, sem, name, arena, K, slots=2):
        self.K = K
        self.raw = [arena.take(f"{name}_raw{s}", [P, K, P], F32) for s in range(slots)]
        self.hi = [arena.take(f"{name}_hi{s}", [P, K, P], F32R) for s in range(slots)]
        self.lo = [arena.take(f"{name}_lo{s}", [P, K, P], F32R) for s in range(slots)]
        self.loaded = [sem(f"{name}_loaded{s}") for s in range(slots)]
        self.hi_done = [sem(f"{name}_hi_done{s}") for s in range(slots)]
        self.lo_done = [sem(f"{name}_lo_done{s}") for s in range(slots)]
        self.used = [sem(f"{name}_used{s}") for s in range(slots)]
        self.evacuated = [sem(f"{name}_evacuated{s}") for s in range(slots)]

    def open(self, engine, semaphores):
        for x in semaphores:
            engine.sem_inc(x, 1)

    def split_hi(self, act, s, n, loads=1):
        act.wait_ge(self.loaded[s], (n + 1) * (16 * loads))
        act.wait_ge(self.used[s], n + 1)
        act.copy(self.hi[s][:, :, :], self.raw[s][:, :, :]).then_inc(self.hi_done[s], 1)

    def split_lo(self, nc, pool, s, n):
        pool.wait_ge(self.hi_done[s], n + 1)
        nc.gpsimd.tensor_sub(self.lo[s][:, :, :], self.raw[s][:, :, :],
                             self.hi[s][:, :, :].bitcast(F32)).then_inc(self.lo_done[s], 1)

    def products(self, pe, s, n, out, xhi, xlo, first=None):
        pe.wait_ge(self.lo_done[s], n + 2)
        for k in range(self.K):
            if first is not None:
                first(k)
            for w, x, a in ((self.hi, xhi, 0), (self.hi, xlo, 1), (self.lo, xhi, 2)):
                for b in range(NBLK):
                    mm = pe.matmul(out[:, b, 0:TB], w[s][:, k, :], x(k)[:, b * TB:(b + 1) * TB],
                                   start=k == 0 and a == 0, stop=k == self.K - 1 and a == 2)
        mm.then_inc(self.used[s], 1)


def program(nc, A):
    ctx = ExitStack()
    with ctx:
        def sem(name):
            return ctx.enter_context(nc.semaphore(name))

        banks = ctx.enter_context(nc.psum_tensor("banks", [P, 8, BANK], F32))
        g = Shared(nc, A, banks)
        g.done = sem("stores_done")
        low = -(-nc.sbuf_base // 32) * 32
        top = nc.sbuf_usable_end // 32 * 32
        fixed = Arena(nc, low, top)
        g.ident = fixed.take("ident", [P, P], F32)
        g.ones = fixed.take("ones", [P, P], F32)
        g.gcol = fixed.take("gain_columns", [P, G_ROWS], F32)
        g.cs_at = fixed.at
        g.cs = fixed.take("cos_sin", [P, TT], F32)
        g.cs_end = fixed.at
        g.xT = fixed.take("xT", [P, KD, TT], F32)
        g.start, g.top = fixed.at, top
        U = TT * 4
        g.h_at = top - 16 * U
        g.z_at = g.start
        for phase in (load_inputs, project_inputs, norms_and_conv, expand_heads, prompt_attention, sample_attention,
                      output_projection, mlp, store_outputs):
            own = []

            def own_semaphore(name):
                own.append(nc.alloc_semaphore(f"{phase.__name__}_{name}"))
                return own[-1]

            g.sem = own_semaphore
            phase(g)
            nc.clear_and_free_semaphores(own)
            nc.all_engine_barrier()


def load_inputs(g):
    nc, A, sem = g.nc, g.A, g.sem
    ar = Arena(nc, g.start, g.h_at)
    top = Arena(nc, g.h_at, g.top)
    g.h_hi = top.take("h_hi", [P, KD, TT], F32R)
    g.h_lo = top.take("h_lo", [P, KD, TT], F32R)
    xt = [ar.take(f"x_tile{i}", [P, D], F32) for i in range(3)]
    grow = ar.take("gain_rows", [G_ROWS, P], F32)
    x_loaded = [sem(f"x_loaded{i}") for i in range(3)]
    gains_loaded, table_loaded = sem("gains_loaded"), sem("table_loaded")
    gains_zeroed, consts = sem("gains_zeroed"), sem("consts")
    x_transposed = sem("x_transposed")
    low_copied, high_copied = sem("low_chunks_copied"), sem("high_chunks_copied")
    g_transposed, g_copied = sem("g_transposed"), sem("g_copied")
    xT, ident, banks = g.xT, g.ident, g.banks
    gbank = banks[:, 7, 0:G_ROWS]
    norm = Norm(nc, sem, "mixnorm", norm_scratch("mixnorm", ar), lambda c: xT[:, c, :], KD, D, lambda c: g.gcol[:, G_MIX + c:G_MIX + c + 1],
                lambda c: g.h_hi[:, c, :], lambda c: g.h_lo[:, c, :], banks[:, 4:7, :], g.ones)
    parts = []
    for t in range(NT):
        at, rows = t * P, min(P, T - t * P)
        p = []
        for name, first, n in (("meta_tokens", 0, META), ("x_prompt", META, SEQ), ("x_sample", TP, NS)):
            a, b = max(at, first), min(at + rows, first + n)
            if a < b:
                p.append((a - at, b - at, A[name][a - first:b - first, :]))
        parts.append((rows, p))
    ends = [0, 0, 0]
    loaded_at = []
    for t, (_, p) in enumerate(parts):
        ends[t % 3] += 16 * len(p)
        loaded_at.append(ends[t % 3])

    with nc.Block() as block:
        @block.sync
        def _(sp):
            for t, (_, p) in enumerate(parts):
                if t >= 3:
                    sp.wait_ge(x_transposed, t - 2)
                for a, b, src in p:
                    sp.dma_start(xt[t % 3][a:b, :], src).then_inc(x_loaded[t % 3], 16)

        @block.gpsimd
        def _(pool):
            nc.gpsimd.memset(ident[:, :], 0.0).then_inc(consts, 1)
            nc.gpsimd.memset(g.ones[:, :], 1.0).then_inc(consts, 1)
            nc.gpsimd.memset(xT[:, :, T:TT], 0.0).then_inc(consts, 1)
            pool.wait_ge(consts, 3)
            nc.gpsimd.affine_select(out=ident[:, :], in_=ident[:, :], compare_op=ALU.not_equal, fill=1.0, base=0,
                                    pattern=[[-1, P]], channel_multiplier=1).then_inc(consts, 1)
            norm.pool(pool)

        @block.scalar
        def _(act):
            act.wait_ge(gains_zeroed, 1)
            for name, row in (("norm_mix_g", G_MIX), ("q_lora_g", G_QL), ("kv_lora_g", G_KVL), ("attn_out_g", G_ATT),
                              ("conv_out_g", G_CONV), ("norm_ffn_g", G_FFN), ("conv_w", G_CW), ("conv_b", G_CB)):
                v = A[name].rearrange("(k p) -> k p", p=P)
                act.dma_start(grow[row:row + v.shape[0], :], v).then_inc(gains_loaded, 16)
            for name, row in (("q_norm_g", G_QN), ("k_norm_g", G_KN)):
                act.dma_start(grow[row:row + 1, 0:QK], A[name].rearrange("(o n) -> o n", o=1)).then_inc(gains_loaded, 16)
            act.dma_start(g.cs[NOPE:P, :], A["rope_table"]).then_inc(table_loaded, 16)
            for t in range(NT):
                rows = parts[t][0]
                act.wait_ge(x_transposed, t + 1)
                act.copy(xT[:, 0:KD // 2, t * P:t * P + rows],
                         banks[:, 2 * (t % 2), :].rearrange("p (k t) -> p k t", t=P)[:, :, 0:rows]).then_inc(low_copied, 1)
            act.wait_ge(low_copied, NT)
            act.wait_ge(high_copied, NT)
            act.wait_ge(consts, 3)
            norm.act(act)
            act.wait_ge(table_loaded, 16)

        @block.vector
        def _(v):
            nc.vector.memset(grow[:, :], 0.0).then_inc(gains_zeroed, 1)
            for t in range(NT):
                rows = parts[t][0]
                v.wait_ge(x_transposed, t + 1)
                nc.vector.tensor_copy(xT[:, KD // 2:KD, t * P:t * P + rows],
                                      banks[:, 2 * (t % 2) + 1, :].rearrange("p (k t) -> p k t", t=P)[:, :, 0:rows])\
                    .then_inc(high_copied, 1)
            v.wait_ge(g_transposed, 1)
            nc.vector.tensor_copy(g.gcol[:, :], gbank).then_inc(g_copied, 1)
            v.wait_ge(g_copied, 1)
            norm.dve(v)

        @block.tensor
        def _(pe):
            pe.wait_ge(consts, 4)
            for t in range(NT):
                rows = parts[t][0]
                pe.wait_ge(x_loaded[t % 3], loaded_at[t])
                if t >= 2:
                    pe.wait_ge(low_copied, t - 1)
                    pe.wait_ge(high_copied, t - 1)
                for k in range(KD):
                    mm = pe.transpose(banks[:, 2 * (t % 2) + k // 4, (k % 4) * P:(k % 4) * P + rows],
                                      xt[t % 3][0:rows, k * P:(k + 1) * P], ident[0:rows, 0:rows])
                mm.then_inc(x_transposed, 1)
            pe.wait_ge(gains_loaded, 16 * 10)
            pe.transpose(gbank, grow[:, :], ident[0:G_ROWS, 0:G_ROWS]).then_inc(g_transposed, 1)
            norm.pe(pe)


def project_inputs(g):
    nc, A, sem = g.nc, g.A, g.sem
    ar = Arena(nc, g.z_at, g.h_at)
    g.zT = ar.take("zT", [P, NZ, TT], F32)
    g.z_end = ar.at
    g.conv_at = g.z_at + Z_GB * TT * 4
    g.z_hc_at = g.z_at + -(-Z_GC * TT * 4 // 32) * 32
    ring = Ring(sem, "w_in", ar, KD)
    zT, banks = g.zT, g.banks
    w = A["w_in"].rearrange("(k p) n -> p k n", p=P)
    kpe0 = QL + KVL
    half = ROPE // 2

    with nc.Block() as block:
        @block.sync
        def _(sp):
            def free(s, n):
                sp.wait_ge(ring.lo_done[s], n + 1)

            for n in range(2):
                for s in range(2):
                    free(s, n)
                    c = 2 * n + s
                    sp.dma_start(ring.raw[s][:, :, :], w[:, :, c * P:(c + 1) * P]).then_inc(ring.loaded[s], 16)
            free(0, 2)
            sp.dma_start(ring.raw[0][:, :, :], w[:, :, 4 * P:5 * P]).then_inc(ring.loaded[0], 16)
            free(1, 2)
            for at in (0, 2 * ROPE):
                sp.dma_start(ring.raw[1][:, :, at:at + ROPE], w[:, :, kpe0:kpe0 + ROPE]).then_inc(ring.loaded[1], 16)
                sp.dma_start(ring.raw[1][:, :, at + ROPE:at + ROPE + half],
                             w[:, :, kpe0 + half:kpe0 + ROPE]).then_inc(ring.loaded[1], 16)
                sp.dma_start(ring.raw[1][:, :, at + ROPE + half:at + 2 * ROPE],
                             w[:, :, kpe0:kpe0 + half]).then_inc(ring.loaded[1], 16)
            with sp.Fori(3, NZ // 2) as i:
                for s in range(2):
                    free(s, i)
                    sp.dma_start(ring.raw[s][:, :, :],
                                 w[:, :, ds(i * (2 * P) + (kpe0 + ROPE - 6 * P + s * P), P)])\
                        .then_inc(ring.loaded[s], 16)

        @block.scalar
        def _(act):
            def split(s, n, extra=0):
                act.wait_ge(ring.loaded[s], n * 16 + (16 + extra))
                act.wait_ge(ring.used[s], n + 1)
                act.copy(ring.hi[s][:, :, :], ring.raw[s][:, :, :]).then_inc(ring.hi_done[s], 1)

            for n in range(2):
                split(0, n)
                split(1, n)
            split(0, 2)
            split(1, 2, 5 * 16)
            with act.Fori(3, NZ // 2) as i:
                split(0, i)
                split(1, i, 5 * 16)

        @block.gpsimd
        def _(pool):
            ring.open(pool, ring.lo_done)
            with pool.Fori(0, NZ // 2) as i:
                for s in range(2):
                    ring.split_lo(nc, pool, s, i)

        @block.tensor
        def _(pe):
            ring.open(pe, ring.used)
            with pe.Fori(0, NZ // 2) as i:
                for s in range(2):
                    pe.wait_ge(ring.evacuated[s], i + 1)
                    ring.products(pe, s, i, banks[:, 3 * s:3 * s + 3, :],
                                  lambda k: g.h_hi[:, k, :], lambda k: g.h_lo[:, k, :])

        @block.vector
        def _(v):
            ring.open(v, ring.evacuated)
            with v.Fori(0, NZ // 2) as i:
                for s in range(2):
                    v.wait_ge(ring.used[s], i + 2)
                    nc.vector.tensor_copy(
                        zT[:, ds(i * 2 + s, 1), :].rearrange("p o (b t) -> p (o b) t", b=NBLK),
                        banks[:, 3 * s:3 * s + 3, 0:TB]).then_inc(ring.evacuated[s], 1)


def norms_and_conv(g):
    nc, A, sem, zT, banks, ident = g.nc, g.A, g.sem, g.zT, g.banks, g.ident
    keep = Arena(nc, g.h_at, g.top)
    g.cq_hi, g.cq_lo = keep.take("cq_hi", [P, KQ, TT], F32R), keep.take("cq_lo", [P, KQ, TT], F32R)
    g.lat_hi, g.lat_lo = keep.take("lat_hi", [P, KL, TT], F32R), keep.take("lat_lo", [P, KL, TT], F32R)
    g.lora_end = keep.at
    g.kpe = keep.take("key_rope", [P, TT], F32)
    g.new_latT = keep.take("new_latT", [P, KL, NS], F32)
    g.new_page = keep.take("new_page", [NS, KVL + ROPE], F32)
    g.qs = keep.take("q_sampled", [P, H, NS], F32)
    g.gg = keep.take("qk_gain", [P, 1], F32)
    g.p4_at = keep.at
    lat = keep.take("lat", [P, KL, TT], F32)
    rows = [keep.take(f"new_rows{i}", [P, KVL + ROPE], F32) for i in range(2)]
    ar = Arena(nc, g.z_end, g.h_at)
    scr = norm_scratch("lora_norms", ar)
    us = keep.take("u_sampled", [P, KC, NSEQ, SDEC + 2], F32)
    ends = keep.take("conv_ends", [P, KC, 2 * NSEQ + 2], F32)
    state = keep.take("state_rows", [2 * NSEQ, CW], F32)
    crows = keep.take("conv_rows", [2 * NSEQ + 2, CW], F32)

    kv = Norm(nc, sem, "kvnorm", scr, lambda c: zT[:, Z_CKV + c, :], KL, KVL,
              lambda c: g.gcol[:, G_KVL + c:G_KVL + c + 1], lambda c: g.lat_hi[:, c, :], lambda c: g.lat_lo[:, c, :],
              banks[:, 0:3, :], g.ones, full=lambda c: lat[:, c, :])
    cq = Norm(nc, sem, "cqnorm", scr, lambda c: zT[:, Z_CQ + c, :], KQ, QL,
              lambda c: g.gcol[:, G_QL + c:G_QL + c + 1], lambda c: g.cq_hi[:, c, :], lambda c: g.cq_lo[:, c, :],
              banks[:, 3:6, :], g.ones)
    state_loaded, state_transposed, state_copied = sem("state_loaded"), sem("state_transposed"), sem("state_copied")
    rope_cos, rope_sin, rope_done = sem("rope_cos"), sem("rope_sin"), sem("rope_done")
    gated, u_sampled, ends_done = sem("gated"), sem("u_sampled"), sem("ends_done")
    taps, conv_done = sem("taps"), sem("conv_done")
    ends_transposed, conv_rows_done = sem("ends_transposed"), sem("conv_rows_done")
    tile_transposed, tile_copied = sem("tile_transposed"), sem("tile_copied")
    new_copied, latT_copied = sem("new_page_copied"), sem("new_latT_copied")
    stored = [sem(f"tile_stored{i}") for i in range(2)]
    sb = banks[:, 6, :]
    tiles = [(t * P, min(P, TP - t * P)) for t in range(NT)] + [(TP, NS)]
    tsb = TT - 2
    cwc = lambda j, c: g.gcol[:, G_CW + KC * j + c:G_CW + KC * j + c + 1]
    scratch = zT[:, Z_KPE, :]

    with nc.Block() as block:
        @block.sync
        def _(sp):
            sp.dma_start(state[:, :], A["state_conv"]).then_inc(state_loaded, 16)
            for t, (at, n) in enumerate(tiles):
                src = rows[t % 2] if t < NT else g.new_page
                sp.wait_ge(tile_copied, t + 1)
                out, o = ("prompt", at) if t < NT else ("sample", 0)
                done = stored[t % 2]
                sp.dma_start(A[f"out_new_lat_{out}"][o:o + n, :], src[0:n, 0:KVL]).then_inc(done, 16)
                sp.dma_start(A[f"out_new_kpe_{out}"][o:o + n, :], src[0:n, KVL:KVL + ROPE]).then_inc(done, 16)
            sp.wait_ge(conv_rows_done, 1)
            sp.dma_start(A["out_new_conv_sample"].rearrange("b j c -> (b j) c"), crows[0:2 * NSEQ, :]).then_inc(g.done, 16)
            sp.dma_start(A["out_new_conv_prompt"], crows[2 * NSEQ:2 * NSEQ + 2, :]).then_inc(g.done, 16)
            sp.wait_ge(stored[0], 32 * ((NT + 2) // 2))
            sp.wait_ge(stored[1], 32 * ((NT + 1) // 2))
            sp.wait_ge(g.done, 32)

        @block.scalar
        def _(act):
            kv.act(act)
            cq.act(act)
            for t, (at, n) in enumerate(tiles):
                dst = rows[t % 2] if t < NT else g.new_page
                act.wait_ge(tile_transposed, t + 1)
                if t >= 2:
                    act.wait_ge(stored[t % 2], 32 * (t // 2))
                act.copy(dst[0:n, :], banks[0:n, t % 2, 0:KVL + ROPE]).then_inc(tile_copied, 1)
            act.wait_ge(ends_transposed, 1)
            act.copy(crows[:, :], banks[0:2 * NSEQ + 2, 7, :]).then_inc(conv_rows_done, 1)

        @block.gpsimd
        def _(pool):
            for c in range(KC):
                nc.gpsimd.tensor_mul(zT[:, Z_GC + c, :], zT[:, Z_GC + c, :], zT[:, Z_HC + c, :]).then_inc(gated, 1)
            kv.pool(pool)
            cq.pool(pool)

        @block.vector
        def _(v):
            nc.vector.tensor_mul(g.kpe[NOPE:QK, :], zT[NOPE:QK, Z_KPE, :], g.cs[NOPE:QK, :]).then_inc(rope_cos, 1)
            v.wait_ge(rope_cos, 1)
            nc.vector.tensor_mul(scratch[NOPE:QK, :], zT[QK:P, Z_KPE, :], g.cs[QK:P, :]).then_inc(rope_sin, 1)
            v.wait_ge(rope_sin, 1)
            nc.vector.tensor_add(g.kpe[NOPE:QK, :], g.kpe[NOPE:QK, :], scratch[NOPE:QK, :]).then_inc(rope_done, 1)
            kv.dve(v)
            v.wait_ge(kv.norm, KL)
            nc.vector.tensor_copy(g.new_latT[:, :, :], lat[:, :, TP:T]).then_inc(latT_copied, 1)
            cq.dve(v)
            v.wait_ge(gated, KC)
            v.wait_ge(state_transposed, 1)
            nc.vector.tensor_copy(us[:, :, :, 2:], zT[:, Z_GC:Z_GC + KC, TP:T].rearrange("p c (b s) -> p c b s", b=NSEQ))\
                .then_inc(u_sampled, 1)
            nc.vector.tensor_copy(us[:, :, :, 0:2], banks[:, 6, 0:KC * 2 * NSEQ]
                                  .rearrange("p (c b j) -> p c b j", c=KC, j=2)).then_inc(u_sampled, 1)
            v.wait_ge(u_sampled, 2)
            nc.vector.tensor_copy(ends[:, :, 0:2 * NSEQ].rearrange("p c (b j) -> p c b j", j=2), us[:, :, :, SDEC:])\
                .then_inc(ends_done, 1)
            nc.vector.tensor_copy(ends[:, :, 2 * NSEQ:], zT[:, Z_GC:Z_GC + KC, TP - 2:TP]).then_inc(ends_done, 1)
            n = 0
            for c in range(KC):
                y, u = zT[:, Z_HC + c, :], zT[:, Z_GC + c, :]
                yp, ys = y[:, 0:TP], y[:, TP:T].rearrange("p (b s) -> p b s", b=NSEQ)
                b = g.gcol[:, G_CB + c:G_CB + c + 1]
                nc.vector.tensor_scalar(y[:, 0:TP], u[:, 0:TP], cwc(2, c), b, ALU.mult, ALU.add).then_inc(taps, 1)
                nc.vector.tensor_scalar(ys, us[:, c, :, 2:2 + SDEC], cwc(2, c), b, ALU.mult, ALU.add).then_inc(taps, 1)
                n += 2
                for j in (1, 0):
                    sh = 2 - j
                    v.wait_ge(taps, n)
                    nc.vector.scalar_tensor_tensor(yp[:, sh:], u[:, 0:TP - sh], cwc(j, c), yp[:, sh:],
                                                   ALU.mult, ALU.add).then_inc(taps, 1)
                    nc.vector.scalar_tensor_tensor(ys, us[:, c, :, j:j + SDEC], cwc(j, c), ys,
                                                   ALU.mult, ALU.add).then_inc(taps, 1)
                    n += 2
                v.wait_ge(taps, n)
                nc.vector.tensor_mul(zT[:, Z_GB + c, 0:T], zT[:, Z_GB + c, 0:T], y[:, 0:T]).then_inc(conv_done, 1)
            v.wait_ge(conv_done, KC)

        @block.tensor
        def _(pe):
            pe.wait_ge(state_loaded, 16)
            for c in range(KC):
                mm = pe.transpose(banks[:, 6, c * 2 * NSEQ:(c + 1) * 2 * NSEQ], state[:, c * P:(c + 1) * P],
                                  ident[0:2 * NSEQ, 0:2 * NSEQ])
            mm.then_inc(state_transposed, 1)
            kv.pe(pe)
            cq.pe(pe)
            pe.wait_ge(rope_done, 1)
            pe.wait_ge(kv.norm, KL)
            pe.wait_ge(kv.mean, 1)
            for t, (at, n) in enumerate(tiles):
                if t >= 2:
                    pe.wait_ge(tile_copied, t - 1)
                for c in range(KL):
                    pe.transpose(banks[0:n, t % 2, c * P:(c + 1) * P], lat[:, c, at:at + n], ident[:, :])
                pe.transpose(banks[0:n, t % 2, KVL:KVL + ROPE], g.kpe[NOPE:QK, at:at + n], ident[NOPE:QK, NOPE:QK])\
                    .then_inc(tile_transposed, 1)
            pe.wait_ge(ends_done, 2)
            for c in range(KC):
                mm = pe.transpose(banks[0:2 * NSEQ + 2, 7, c * P:(c + 1) * P], ends[:, c, :], ident[:, :])
            mm.then_inc(ends_transposed, 1)


def expand_heads(g):
    nc, A, sem, banks, ident = g.nc, g.A, g.sem, g.banks, g.ident
    ar, low, small = Arena(nc, g.z_hc_at, g.h_at), Arena(nc, g.z_at, g.conv_at), Arena(nc, g.cs_at, g.cs_end)
    g.q_tok, g.v_tok = ar.take("q_tokens", [P, NT, H * QK], F32), ar.take("v_tokens", [P, NT, AW], F32)
    g.heads_end = ar.at
    g.k_tok = Arena(nc, g.p4_at, g.top).take("k_tokens", [P, NT, H * NOPE], F32)
    g.kpe_tok, g.rq, g.rk = (small.take(n, [P, NT, c], F32) for n, c in (("kpe_tokens", ROPE), ("q_scale", H), ("k_scale", H)))
    turns = small.take("rope_rows", [P, NT, ROPE], F32)
    part = small.take("rope_part", [P, H, ROPE], F32)
    uq_hi = ar.take("w_uq_hi", [P, KQ, H * QK], F32R)
    sq = ar.take("q_squares", [P, H * QK], F32)
    at = low.at
    uq_raw, ukv_raw = low.take("w_uq_raw", [P, KQ, H * QK], F32), low.take("w_ukv_raw", [P, KL, 2 * AW], F32)
    again = Arena(nc, at, low.at)
    uq_lo, ukv_lo = again.take("w_uq_lo", [P, KQ, H * QK], F32R), again.take("w_ukv_lo", [P, KL, 2 * AW], F32R)
    ukv_hi = low.take("w_ukv_hi", [P, KL, 2 * AW], F32R)

    uq_loaded, ukv_loaded, turns_loaded = sem("w_uq_loaded"), sem("w_ukv_loaded"), sem("rope_rows_loaded")
    zeroed, w_hi_done, w_lo_done = sem("zeroed"), sem("w_hi_done"), sem("w_lo_done")
    kpe_transposed, kpe_copied = sem("kpe_transposed"), sem("kpe_copied")
    q_projected, kv_projected, q_copied, kv_copied = (sem(n) for n in ("q_projected", "kv_projected", "q_copied", "kv_copied"))
    rope_steps, q_squared, q_summed = sem("rope_steps"), sem("q_squared"), sem("q_summed")
    k_squared, k_summed, kpe_squared = sem("k_squared"), sem("k_summed"), sem("kpe_squared")
    norm_steps, rooted = sem("norm_steps"), sem("rooted")
    rows = lambda t: min(P, T - t * P)
    half = ROPE // 2
    heads = lambda ap: ap.rearrange("p (h c) -> p h c", h=H)
    qbanks = lambda t: banks[0:rows(t), 4 * (t % 2):4 * (t % 2) + 2, 0:H * QK // 2]
    kvbanks = lambda t: banks[0:rows(t), 4 * (t % 2) + 2:4 * (t % 2) + 4, :].rearrange("p b (h c) -> p (b h) c", c=P)

    with nc.Block() as block:
        @block.sync
        def _(sp):
            sp.dma_start(uq_raw[:, :, :], A["w_uq"].rearrange("(k p) n -> p k n", p=P)).then_inc(uq_loaded, 16)
            sp.dma_start(ukv_raw[:, :, :], A["w_ukv"].rearrange("(k p) n -> p k n", p=P)).then_inc(ukv_loaded, 16)
            whole = T // P
            sp.dma_start(turns[:, 0:whole, :], A["rope_rows"][0:whole * P, :].rearrange("(t p) c -> p t c", p=P))\
                .then_inc(turns_loaded, 16)
            sp.dma_start(turns[0:T - whole * P, whole, :], A["rope_rows"][whole * P:T, :]).then_inc(turns_loaded, 16)

        @block.gpsimd
        def _(pool):
            for t in (g.q_tok, g.k_tok, g.v_tok, g.kpe_tok, g.rq, g.rk):
                nc.gpsimd.memset(t[:, NT - 1, :], 0.0).then_inc(zeroed, 1)
            pool.wait_ge(turns_loaded, 32)
            for t in range(NT):
                n = rows(t)
                x = heads(g.q_tok[0:n, t, :])
                x1, x2 = x[:, :, NOPE:NOPE + half], x[:, :, NOPE + half:QK]
                p1, p2 = part[0:n, :, 0:half], part[0:n, :, half:ROPE]
                cos, sin = (turns[0:n, t, a:a + half].unsqueeze(1).broadcast_to([n, H, half]) for a in (0, half))
                pool.wait_ge(q_copied, t + 1)
                if t > 0:
                    pool.wait_ge(rope_steps, t * 6)
                nc.gpsimd.tensor_mul(p1, x2, sin).then_inc(rope_steps, 1)
                nc.gpsimd.tensor_mul(p2, x1, sin).then_inc(rope_steps, 1)
                nc.gpsimd.tensor_mul(x1, x1, cos).then_inc(rope_steps, 1)
                nc.gpsimd.tensor_mul(x2, x2, cos).then_inc(rope_steps, 1)
                pool.wait_ge(rope_steps, t * 6 + 4)
                nc.gpsimd.tensor_sub(x1, x1, p1).then_inc(rope_steps, 1)
                nc.gpsimd.tensor_add(x2, x2, p2).then_inc(rope_steps, 1)
            pool.wait_ge(kpe_copied, 2)
            pool.wait_ge(q_summed, NT)
            nc.gpsimd.tensor_mul(sq[:, 0:NT * ROPE], g.kpe_tok[:, :, :].rearrange("p t c -> p (t c)"),
                                 g.kpe_tok[:, :, :].rearrange("p t c -> p (t c)")).then_inc(kpe_squared, 1)

        @block.scalar
        def _(act):
            act.wait_ge(uq_loaded, 16)
            act.copy(uq_hi[:, :, :], uq_raw[:, :, :]).then_inc(w_hi_done, 1)
            act.wait_ge(ukv_loaded, 16)
            act.copy(ukv_hi[:, :, :], ukv_raw[:, :, :]).then_inc(w_hi_done, 1)
            act.wait_ge(kpe_transposed, 1)
            act.wait_ge(zeroed, 6)
            n = rows(NT - 1)
            act.copy(g.kpe_tok[:, 0:NT - 1, :].rearrange("p t c -> p (t c)"), banks[:, 7, 0:(NT - 1) * ROPE]).then_inc(kpe_copied, 1)
            act.copy(g.kpe_tok[0:n, NT - 1, :], banks[0:n, 7, (NT - 1) * ROPE:NT * ROPE]).then_inc(kpe_copied, 1)

            def square_q(t):
                act.wait_ge(rope_steps, t * 6 + 6)
                if t > 0:
                    act.wait_ge(q_summed, t)
                act.activation(sq[0:rows(t), :], g.q_tok[0:rows(t), t, :], ACT.Square).then_inc(q_squared, 1)

            for t in range(NT):
                act.wait_ge(q_projected, t + 1)
                act.copy(g.q_tok[0:rows(t), t, :].rearrange("p (b c) -> p b c", b=2), qbanks(t)).then_inc(q_copied, 1)
                if t > 0:
                    square_q(t - 1)
                act.wait_ge(kv_copied, 2 * t + 2)
                act.activation(kvbanks(t)[:, :, 0:NOPE], kvbanks(t)[:, :, 0:NOPE], ACT.Square).then_inc(k_squared, 1)
            square_q(NT - 1)
            act.wait_ge(norm_steps, 4)
            act.activation(g.rq[:, :, :], g.rq[:, :, :], ACT.Sqrt).then_inc(rooted, 1)
            act.activation(g.rk[:, :, :], g.rk[:, :, :], ACT.Sqrt).then_inc(rooted, 1)

        @block.vector
        def _(v):
            for i, (lo, raw, hi) in enumerate(((uq_lo, uq_raw, uq_hi), (ukv_lo, ukv_raw, ukv_hi))):
                v.wait_ge(w_hi_done, i + 1)
                nc.vector.tensor_sub(lo[:, :, :], raw[:, :, :], hi[:, :, :].bitcast(F32)).then_inc(w_lo_done, 1)
            v.wait_ge(zeroed, 6)

            def sum_q(t):
                v.wait_ge(q_squared, t + 1)
                nc.vector.tensor_reduce(g.rq[0:rows(t), t, :], heads(sq[0:rows(t), :]), AX_X, ALU.add).then_inc(q_summed, 1)

            for t in range(NT):
                v.wait_ge(kv_projected, t + 1)
                nc.vector.tensor_copy(heads(g.k_tok[0:rows(t), t, :]), kvbanks(t)[:, :, 0:NOPE]).then_inc(kv_copied, 1)
                nc.vector.tensor_copy(heads(g.v_tok[0:rows(t), t, :]), kvbanks(t)[:, :, NOPE:P]).then_inc(kv_copied, 1)
                if t > 0:
                    sum_q(t - 1)
                v.wait_ge(k_squared, t + 1)
                nc.vector.tensor_reduce(g.rk[0:rows(t), t, :], kvbanks(t)[:, :, 0:NOPE], AX_X, ALU.add).then_inc(k_summed, 1)
            sum_q(NT - 1)
            v.wait_ge(kpe_squared, 1)
            kpe_sum = part[:, 0, 0:NT]
            v.wait_ge(rope_steps, NT * 6)
            nc.vector.tensor_reduce(kpe_sum, sq[:, 0:NT * ROPE].rearrange("p (t c) -> p t c", c=ROPE), AX_X, ALU.add)\
                .then_inc(norm_steps, 1)
            v.wait_ge(q_summed, NT)
            nc.vector.tensor_scalar(g.rq[:, :, :], g.rq[:, :, :], 1.0 / QK, EPS, ALU.mult, ALU.add).then_inc(norm_steps, 1)
            v.wait_ge(norm_steps, 1)
            v.wait_ge(k_summed, NT)
            nc.vector.tensor_add(g.rk[:, :, :], g.rk[:, :, :], kpe_sum.unsqueeze(2).broadcast_to([P, NT, H])).then_inc(norm_steps, 1)
            v.wait_ge(norm_steps, 3)
            nc.vector.tensor_scalar(g.rk[:, :, :], g.rk[:, :, :], 1.0 / QK, EPS, ALU.mult, ALU.add).then_inc(norm_steps, 1)
            v.wait_ge(rooted, 2)
            nc.vector.reciprocal(g.rq[:, :, :], g.rq[:, :, :]).then_inc(norm_steps, 1)
            nc.vector.reciprocal(g.rk[:, :, :], g.rk[:, :, :]).then_inc(norm_steps, 1)
            v.wait_ge(norm_steps, 6)

        @block.tensor
        def _(pe):
            for t in range(NT):
                mm = pe.transpose(banks[0:rows(t), 7, t * ROPE:(t + 1) * ROPE], g.kpe[NOPE:QK, t * P:t * P + rows(t)],
                                  ident[NOPE:QK, NOPE:QK])
            mm.then_inc(kpe_transposed, 1)
            for t in range(NT):
                cols = slice(t * P, t * P + rows(t))
                for K, xhi, xlo, whi, wlo, bank, width, ready, free, done in (
                        (KQ, g.cq_hi, g.cq_lo, uq_hi, uq_lo, 0, H * QK // 2, 1, q_copied, q_projected),
                        (KL, g.lat_hi, g.lat_lo, ukv_hi, ukv_lo, 2, AW, 2, k_summed, kv_projected)):
                    pe.wait_ge(w_lo_done, ready)
                    if t >= 2:
                        pe.wait_ge(free, t - 1)
                    if t == 1:
                        pe.wait_ge(kpe_copied, 2)
                    for k in range(K):
                        for x, w, a in ((xhi, whi, 0), (xhi, wlo, 1), (xlo, whi, 2)):
                            for b in range(2):
                                mm = pe.matmul(banks[0:rows(t), 4 * (t % 2) + bank + b, 0:width], x[:, k, cols],
                                               w[:, k, b * width:(b + 1) * width], start=k == 0 and a == 0,
                                               stop=k == K - 1 and a == 2)
                    mm.then_inc(done, 1)


def prompt_attention(g):
    nc, A, sem, banks, ident = g.nc, g.A, g.sem, g.banks, g.ident
    low, ar, lora = Arena(nc, g.z_at, g.conv_at), Arena(nc, g.heads_end, g.h_at), Arena(nc, g.h_at, g.lora_end)
    g.attnT = low.take("attnT", [P, AW // P, TT], F32)
    pt = [low.take(f"probsT{i}", [P, 4, P], F32) for i in range(2)]
    mask, ident_half = low.take("causal_mask", [P, P], BF16), low.take("ident_bf16", [P, P], BF16)
    qh, kh = low.take("q_head", [P, NT, QK], F32), ar.take("k_head", [P, NT, QK], F32)
    mx, nb, rs, ri = (low.take(n, [P, NT], F32) for n in ("row_max", "neg_max", "row_sum", "row_inv"))
    probs = [ar.take(f"probs{i}", [P, TQ], F32) for i in range(2)]
    vh = [a.take(f"v_head{i}", [P, NT, VH], F32) for i, a in enumerate((ar, lora))]
    q_hi, q_lo, k_hi, k_lo = ([lora.take(f"{n}{i}", [P, TQ], F32R) for i in range(2)] for n in ("q_hi", "q_lo", "k_hi", "k_lo"))

    LEAD = 4
    s = {n: sem(n) for n in (
        "ready gain_done q_head_ready k_head_ready v_head_ready unit_transposed unit_hi_done unit_lo_done scored "
        "maxed biased exped inverted normed p_transposed p_copied pv_done out_copied").split()}

    UNITS = [[(True, 0, 4, 0)], [(True, 4, 4, 0)], [(False, 0, 4, 0)], [(False, 4, 4, 0)], [(True, 8, 1, 0), (False, 8, 1, 1)]]
    NU = len(UNITS)
    SCORE_BANK = (0, 1, 2, 0, 3, 0, 3, 0, 2)
    SCORE_FREE = (-1, -1, 0, 1, 0, 4, 5, 6, 7)

    def chunks(t):
        return [(j, min(4, t + 1 - j)) for j in range(0, t + 1, 4)]

    NCH = sum(len(chunks(t)) for t in range(NT))

    def before(t):
        return sum(len(chunks(x)) for x in range(t)) - sum(len(chunks(NT + x)) for x in range(t, 0))

    def score_shape(t):
        pieces = -(-(t + 1) * P // BANK)
        return pieces, (t + 1) * P // pieces

    def scores(t):
        pieces, n = score_shape(t)
        return banks[:, SCORE_BANK[t]:SCORE_BANK[t] + pieces, 0:n]

    def heads(engine, head):
        head(0, 0, True, False)
        with engine.Fori(0, (H - 2) // 2) as i:
            head(i * 2 + 1, 1, False, False)
            head(i * 2 + 2, 0, False, False)
        head(H - 1, 1, False, True)

    with nc.Block() as block:
        @block.gpsimd
        def _(pool):
            nc.gpsimd.memset(mask[:, :], 0.0).then_inc(s["ready"], 1)
            pool.wait_ge(s["ready"], 1)
            nc.gpsimd.affine_select(out=mask[:, :], in_=mask[:, :], compare_op=ALU.is_ge, fill=MASKED, base=0,
                                    pattern=[[-1, P]], channel_multiplier=1).then_inc(s["ready"], 1)
            nc.gpsimd.tensor_copy(ident_half[:, :], ident[:, :]).then_inc(s["ready"], 1)

            def prepare(n, par):
                scale = lambda r, c: r[:, :, ds(n, 1)].broadcast_to([P, NT, c])
                pool.wait_ge(s["unit_transposed"], LEAD + n * NU)
                nc.gpsimd.tensor_mul(qh[:, :, :], g.q_tok[:, :, ds(n * QK, QK)], scale(g.rq, QK)).then_inc(s["q_head_ready"], 1)
                nc.gpsimd.tensor_mul(kh[:, :, 0:NOPE], g.k_tok[:, :, ds(n * NOPE, NOPE)], scale(g.rk, NOPE))\
                    .then_inc(s["k_head_ready"], 1)
                nc.gpsimd.tensor_mul(kh[:, :, NOPE:QK], g.kpe_tok[:, :, :], scale(g.rk, ROPE)).then_inc(s["k_head_ready"], 1)
                if not isinstance(n, int) or n > 1:
                    pool.wait_ge(s["pv_done"], LEAD + n * NCH - NCH)
                nc.gpsimd.tensor_copy(vh[par][:, :, :], g.v_tok[:, :, ds(n * VH, VH)]).then_inc(s["v_head_ready"], 1)

            def head(n, par, first, last):
                if first:
                    prepare(0, 0)
                if not last:
                    prepare(n + 1, 1 - par)

            heads(pool, head)

        @block.scalar
        def _(act):
            act.sem_inc(s["exped"], LEAD)
            act.sem_inc(s["p_copied"], LEAD)
            act.wait_ge(s["gain_done"], 1)

            def split_hi(n, par, u):
                act.wait_ge(s["unit_transposed"], LEAD + n * NU + (u + 1))
                for queries, t, m, place in UNITS[u]:
                    src = banks[0:QK, 5, place * P:(place + m) * P]
                    if queries:
                        act.activation(q_hi[par][0:QK, t * P:(t + m) * P], src, ACT.Copy, scale=g.gg[0:QK, :])\
                            .then_inc(s["unit_hi_done"], 1)
                    else:
                        act.copy(k_hi[par][0:QK, t * P:(t + m) * P], src).then_inc(s["unit_hi_done"], 1)

            def probabilities(n, par, t):
                m = (t + 1) * P
                pieces, L = score_shape(t)
                act.wait_ge(s["biased"], n * NT + (t + 1))
                act.wait_ge(s["p_transposed"], LEAD + n * NCH + before(t - 1))
                act.activation(probs[(par + t) % 2][:, 0:m].rearrange("p (a b) -> p a b", a=pieces), scores(t), ACT.Exp,
                               bias=nb[:, t:t + 1], scale=SCALE, accum_out=rs[:, t:t + 1]).then_inc(s["exped"], 1)

            def head(n, par, first, last):
                if first:
                    for u in range(NU):
                        split_hi(0, 0, u)
                    probabilities(0, 0, 0)
                c = 0
                for t in range(NT):
                    if t + 1 < NT:
                        probabilities(n, par, t + 1)
                    elif not last:
                        probabilities(n + 1, 1 - par, 0)
                    if not last and 1 <= t <= NU:
                        split_hi(n + 1, 1 - par, t - 1)
                    for j, m in chunks(t):
                        act.wait_ge(s["p_transposed"], LEAD + n * NCH + (c + 1))
                        act.wait_ge(s["pv_done"], LEAD + n * NCH + (c - 1))
                        act.copy(pt[(par + c) % 2][:, 0:m, :], banks[:, 6, 0:m * P].rearrange("p (j q) -> p j q", q=P))\
                            .then_inc(s["p_copied"], 1)
                        c += 1

            heads(act, head)

        @block.vector
        def _(v):
            v.sem_inc(s["unit_lo_done"], LEAD)
            v.sem_inc(s["out_copied"], LEAD)
            nc.vector.tensor_mul(g.gg[:, :], g.gcol[:, G_QN:G_QN + 1], g.gcol[:, G_KN:G_KN + 1]).then_inc(s["gain_done"], 1)
            v.wait_ge(s["gain_done"], 1)

            def split_lo(n, par, u):
                last = u == NU - 1
                v.wait_ge(s["unit_hi_done"], n * (NU + 1) + (u + 1 + last))
                for queries, t, m, place in UNITS[u]:
                    src = banks[0:QK, 5, place * P:(place + m) * P]
                    cols = slice(t * P, (t + m) * P)
                    if queries:
                        done = nc.vector.scalar_tensor_tensor(q_lo[par][0:QK, cols], src, g.gg[0:QK, :],
                                                              q_hi[par][0:QK, cols].bitcast(F32), ALU.mult, ALU.subtract)
                    else:
                        done = nc.vector.tensor_sub(k_lo[par][0:QK, cols], src, k_hi[par][0:QK, cols].bitcast(F32))
                if last:
                    at = TP - (NT - 1) * P
                    nc.vector.tensor_scalar(g.qs[0:QK, ds(n, 1), :].rearrange("p o t -> p (o t)"), banks[0:QK, 5, at:at + NS],
                                            g.gg[0:QK, :], None, ALU.mult).then_inc(s["unit_lo_done"], 1)
                else:
                    done.then_inc(s["unit_lo_done"], 1)

            def maxima(n, par, t):
                v.wait_ge(s["scored"], n * NT + (t + 1))
                nc.vector.tensor_reduce(mx[:, t:t + 1], scores(t), mybir.AxisListType.XY, ALU.max).then_inc(s["maxed"], 1)
                v.wait_ge(s["maxed"], n * NT + (t + 1))
                nc.vector.tensor_scalar(nb[:, t:t + 1], mx[:, t:t + 1], -SCALE, None, ALU.mult).then_inc(s["biased"], 1)

            def keep_output(n, par, t):
                v.wait_ge(s["pv_done"], LEAD + n * NCH + before(t + 1))
                w = min(P, TP - t * P)
                nc.vector.tensor_copy(g.attnT[VH * par:VH * par + VH, ds(n // 2, 1), t * P:t * P + w]
                                      .rearrange("p o t -> p (o t)"), banks[0:VH, 7, 0:w]).then_inc(s["out_copied"], 1)

            def head(n, par, first, last):
                if first:
                    for u in range(NU):
                        split_lo(0, 0, u)
                    maxima(0, 0, 0)
                    maxima(0, 0, 1)
                for t in range(NT):
                    v.wait_ge(s["exped"], LEAD + n * NT + (t + 1))
                    nc.vector.reciprocal(ri[:, t:t + 1], rs[:, t:t + 1]).then_inc(s["inverted"], 1)
                    v.wait_ge(s["inverted"], n * NT + (t + 1))
                    pr = probs[(par + t) % 2][:, 0:(t + 1) * P]
                    nc.vector.tensor_scalar(pr, pr, ri[:, t:t + 1], None, ALU.mult).then_inc(s["normed"], 1)
                    if t + 2 < NT:
                        maxima(n, par, t + 2)
                    elif not last:
                        maxima(n + 1, 1 - par, t + 2 - NT)
                    if not last and 1 <= t <= NU:
                        split_lo(n + 1, 1 - par, t - 1)
                    if t >= 1:
                        keep_output(n, par, t - 1)
                    elif not first:
                        keep_output(n - 1, 1 - par, NT - 1)
                if last:
                    keep_output(n, par, NT - 1)

            heads(v, head)

        @block.tensor
        def _(pe):
            for name in ("unit_transposed", "p_transposed", "pv_done"):
                pe.sem_inc(s[name], LEAD)

            def transpose_unit(n, u):
                pe.wait_ge(s["unit_lo_done"], LEAD + n * NU + u)
                pe.wait_ge(s["q_head_ready"], n + 1)
                pe.wait_ge(s["k_head_ready"], n * 2 + 2)
                for queries, t, m, place in UNITS[u]:
                    for x in range(m):
                        mm = pe.transpose(banks[0:QK, 5, (place + x) * P:(place + x + 1) * P], (qh if queries else kh)[:, t + x, :],
                                          ident[:, :])
                mm.then_inc(s["unit_transposed"], 1)

            def score(n, par, t):
                pieces, L = score_shape(t)
                if t == 0:
                    pe.wait_ge(s["unit_lo_done"], LEAD + n * NU + NU)
                pe.wait_ge(s["exped"], LEAD + n * NT + SCORE_FREE[t])
                for b in range(pieces):
                    for q, k, a in ((q_hi, k_hi, 0), (q_hi, k_lo, 1), (q_lo, k_hi, 2)):
                        if b == pieces - 1 and a == 2:
                            pe.matmul(banks[:, SCORE_BANK[t] + b, L - P:L], ident_half[:, :], mask[:, :], start=False, stop=False)
                        mm = pe.matmul(banks[:, SCORE_BANK[t] + b, 0:L], q[par][0:QK, t * P:(t + 1) * P],
                                       k[par][0:QK, b * L:(b + 1) * L], start=a == 0, stop=a == 2)
                mm.then_inc(s["scored"], 1)

            def values(n, par, t, c, j, m):
                pe.wait_ge(s["p_copied"], LEAD + n * NCH + (c + 1))
                if j == 0:
                    pe.wait_ge(s["out_copied"], LEAD + n * NT + t)
                for x in range(m):
                    mm = pe.matmul(banks[0:VH, 7, 0:P], vh[par][:, j + x, :], pt[(par + c) % 2][:, x, :],
                                   start=j + x == 0, stop=j + x == t)
                mm.then_inc(s["pv_done"], 1)

            def head(n, par, first, last):
                if first:
                    pe.wait_ge(s["ready"], 3)
                    for u in range(NU):
                        transpose_unit(0, u)
                    score(0, 0, 0)
                    score(0, 0, 1)
                pe.wait_ge(s["v_head_ready"], n + 1)
                c, behind = 0, None
                for t in range(NT):
                    if t + 2 < NT:
                        score(n, par, t + 2)
                    elif not last:
                        score(n + 1, 1 - par, t + 2 - NT)
                    if not last and 1 <= t <= NU:
                        transpose_unit(n + 1, t - 1)
                    pe.wait_ge(s["normed"], n * NT + (t + 1))
                    for j, m in chunks(t):
                        pe.wait_ge(s["p_copied"], LEAD + n * NCH + c)
                        for x in range(m):
                            mm = pe.transpose(banks[:, 6, x * P:(x + 1) * P],
                                              probs[(par + t) % 2][:, (j + x) * P:(j + x + 1) * P], ident[:, :])
                        mm.then_inc(s["p_transposed"], 1)
                        if behind:
                            values(n, par, *behind)
                        behind = (t, c, j, m)
                        c += 1
                values(n, par, *behind)

            heads(pe, head)


def sample_attention(g):
    nc, A, sem, banks, ident = g.nc, g.A, g.sem, g.banks, g.ident
    G = 8
    SETS = 4
    AHEAD = 4
    GROUPS = NSEQ * NPAGES // G
    PER_SEQ = NPAGES // G
    HS = H * SDEC
    HC = H // 2
    WK = HC * NOPE
    WC = WK + HC * SDEC
    KW = NOPE + VH
    ar = Arena(nc, g.z_hc_at, g.h_at)
    comb_hi = [ar.take(f"comb_hi{i}", [P, KL, 2, WC], F32R) for i in range(2)]
    comb_lo = [ar.take(f"comb_lo{i}", [P, KL, 2, WC], F32R) for i in range(2)]
    lora = Arena(nc, g.h_at, g.lora_end)
    X = [a.take(f"page_latents{i}", [P, G, KVL + 2], F32) for i, a in enumerate((ar, ar, lora, lora))]
    R = [a.take(f"page_ropes{i}", [P, G * ROPE], F32) for i, a in enumerate((ar, ar, lora, lora))]
    xT_hi = [lora.take(f"pageT_hi{i}", [P, KL, P], F32R) for i in range(AHEAD)]
    xT_lo = [lora.take(f"pageT_lo{i}", [P, KL, P], F32R) for i in range(AHEAD)]
    sq = [ar.take(f"k_sq{i}", [P, H * NOPE], F32) for i in range(2)]
    ctxs = ar.take("context", [HS, NSEQ, KVL + 1], F32)
    tail = Arena(nc, g.p4_at, g.top)
    wkv = ar.take("w_ukv", [P, KL, H * KW], F32)
    qab = tail.take("q_latent", [P, NSEQ, KL, HS], F32)
    qab_hi, qab_lo = (tail.take(n, [P, NSEQ, KL, HS], F32R) for n in ("q_latent_hi", "q_latent_lo"))
    rT = tail.take("ropesT", [P, 2 * P], F32)
    rsq = tail.take("rope_sq", [P, G, ROPE], F32)
    qr4 = tail.take("q_rope4", [P, NSEQ, HS], F32)
    own = tail.take("own_block", [P, 4, HS], F32)
    qbd = [tail.take(f"q_rope_blocks{i}", [P, 4, HS], F32) for i in range(2)]
    sc = [tail.take(f"scores{i}", [P, G, HS], F32) for i in range(2)]
    st = tail.take("scaled_scores", [P, G, HS], F32)
    pr = tail.take("probabilities", [P, G, HS], F32)
    ksum = [tail.take(f"k_sums{i}", [P, G, H], F32) for i in range(2)]
    rk, rsum = tail.take("k_inv_root", [P, G * H], F32), tail.take("rope_sums", [P, G], F32)
    mx, diag = tail.take("maxima", [P, HS], F32), tail.take("max_diagonal", [HS, HS], F32)
    gmax, mnew, dmax, alpha = (tail.take(n, [HS, 1], F32) for n in ("group_max", "new_max", "max_fall", "alpha"))
    mrun = tail.take("running_max", [HS, NSEQ], F32)
    linv = tail.take("sum_inv", [HS, NSEQ], F32)
    pages = tail.take("page_table", [1, NSEQ * NPAGES], I32)
    mask0 = tail.take("new_mask", [NS, NSEQ, SDEC], F32)
    wukT = Arena(nc, g.z_at + -(-KC * TT * 4 // 32) * 32, g.conv_at).take("w_ukT", [P, H * KL, P], F32)

    names = ("w_loaded table_loaded constants memsets wT_done wT_copied qab_done "
             "qab_copied qab_split qab_lo_done comb_w_hi comb_w_lo kn0_done sq0_done k0_parts k0_mean k0_root k0_inv s0_done "
             "s0_steps s0_transposed m0_done s0_shifted p0_done l0_done p0_transposed p0_copied ctx0_done ctx0_copied "
             "x_transposed hi_done lo_done kn_done sq_done sc_copied summed r_transposed r_copied rp_done ropes_squared "
             "comb_ready qbd_ready s_added k_tot k_mean k_root k_inv s_steps maxed max_transposed max_steps diag_done "
             "alpha_done max_spread shifted exped ctx_done final_inv final_scaled ctxT_done ctxT_copied "
             "out_done out_copied qr_copied").split()
    s = {n: sem(n) for n in names}
    loaded = [sem(f"pages_loaded{i}") for i in range(SETS)]
    ropes_loaded = [sem(f"ropes_loaded{i}") for i in range(SETS)]
    s["pages_free"] = [sem(f"pages_free{i}") for i in range(SETS)]

    def ge(engine, semaphore, value):
        if not isinstance(value, int) or value > 0:
            engine.wait_ge(semaphore, value)

    nope = wkv[:, :, :].rearrange("p k (h c) -> p (k h) c", c=KW)
    lat_cache, rope_cache = A["cache_kv_latent"], A["cache_k_rope"]
    n_pool = lat_cache.shape[0]
    pageT = lambda j: banks[:, 4 + j % 2, 0:KVL]
    MT, MB, CT = 0, P, P + HS

    with nc.Block() as block:
        @block.sync
        def _(sp):
            sp.dma_start(pages[:, :], A["page_table"]).then_inc(s["table_loaded"], 16)
            sp.dma_start(wkv[:, :, :], A["w_ukv"].rearrange("(k p) n -> p k n", p=P)).then_inc(s["w_loaded"], 16)
            sp.wait_ge(s["table_loaded"], 16)
            with sp.Fori(0, GROUPS // SETS) as i:
                for q in range(SETS):
                    for j in range(G):
                        page = sp.value_load(pages[0:1, ds(i * (SETS * G) + (q * G + j), 1)], min_val=0,
                                             max_val=n_pool - 1)
                        if j == 0:
                            sp.wait_ge(s["pages_free"][q], i + 1)
                        sp.dma_start(X[q][:, j, 0:KVL], lat_cache[ds(page, 1), :, :].rearrange("o p n -> p (o n)"))\
                            .then_inc(loaded[q], 16)
                        sp.dma_start(R[q][:, j * ROPE:(j + 1) * ROPE],
                                     rope_cache[ds(page, 1), :, :].rearrange("o p n -> p (o n)")).then_inc(ropes_loaded[q], 16)

        def groups(engine, step, last):
            at = lambda n: (n, n % SETS, n // SETS)
            step(at(0), None, None)
            step(at(1), at(0), None)
            with engine.Fori(0, (GROUPS - SETS) // SETS) as i:
                inside = lambda c: (i * SETS + c, c % SETS, i + c // SETS)
                for c in range(2, 2 + SETS):
                    step(inside(c), inside(c - 1), inside(c - 2))
            step(at(GROUPS - 2), at(GROUPS - 3), at(GROUPS - 4))
            step(at(GROUPS - 1), at(GROUPS - 2), at(GROUPS - 3))
            last(at(GROUPS - 1), at(GROUPS - 2))

        def following(group, j):
            n, q, fill = group
            if j < G:
                return q, fill, j
            if isinstance(n, int) and n == GROUPS - 1:
                return None
            return (q + 1) % SETS, fill + (q + 1) // SETS, j - G

        @block.gpsimd
        def _(pool):
            nc.gpsimd.memset(mask0[:, :, :], 0.0).then_inc(s["memsets"], 1)
            nc.gpsimd.memset(own[:, :, :], 1.0).then_inc(s["memsets"], 1)
            for q in range(SETS):
                nc.gpsimd.memset(X[q][:, :, KVL:KVL + 1], 1.0).then_inc(s["memsets"], 1)
            nc.gpsimd.memset(g.attnT[:, :, T:TT], 0.0).then_inc(s["memsets"], 1)
            pool.wait_ge(s["memsets"], 3 + SETS)
            nc.gpsimd.affine_select(out=mask0[:, :, :], in_=mask0[:, :, :], compare_op=ALU.is_ge, fill=MASKED, base=0,
                                    pattern=[[-SDEC, NSEQ], [0, SDEC]], channel_multiplier=1).then_inc(s["constants"], 1)
            nc.gpsimd.affine_select(out=own[:, :, :], in_=own[:, :, :], compare_op=ALU.is_ge, fill=0.0, base=0,
                                    pattern=[[-ROPE, 4], [0, HS]], channel_multiplier=1).then_inc(s["constants"], 1)
            pool.wait_ge(s["constants"], 2)
            nc.gpsimd.affine_select(out=mask0[:, :, :], in_=mask0[:, :, :], compare_op=ALU.is_ge, fill=MASKED, base=0,
                                    pattern=[[SDEC, NSEQ], [1, SDEC]], channel_multiplier=-1).then_inc(s["constants"], 1)
            nc.gpsimd.affine_select(out=own[:, :, :], in_=own[:, :, :], compare_op=ALU.is_ge, fill=0.0, base=ROPE - 1,
                                    pattern=[[ROPE, 4], [0, HS]], channel_multiplier=-1).then_inc(s["constants"], 1)
            pool.wait_ge(s["constants"], 4)
            pool.wait_ge(s["qab_lo_done"], 1)
            pool.wait_ge(s["qr_copied"], 4)
            pool.wait_ge(s["comb_w_lo"], 2)

            def step(group, *_):
                n, q, fill = group
                b, par = n // PER_SEQ, q % 2
                ge(pool, s["kn_done"], n * G - G + 1)
                for t, src in ((comb_hi, qab_hi), (comb_lo, qab_lo)):
                    nc.gpsimd.tensor_copy(t[par][:, :, :, WK:WC],
                                          src[:, ds(b, 1), :, :].bitcast(F32).rearrange("p o k (a q) -> p (o k) a q", a=2))\
                        .then_inc(s["comb_ready"], 1)
                ge(pool, s["rp_done"], n)
                nc.gpsimd.tensor_mul(qbd[par][:, :, :], own[:, :, :],
                                     qr4[:, ds(b, 1), :].broadcast_to([P, 4, HS])).then_inc(s["qbd_ready"], 1)
                pool.wait_ge(ropes_loaded[q], fill * (16 * G) + 16 * G)
                ge(pool, s["k_tot"], n * 2)
                nc.gpsimd.tensor_mul(rsq[:, :, :].rearrange("p j r -> p (j r)"), R[q][:, :], R[q][:, :])\
                    .then_inc(s["ropes_squared"], 1)

            groups(pool, step, lambda *_: None)

        @block.scalar
        def _(act):
            act.wait_ge(s["wT_done"], 1)
            act.copy(wukT[0:NOPE, :, :].rearrange("p (a b) c -> p a (b c)", a=4), banks[0:NOPE, 2:6, :])\
                .then_inc(s["wT_copied"], 1)
            for p in range(2):
                act.copy(comb_hi[p][:, :, :, 0:WK].rearrange("p k a (h c) -> p (k a) h c", c=NOPE),
                         nope[:, :, 0:NOPE].rearrange("p (a h) c -> p a h c", h=HC)).then_inc(s["comb_w_hi"], 1)
            act.wait_ge(s["kn0_done"], 1)
            act.activation(sq[0][0:NS, :], banks[0:NS, 1, :], ACT.Square).then_inc(s["sq0_done"], 1)
            act.wait_ge(s["qab_copied"], KL)
            act.copy(qab_hi[:, :, :, :], qab[:, :, :, :]).then_inc(s["qab_split"], 1)
            for quad in range(4):
                act.copy(qr4[quad * ROPE:(quad + 1) * ROPE, :, :].rearrange("p b (h s) -> p b h s", h=H),
                         g.qs[NOPE:QK, :, :].rearrange("p h (b s) -> p b h s", s=SDEC)).then_inc(s["qr_copied"], 1)
            act.wait_ge(s["k0_mean"], 1)
            act.activation(rk[0:NS, 0:H], rk[0:NS, 0:H], ACT.Sqrt).then_inc(s["k0_root"], 1)
            act.wait_ge(s["s0_shifted"], 1)
            act.activation(sc[0][0:HS, :, :], sc[0][0:HS, :, :], ACT.Exp, scale=SCALE).then_inc(s["p0_done"], 1)
            act.wait_ge(s["p0_transposed"], 1)
            act.copy(pr[0:NS, :, :].rearrange("p a b -> p (a b)"), banks[0:NS, 7, 0:NSEQ * HS]).then_inc(s["p0_copied"], 1)
            act.wait_ge(s["ctx0_done"], 1)
            act.copy(ctxs[:, :, 0:KVL].rearrange("p (a b) c -> p a b c", a=4),
                     banks[0:HS, 2:6, :].rearrange("p a (b c) -> p a b c", b=2)).then_inc(s["ctx0_copied"], 1)

            def sqrt_step(n):
                act.wait_ge(s["k_mean"], n + 1)
                act.activation(rk[:, :], rk[:, :], ACT.Sqrt).then_inc(s["k_root"], 1)

            def alpha_step(n):
                act.wait_ge(s["max_steps"], n * 3 + 3)
                act.activation(alpha[:, :], dmax[:, :], ACT.Exp, scale=SCALE).then_inc(s["alpha_done"], 1)

            def exp_step(n):
                act.wait_ge(s["shifted"], n + 1)
                act.activation(pr[:, :, :], st[:, :, :], ACT.Exp, scale=SCALE).then_inc(s["exped"], 1)

            def step(group, soft, _):
                n, q, fill = group
                base, par = n * G, q % 2

                def hi(j):
                    if following(group, j):
                        act.wait_ge(s["x_transposed"], base + (j + 1))
                        ge(act, s["kn_done"], base + (j - AHEAD + 1 + 1))
                        act.copy(xT_hi[j % AHEAD][:, :, :].rearrange("p k t -> p (k t)"), pageT(j)).then_inc(s["hi_done"], 1)

                if soft is None:
                    hi(0)
                    hi(1)
                for j in range(G):
                    hi(j + 2)
                    if soft is not None:
                        if j == 2:
                            sqrt_step(soft[0])
                        if j == 6:
                            alpha_step(soft[0])
                        if j == 7:
                            exp_step(soft[0])
                    act.wait_ge(s["kn_done"], base + (j + 1 + 1))
                    ge(act, s["summed"], base + (j - 1))
                    kn = banks[:, 2 * (j % 2):2 * (j % 2) + 2, :]
                    act.activation(sq[j % 2][:, :].rearrange("p (a c) -> p a c", a=2), kn[:, :, 0:WK], ACT.Square)\
                        .then_inc(s["sq_done"], 1)
                    if j == 0:
                        ge(act, s["s_added"], n)
                    act.copy(sc[par][:, j, :].rearrange("p (a q) -> p a q", a=2), kn[:, :, WK:WC]).then_inc(s["sc_copied"], 1)
                    if j == 3:
                        act.wait_ge(s["r_transposed"], n + 1)
                        ge(act, s["rp_done"], n + 1)
                        act.copy(rT[:, :], banks[:, 6, 0:2 * P]).then_inc(s["r_copied"], 1)

            def last(soft, _):
                sqrt_step(soft[0])
                alpha_step(soft[0])
                exp_step(soft[0])

            groups(act, step, last)
            act.wait_ge(s["ctxT_done"], 1)
            act.copy(wukT[:, 0:2 * NSEQ * HS // P, :].rearrange("p a b -> p (a b)"), banks[:, 0, :]).then_inc(s["ctxT_copied"], 1)

        @block.vector
        def _(v):
            for opening in (s["s_added"], s["k_tot"], s["ctx_done"]):
                v.sem_inc(opening, 1)
            f8 = lambda t, n: t[0:n, :, :].rearrange("p a b -> p (a b)")
            v.wait_ge(s["qab_done"], 1)
            for k in range(KL):
                nc.vector.tensor_copy(qab[:, :, k, :].rearrange("p b (h s) -> p b h s", h=H),
                                      banks[:, 0, k * H * NS:(k + 1) * H * NS].rearrange("p (h b s) -> p b h s", b=NSEQ, s=SDEC))\
                    .then_inc(s["qab_copied"], 1)
            v.wait_ge(s["qab_copied"], KL)
            v.wait_ge(s["qab_split"], 1)
            nc.vector.tensor_sub(qab_lo[:, :, :, :].rearrange("p b k q -> p (b k q)"), qab[:, :, :, :].rearrange("p b k q -> p (b k q)"),
                                 qab_hi[:, :, :, :].bitcast(F32).rearrange("p b k q -> p (b k q)")).then_inc(s["qab_lo_done"], 1)
            for p in range(2):
                v.wait_ge(s["comb_w_hi"], p + 1)
                nc.vector.tensor_sub(comb_lo[p][:, :, :, 0:WK].rearrange("p k a (h c) -> p (k a) h c", c=NOPE),
                                     nope[:, :, 0:NOPE].rearrange("p (a h) c -> p a h c", h=HC),
                                     comb_hi[p][:, :, :, 0:WK].bitcast(F32).rearrange("p k a (h c) -> p (k a) h c", c=NOPE))\
                    .then_inc(s["comb_w_lo"], 1)
            v.wait_ge(s["sq0_done"], 1)
            nc.vector.tensor_reduce(ksum[0][0:NS, 0, :], sq[0][0:NS, :].rearrange("p (h c) -> p h c", h=H), AX_X, ALU.add)\
                .then_inc(s["k0_parts"], 1)
            rope = g.new_page[:, KVL:KVL + ROPE]
            nc.vector.tensor_mul(diag[:, :], rope, rope).then_inc(s["k0_parts"], 1)
            v.wait_ge(s["k0_parts"], 2)
            nc.vector.reduce_sum(rsum[0:NS, 0:1], diag[:, :], AX_X).then_inc(s["k0_parts"], 1)
            v.wait_ge(s["k0_parts"], 3)
            nc.vector.tensor_scalar(rk[0:NS, 0:H], ksum[0][0:NS, 0, :], rsum[0:NS, 0:1], 1.0 / QK, ALU.add, ALU.mult)\
                .then_inc(s["k0_parts"], 1)
            v.wait_ge(s["k0_parts"], 4)
            nc.vector.tensor_scalar(rk[0:NS, 0:H], rk[0:NS, 0:H], EPS, None, ALU.add).then_inc(s["k0_mean"], 1)
            v.wait_ge(s["k0_root"], 1)
            nc.vector.reciprocal(rk[0:NS, 0:H], rk[0:NS, 0:H]).then_inc(s["k0_inv"], 1)
            v.wait_ge(s["s0_done"], 1)
            s0 = f8(st, NS)
            s04 = st[0:NS, :, :].rearrange("p b (h s) -> p b h s", h=H)
            nc.vector.tensor_copy(s0, banks[0:NS, 6, 0:NSEQ * HS]).then_inc(s["s0_steps"], 1)
            v.wait_ge(s["s0_steps"], 1)
            nc.vector.tensor_add(s0, s0, banks[0:NS, 7, 0:NSEQ * HS]).then_inc(s["s0_steps"], 1)
            v.wait_ge(s["s0_steps"], 2)
            v.wait_ge(s["k0_inv"], 1)
            nc.vector.tensor_mul(s04, s04, rk[0:NS, 0:H].unsqueeze(1).unsqueeze(3).broadcast_to([NS, NSEQ, H, SDEC]))\
                .then_inc(s["s0_steps"], 1)
            v.wait_ge(s["s0_steps"], 3)
            v.wait_ge(s["constants"], 4)
            nc.vector.tensor_add(s04, s04, mask0[:, :, :].unsqueeze(2).broadcast_to([NS, NSEQ, H, SDEC])).then_inc(s["s0_steps"], 1)
            v.wait_ge(s["s0_transposed"], 1)
            s0T = banks[0:HS, 6, 0:NSEQ * NS].rearrange("p (b t) -> p b t", b=NSEQ)
            nc.vector.tensor_reduce(mrun[:, :], s0T, AX_X, ALU.max).then_inc(s["m0_done"], 1)
            v.wait_ge(s["m0_done"], 1)
            nc.vector.tensor_sub(sc[0][0:HS, :, :], s0T, mrun[:, :].unsqueeze(2).broadcast_to([HS, NSEQ, NS])).then_inc(s["s0_shifted"], 1)
            v.wait_ge(s["p0_done"], 1)
            nc.vector.tensor_reduce(ctxs[:, :, KVL:KVL + 1].rearrange("p b o -> p (b o)"), sc[0][0:HS, :, :], AX_X, ALU.add)\
                .then_inc(s["l0_done"], 1)
            v.wait_ge(s["l0_done"], 1)
            v.wait_ge(s["ctx0_copied"], 1)

            def soft_mean(n, par):
                v.wait_ge(s["ropes_squared"], n + 1)
                nc.vector.tensor_reduce(rsum[:, :], rsq[:, :, :], AX_X, ALU.add).then_inc(s["k_tot"], 1)
                v.wait_ge(s["k_tot"], n * 2 + 2)
                v.wait_ge(s["summed"], n * G + G)
                nc.vector.tensor_add(rk[:, :].rearrange("p (j h) -> p j h", h=H), ksum[par][:, :, :],
                                     rsum[:, :].unsqueeze(2).broadcast_to([P, G, H])).then_inc(s["k_tot"], 1)
                v.wait_ge(s["k_tot"], n * 2 + 3)
                nc.vector.tensor_scalar(rk[:, :], rk[:, :], 1.0 / QK, EPS, ALU.mult, ALU.add).then_inc(s["k_mean"], 1)
                v.wait_ge(s["rp_done"], n + 2)
                v.wait_ge(s["sc_copied"], n * G + G)
                nc.vector.tensor_add(f8(st, P), f8(sc[par], P), banks[:, 6, 2 * P:4 * P]).then_inc(s["s_added"], 1)

            def soft_scores(n):
                v.wait_ge(s["k_root"], n + 1)
                nc.vector.reciprocal(rk[:, :], rk[:, :]).then_inc(s["k_inv"], 1)
                v.wait_ge(s["k_inv"], n + 1)
                v.wait_ge(s["s_added"], n + 2)
                sv = f8(st, P).rearrange("p (a s) -> p a s", s=SDEC)
                nc.vector.tensor_mul(sv, sv, rk[:, :].unsqueeze(2).broadcast_to([P, G * H, SDEC])).then_inc(s["s_steps"], 1)

            def soft_maxima(n):
                v.wait_ge(s["s_steps"], n + 1)
                nc.vector.tensor_reduce(mx[:, :], st[:, :, :].rearrange("p j q -> p q j"), AX_X, ALU.max).then_inc(s["maxed"], 1)

            def soft_max(n, b):
                v.wait_ge(s["max_transposed"], n + 1)
                nc.vector.reduce_max(gmax[:, :], banks[0:HS, 7, MT:MT + P], AX_X).then_inc(s["max_steps"], 1)
                v.wait_ge(s["max_steps"], n * 3 + 1)
                nc.vector.tensor_max(mnew[:, :], gmax[:, :], mrun[:, ds(b, 1)]).then_inc(s["max_steps"], 1)
                v.wait_ge(s["max_steps"], n * 3 + 2)
                nc.vector.tensor_scalar(diag[:, :], ident[0:HS, 0:HS], mnew[:, :], None, ALU.mult).then_inc(s["diag_done"], 1)
                nc.vector.tensor_sub(dmax[:, :], mrun[:, ds(b, 1)], mnew[:, :]).then_inc(s["max_steps"], 1)
                v.wait_ge(s["max_steps"], n * 3 + 3)
                nc.vector.tensor_scalar(mrun[:, ds(b, 1)], mnew[:, :], 1.0, None, ALU.mult).then_inc(s["m0_done"], 1)

            def soft_shift(n):
                v.wait_ge(s["max_spread"], n + 1)
                nc.vector.tensor_sub(st[:, :, :], st[:, :, :], banks[:, 7, MB:MB + HS].unsqueeze(1).broadcast_to([P, G, HS]))\
                    .then_inc(s["shifted"], 1)

            def soft_context(group):
                n, q, fill = group
                b = n // PER_SEQ
                v.wait_ge(s["pages_free"][q], fill + 2)
                v.wait_ge(s["alpha_done"], n + 1)
                v.wait_ge(s["m0_done"], n + 2)
                ge(v, s["ctx_done"], n + 1)
                c = ctxs[:, ds(b, 1), :].rearrange("p o c -> p (o c)")
                nc.vector.scalar_tensor_tensor(c, c, alpha[:, :], banks[0:HS, 7, CT:CT + KVL + 1], ALU.mult, ALU.add)\
                    .then_inc(s["ctx_done"], 1)

            def step(group, soft, added):
                n, q, fill = group
                base, par = n * G, q % 2

                def lo(j):
                    if following(group, j):
                        v.wait_ge(s["hi_done"], base + (j + 1))
                        nc.vector.tensor_sub(xT_lo[j % AHEAD][:, :, :].rearrange("p k t -> p (k t)"), pageT(j),
                                             xT_hi[j % AHEAD][:, :, :].bitcast(F32).rearrange("p k t -> p (k t)"))\
                            .then_inc(s["lo_done"], 1)

                if soft is None:
                    lo(0)
                    lo(1)
                for j in range(G):
                    lo(j + 2)
                    if added is not None and j == 0:
                        soft_context(added)
                    if soft is not None:
                        if j == 1:
                            soft_mean(soft[0], 1 - par)
                        if j == 3:
                            soft_scores(soft[0])
                        if j == 4:
                            soft_maxima(soft[0])
                        if j == 5:
                            soft_max(soft[0], soft[0] // PER_SEQ)
                        if j == 6:
                            soft_shift(soft[0])
                    v.wait_ge(s["sq_done"], base + (j + 1))
                    if j == 0:
                        ge(v, s["k_tot"], n * 2 - 1)
                    nc.vector.tensor_reduce(ksum[par][:, j, :], sq[j % 2][:, :].rearrange("p (h c) -> p h c", h=H), AX_X, ALU.add)\
                        .then_inc(s["summed"], 1)

            def last(soft, added):
                n = soft[0]
                soft_context(added)
                soft_mean(n, n % 2)
                soft_scores(n)
                soft_maxima(n)
                soft_max(n, n // PER_SEQ)
                soft_shift(n)
                soft_context(soft)

            groups(v, step, last)
            v.wait_ge(s["ctx_done"], GROUPS + 1)
            nc.vector.reciprocal(linv[:, :], ctxs[:, :, KVL:KVL + 1].rearrange("p b o -> p (b o)")).then_inc(s["final_inv"], 1)
            v.wait_ge(s["final_inv"], 1)
            nc.vector.tensor_mul(ctxs[:, :, 0:KVL], ctxs[:, :, 0:KVL], linv[:, :].unsqueeze(2).broadcast_to([HS, NSEQ, KVL]))\
                .then_inc(s["final_scaled"], 1)
            v.wait_ge(s["out_done"], 1)
            o = banks[0:VH, 1, 0:H * NS].rearrange("p (c a t) -> p c a t", a=2, t=NS)
            for a in range(2):
                nc.vector.tensor_copy(g.attnT[VH * a:VH * a + VH, :, TP:T], o[:, :, a, :]).then_inc(s["out_copied"], 1)
            v.wait_ge(s["out_copied"], 2)

        @block.tensor
        def _(pe):
            for opening in (*s["pages_free"], s["kn_done"], s["rp_done"]):
                pe.sem_inc(opening, 1)
            pe.wait_ge(s["w_loaded"], 16)
            for x in range(H * KL):
                h, k = x // KL, x % KL
                mm = pe.transpose(banks[0:NOPE, 2 + x // 4, (x % 4) * P:(x % 4 + 1) * P], wkv[:, k, h * KW:h * KW + NOPE],
                                  ident[:, :])
            mm.then_inc(s["wT_done"], 1)
            pe.wait_ge(s["wT_copied"], 1)
            for h in range(H):
                for k in range(KL):
                    at = k * H * NS + h * NS
                    mm = pe.matmul(banks[:, 0, at:at + NS], wukT[0:NOPE, h * KL + k, :], g.qs[0:NOPE, h, :], start=True, stop=True)
            mm.then_inc(s["qab_done"], 1)
            for k in range(KL):
                mm = pe.matmul(banks[0:NS, 1, :], g.new_latT[:, k, :], nope[:, k * H:(k + 1) * H, 0:NOPE],
                               start=k == 0, stop=k == KL - 1)
            mm.then_inc(s["kn0_done"], 1)
            pe.wait_ge(s["qab_copied"], KL)
            for k in range(KL):
                pe.matmul(banks[0:NS, 6, 0:NSEQ * HS], g.new_latT[:, k, :], qab[:, :, k, :], start=k == 0, stop=k == KL - 1)
            pe.matmul(banks[0:NS, 7, 0:NSEQ * HS], g.kpe[NOPE:QK, TP:T],
                      g.qs[NOPE:QK, :, :].rearrange("p h (b s) -> p b h s", s=SDEC), start=True, stop=True).then_inc(s["s0_done"], 1)
            pe.wait_ge(s["s0_steps"], 4)
            for b in range(NSEQ):
                mm = pe.transpose(banks[0:HS, 6, b * NS:(b + 1) * NS], st[0:NS, b, :], ident[0:NS, 0:NS])
            mm.then_inc(s["s0_transposed"], 1)
            pe.wait_ge(s["p0_done"], 1)
            for b in range(NSEQ):
                mm = pe.transpose(banks[0:NS, 7, b * HS:(b + 1) * HS], sc[0][0:HS, b, :], ident[0:HS, 0:HS])
            mm.then_inc(s["p0_transposed"], 1)
            pe.wait_ge(s["p0_copied"], 1)
            for b in range(NSEQ):
                mm = pe.matmul(banks[0:HS, 2 + b // 2, (b % 2) * KVL:(b % 2 + 1) * KVL], pr[0:NS, b, :], g.new_page[:, 0:KVL],
                               start=True, stop=True)
            mm.then_inc(s["ctx0_done"], 1)
            pe.wait_ge(s["ctx0_copied"], 1)

            def spread_max(n):
                pe.wait_ge(s["diag_done"], n + 1)
                pe.matmul(banks[:, 7, MB:MB + HS], g.ones[0:HS, :], diag[:, :], start=True, stop=True).then_inc(s["max_spread"], 1)

            def transpose_max(n):
                pe.wait_ge(s["maxed"], n + 1)
                ge(pe, s["ctx_done"], n + 1)
                pe.transpose(banks[0:HS, 7, MT:MT + P], mx[:, :], ident[:, :]).then_inc(s["max_transposed"], 1)

            def context(group):
                n, q, _ = group
                pe.wait_ge(s["exped"], n + 1)
                for j in range(G):
                    mm = pe.matmul(banks[0:HS, 7, CT:CT + KVL + 1], pr[:, j, :], X[q][:, j, 0:KVL + 1],
                                   start=j == 0, stop=j == G - 1)
                mm.then_inc(s["pages_free"][q], 1)

            def step(group, soft, _):
                n, q, fill = group
                base, par = n * G, q % 2

                def transposes(j):
                    page = following(group, j)
                    if page:
                        at, turn, place = page
                        if place == 0:
                            pe.wait_ge(loaded[at], turn * (16 * G) + 16 * G)
                        ge(pe, s["lo_done"], base + (j - 1))
                        for k in range(KL):
                            mm = pe.transpose(pageT(j)[:, k * P:(k + 1) * P], X[at][:, place, k * P:(k + 1) * P], ident[:, :])
                        mm.then_inc(s["x_transposed"], 1)

                def expand(j):
                    pe.wait_ge(s["lo_done"], base + (j + 1))
                    ge(pe, s["sq_done"], base + (j - 1))
                    ge(pe, s["sc_copied"], base + (j - 1))
                    for k in range(KL):
                        for x, w, a in ((xT_hi, comb_hi, 0), (xT_hi, comb_lo, 1), (xT_lo, comb_hi, 2)):
                            for half in range(2):
                                mm = pe.matmul(banks[:, 2 * (j % 2) + half, 0:WC], x[j % AHEAD][:, k, :], w[par][:, k, half, :],
                                               start=k == 0 and a == 0, stop=k == KL - 1 and a == 2)
                    mm.then_inc(s["kn_done"], 1)

                if soft is None:
                    transposes(0)
                    transposes(1)
                for j in range(G):
                    transposes(j + 2)
                    if j == 0:
                        pe.wait_ge(s["comb_ready"], n * 2 + 2)
                    if soft is not None:
                        if j == 5:
                            transpose_max(soft[0])
                        if j == 6:
                            spread_max(soft[0])
                    expand(j)
                    if j == 3:
                        pe.wait_ge(ropes_loaded[q], fill * (16 * G) + 16 * G)
                        ge(pe, s["s_added"], n + 1)
                        for x in range(2):
                            mm = pe.transpose(banks[:, 6, x * P:(x + 1) * P], R[q][:, x * P:(x + 1) * P], ident[:, :])
                        mm.then_inc(s["r_transposed"], 1)
                    if j == 6:
                        pe.wait_ge(s["r_copied"], n + 1)
                        pe.wait_ge(s["qbd_ready"], n + 1)
                        for x in range(2):
                            mm = pe.matmul(banks[:, 6, (2 + x) * P:(3 + x) * P], rT[:, x * P:(x + 1) * P],
                                           qbd[par][:, :, :].rearrange("p a b -> p (a b)"), start=True, stop=True)
                        mm.then_inc(s["rp_done"], 1)
                if soft is not None:
                    context(soft)

            def last(soft, _):
                transpose_max(soft[0])
                spread_max(soft[0])
                context(soft)

            groups(pe, step, last)
            pe.wait_ge(s["final_scaled"], 1)
            for k in range(KL):
                for b in range(NSEQ):
                    at = (k * NSEQ + b) * HS
                    mm = pe.transpose(banks[:, 0, at:at + HS], ctxs[:, b, k * P:(k + 1) * P], ident[0:HS, 0:HS])
            mm.then_inc(s["ctxT_done"], 1)
            pe.wait_ge(s["ctxT_copied"], 1)
            cT = wukT[:, 0:2 * NSEQ * HS // P, :].rearrange("p a b -> p (a b)")\
                .rearrange("p (k b h s) -> p k b h s", k=KL, b=NSEQ, h=H)
            for h in range(H):
                for k in range(KL):
                    mm = pe.matmul(banks[0:VH, 1, h * NS:(h + 1) * NS], wkv[:, k, h * KW + NOPE:(h + 1) * KW], cT[:, k, :, h, :],
                                   start=k == 0, stop=k == KL - 1)
            mm.then_inc(s["out_done"], 1)


def output_projection(g):
    nc, A, sem, zT, banks = g.nc, g.A, g.sem, g.zT, g.banks
    top = Arena(nc, g.h_at, g.top)
    mix_hi, mix_lo = top.take("mix_hi", [P, KD, TT], F32R), top.take("mix_lo", [P, KD, TT], F32R)
    ar = Arena(nc, g.z_hc_at, g.h_at)
    scr = norm_scratch("mix_norms", ar)
    ring = Ring(sem, "w_o", ar, KD)
    conv = Norm(nc, sem, "convnorm", scr, lambda c: zT[:, Z_GB + c, :], KC, CW,
                lambda c: g.gcol[:, G_CONV + c:G_CONV + c + 1], lambda c: mix_hi[:, KC + c, :],
                lambda c: mix_lo[:, KC + c, :], banks[:, 0:3, :], g.ones)
    att = Norm(nc, sem, "attnorm", scr, lambda c: g.attnT[:, c, :], KC, AW,
               lambda c: g.gcol[:, G_ATT + c:G_ATT + c + 1], lambda c: mix_hi[:, c, :],
               lambda c: mix_lo[:, c, :], banks[:, 3:6, :], g.ones)
    w = A["w_o"].rearrange("(k p) n -> p k n", p=P)

    with nc.Block() as block:
        @block.sync
        def _(sp):
            with sp.Fori(0, KD // 2) as i:
                for s in range(2):
                    sp.wait_ge(ring.lo_done[s], i + 1)
                    sp.dma_start(ring.raw[s][:, :, :], w[:, :, ds(i * (2 * P) + s * P, P)]).then_inc(ring.loaded[s], 16)

        @block.scalar
        def _(act):
            conv.act(act)
            att.act(act)
            with act.Fori(0, KD // 2) as i:
                for s in range(2):
                    ring.split_hi(act, s, i)

        @block.gpsimd
        def _(pool):
            ring.open(pool, ring.lo_done)
            conv.pool(pool)
            att.pool(pool)
            with pool.Fori(0, KD // 2) as i:
                for s in range(2):
                    ring.split_lo(nc, pool, s, i)

        @block.tensor
        def _(pe):
            ring.open(pe, ring.used)
            conv.pe(pe)
            att.pe(pe)
            pe.wait_ge(att.lo_done, KC)
            pe.wait_ge(conv.lo_done, KC)
            pe.wait_ge(conv.mean, 1)
            pe.wait_ge(att.mean, 1)
            with pe.Fori(0, KD // 2) as i:
                for s in range(2):
                    pe.wait_ge(ring.evacuated[s], i + 1)
                    ring.products(pe, s, i, banks[:, 3 * s:3 * s + 3, :],
                                  lambda k: mix_hi[:, k, :], lambda k: mix_lo[:, k, :])

        @block.vector
        def _(v):
            ring.open(v, ring.evacuated)
            conv.dve(v)
            v.wait_ge(conv.lo_done, KC)
            v.wait_ge(conv.norm, KC)
            att.dve(v)
            with v.Fori(0, KD // 2) as i:
                for s in range(2):
                    v.wait_ge(ring.used[s], i + 2)
                    x = g.xT[:, ds(i * 2 + s, 1), :].rearrange("p o (b t) -> p (o b) t", b=NBLK)
                    nc.vector.tensor_add(x, x, banks[:, 3 * s:3 * s + 3, 0:TB]).then_inc(ring.evacuated[s], 1)


def mlp(g):
    nc, A, sem, banks, xT = g.nc, g.A, g.sem, g.banks, g.xT
    FC = 4
    GROUPS = DFF // (FC * P)
    top = Arena(nc, g.h_at, g.top)
    hf_hi, hf_lo = top.take("hf_hi", [P, KD, TT], F32R), top.take("hf_lo", [P, KD, TT], F32R)
    ar = Arena(nc, g.start, g.h_at)
    a_hi, a_lo = ar.take("a_hi", [P, FC, TT], F32R), ar.take("a_lo", [P, FC, TT], F32R)
    up = Ring(sem, "w_up", ar, KD)
    down = Ring(sem, "w_down", ar, FC)
    scr = norm_scratch("ffn_norm", ar)
    norm = Norm(nc, sem, "ffnnorm", scr, lambda c: xT[:, c, :], KD, D, lambda c: g.gcol[:, G_FFN + c:G_FFN + c + 1],
                lambda c: hf_hi[:, c, :], lambda c: hf_lo[:, c, :], banks[:, 0:3, :], g.ones)
    relu, full = scr[0], scr[2]
    relu_done = sem("relu_done")
    hi_done, sq_done, act_ready = sem("a_hi_done"), sem("a_squared"), sem("a_ready")
    w_up = A["w_up"].rearrange("(k p) n -> p k n", p=P)
    w_down = A["w_down"].rearrange("(g k p) n -> p g k n", k=FC, p=P)
    per = KD // 2

    with nc.Block() as block:
        @block.sync
        def _(sp):
            with sp.Fori(0, GROUPS) as i:
                for f in range(FC):
                    s = f % 2
                    sp.wait_ge(up.lo_done[s], i * (FC // 2) + (f // 2 + 1))
                    sp.dma_start(up.raw[s][:, :, :], w_up[:, :, ds(i * (FC * P) + f * P, P)])\
                        .then_inc(up.loaded[s], 16)
                for m in range(KD):
                    s = m % 2
                    sp.wait_ge(down.lo_done[s], i * per + (m // 2 + 1))
                    sp.dma_start(down.raw[s][:, :, :],
                                 w_down[:, ds(i, 1), :, m * P:(m + 1) * P].rearrange("p o k n -> p (o k) n"))\
                        .then_inc(down.loaded[s], 16)

        @block.scalar
        def _(act):
            norm.act(act)
            act.wait_ge(norm.lo_done, KD)
            with act.Fori(0, GROUPS) as i:
                up.split_hi(act, 0, i * 2)
                for f in range(FC):
                    if f + 1 < FC:
                        up.split_hi(act, (f + 1) % 2, i * 2 + (f + 1) // 2)
                    else:
                        down.split_hi(act, 0, i * per)
                    act.wait_ge(up.used[f % 2], i * 2 + (f // 2 + 2))
                    act.wait_ge(act_ready, i * FC + max(f, 1))
                    act.activation(relu[:, f % 2, :].rearrange("p (b t) -> p b t", b=NBLK),
                                   banks[:, 3 * (f % 2):3 * (f % 2) + 3, 0:TB], ACT.Relu)\
                        .then_inc(up.evacuated[f % 2], 1)
                    act.wait_ge(up.evacuated[f % 2], i * 2 + (f // 2 + 1))
                    act.activation(a_hi[:, f, :], relu[:, f % 2, :], ACT.Square).then_inc(hi_done, 1)
                for m in range(1, KD):
                    down.split_hi(act, m % 2, i * per + m // 2)

        @block.gpsimd
        def _(pool):
            up.open(pool, up.lo_done)
            down.open(pool, down.lo_done)
            norm.pool(pool)
            with pool.Fori(0, GROUPS) as i:
                for f in range(FC):
                    up.split_lo(nc, pool, f % 2, i * 2 + f // 2)
                for m in range(KD):
                    down.split_lo(nc, pool, m % 2, i * per + m // 2)

        @block.tensor
        def _(pe):
            up.open(pe, up.used)
            down.open(pe, down.used)
            norm.pe(pe)
            pe.wait_ge(norm.lo_done, KD)
            pe.wait_ge(norm.mean, 1)
            with pe.Fori(0, GROUPS) as i:
                for f in range(FC):
                    s = f % 2
                    if f < 2:
                        pe.wait_ge(down.evacuated[s], i * per + 1)
                    else:
                        pe.wait_ge(up.evacuated[s], i * 2 + 1)
                    up.products(pe, s, i * 2 + f // 2, banks[:, 3 * s:3 * s + 3, :],
                                lambda k: hf_hi[:, k, :], lambda k: hf_lo[:, k, :])
                for m in range(KD):
                    s = m % 2
                    if m < 2:
                        pe.wait_ge(up.evacuated[s], i * 2 + 2)
                    else:
                        pe.wait_ge(down.evacuated[s], i * per + (m // 2 + 1))

                    def hidden(k, m=m):
                        if m == 0:
                            pe.wait_ge(act_ready, i * FC + (k + 2))
                    down.products(pe, s, i * per + m // 2, banks[:, 3 * s:3 * s + 3, :],
                                  lambda k: a_hi[:, k, :], lambda k: a_lo[:, k, :], first=hidden)

        @block.vector
        def _(v):
            down.open(v, down.evacuated)
            down.open(v, [act_ready])
            norm.dve(v)
            v.wait_ge(norm.lo_done, KD)
            v.wait_ge(norm.norm, KD)
            with v.Fori(0, GROUPS) as i:
                for f in range(FC):
                    s = f % 2
                    v.wait_ge(up.evacuated[s], i * 2 + (f // 2 + 1))
                    v.wait_ge(act_ready, i * FC + max(f, 1))
                    nc.vector.tensor_mul(full[:, s, :], relu[:, s, :], relu[:, s, :]).then_inc(sq_done, 1)
                    v.wait_ge(sq_done, i * FC + (f + 1))
                    v.wait_ge(hi_done, i * FC + (f + 1))
                    nc.vector.tensor_sub(a_lo[:, f, :], full[:, s, :], a_hi[:, f, :].bitcast(F32))\
                        .then_inc(act_ready, 1)
                for m in range(KD):
                    s = m % 2
                    v.wait_ge(down.used[s], i * per + (m // 2 + 2))
                    v.wait_ge(down.evacuated[s], i * per + (m // 2 + 1))
                    x = xT[:, m, :].rearrange("p (b t) -> p b t", b=NBLK)
                    nc.vector.tensor_add(x, x, banks[:, 3 * s:3 * s + 3, 0:TB]).then_inc(down.evacuated[s], 1)


def store_outputs(g):
    nc, A, sem, banks, xT = g.nc, g.A, g.sem, g.banks, g.xT
    ar = Arena(nc, g.start, g.top)
    y = [ar.take(f"y_tile{i}", [P, D], F32) for i in range(3)]
    tiles = [(META + t * P, P, A["out_y_prompt"][t * P:(t + 1) * P, :]) for t in range(SEQ // P)]
    tiles.append((TP, NS, A["out_y_sample"]))
    transposed, low_copied, high_copied = sem("y_transposed"), sem("y_low_copied"), sem("y_high_copied")
    stored = [sem(f"y_stored{i}") for i in range(3)]

    with nc.Block() as block:
        @block.tensor
        def _(pe):
            for t, (at, n, _) in enumerate(tiles):
                if t >= 4:
                    pe.wait_ge(low_copied, t - 3)
                    pe.wait_ge(high_copied, t - 3)
                for k in range(KD):
                    mm = pe.transpose(banks[0:n, 2 * (t % 4) + k // 4, (k % 4) * P:(k % 4 + 1) * P],
                                      xT[:, k, at:at + n], g.ident[:, :])
                mm.then_inc(transposed, 1)

        @block.scalar
        def _(act):
            for t, (at, n, _) in enumerate(tiles):
                act.wait_ge(transposed, t + 1)
                if t >= 3:
                    act.wait_ge(stored[t % 3], 16 * (t // 3))
                act.copy(y[t % 3][0:n, 0:BANK], banks[0:n, 2 * (t % 4), :]).then_inc(low_copied, 1)

        @block.vector
        def _(v):
            for t, (at, n, _) in enumerate(tiles):
                v.wait_ge(transposed, t + 1)
                if t >= 3:
                    v.wait_ge(stored[t % 3], 16 * (t // 3))
                nc.vector.tensor_copy(y[t % 3][0:n, BANK:D], banks[0:n, 2 * (t % 4) + 1, :]).then_inc(high_copied, 1)

        @block.sync
        def _(sp):
            for t, (at, n, out) in enumerate(tiles):
                sp.wait_ge(low_copied, t + 1)
                sp.wait_ge(high_copied, t + 1)
                sp.dma_start(out, y[t % 3][0:n, :]).then_inc(stored[t % 3], 16)
            for i in range(3):
                sp.wait_ge(stored[i], 16 * len(tiles[i::3]))


_OUTS = [("y_prompt", (SEQ, D)), ("y_sample", (NS, D)), ("new_lat_prompt", (TP, KVL)), ("new_kpe_prompt", (TP, ROPE)),
         ("new_conv_prompt", (2, CW)), ("new_lat_sample", (NS, KVL)), ("new_kpe_sample", (NS, ROPE)),
         ("new_conv_sample", (NSEQ, 2, CW))]


def rope_tables():
    import numpy as np
    inv = (np.float32(10000.0) ** (-(np.arange(0, ROPE, 2, dtype=np.float32) / np.float32(ROPE)))).astype(np.float32)
    pos = np.concatenate([np.arange(TP), np.tile(PAST + np.arange(SDEC), NSEQ)]).astype(np.float32)
    ang = pos[None, :] * inv[:, None]
    out = np.zeros((2 * ROPE, TT), np.float32)
    c, s = np.cos(ang), np.sin(ang)
    out[:, :T] = np.concatenate([c, c, -s, s], axis=0)
    return out, np.ascontiguousarray(np.concatenate([c, s], axis=0).T)


def kernel(x_prompt, x_sample, cache_kv_latent, cache_k_rope, state_conv, page_table, meta_tokens,
           norm_mix_g, w_in, q_lora_g, kv_lora_g, w_uq, w_ukv, q_norm_g, k_norm_g, conv_w, conv_b,
           attn_out_g, conv_out_g, w_o, norm_ffn_g, w_up, w_down):
    import numpy as np
    from concourse import bacc
    from concourse.bass_utils import run_bass_kernel_spmd

    nc = bacc.Bacc("TRN2", target_bir_lowering=False, num_devices=1)
    given = dict(x_prompt=x_prompt, x_sample=x_sample, cache_kv_latent=cache_kv_latent, cache_k_rope=cache_k_rope,
                 state_conv=state_conv, page_table=page_table, meta_tokens=meta_tokens, norm_mix_g=norm_mix_g,
                 w_in=w_in, q_lora_g=q_lora_g, kv_lora_g=kv_lora_g, w_uq=w_uq, w_ukv=w_ukv, q_norm_g=q_norm_g,
                 k_norm_g=k_norm_g, conv_w=conv_w, conv_b=conv_b, attn_out_g=attn_out_g, conv_out_g=conv_out_g,
                 w_o=w_o, norm_ffn_g=norm_ffn_g, w_up=w_up, w_down=w_down)
    npool = cache_kv_latent.shape[1]
    shapes = dict(x_prompt=(SEQ, D), x_sample=(NS, D), cache_kv_latent=(npool, PAGE, KVL),
                  cache_k_rope=(npool, PAGE, ROPE), state_conv=(NSEQ * 2, CW), page_table=(1, NSEQ * NPAGES),
                  norm_mix_g=(D,), w_in=w_in.shape[1:], q_lora_g=(QL,), kv_lora_g=(KVL,), w_uq=w_uq.shape[1:],
                  w_ukv=w_ukv.shape[1:], q_norm_g=(QK,), k_norm_g=(QK,), conv_w=(3 * CW,), conv_b=(CW,),
                  attn_out_g=(AW,), conv_out_g=(CW,), w_o=(D, D), norm_ffn_g=(D,), w_up=(D, DFF), w_down=(DFF, D))
    arrays, A = {}, {}
    given["rope_table"], given["rope_rows"] = rope_tables()
    for name, a in given.items():
        a = np.ascontiguousarray(np.asarray(a)).reshape(shapes.get(name, np.shape(a)))
        arrays[f"in_{name}"] = a
        A[name] = nc.dram_tensor(f"in_{name}", a.shape, mybir.dt.from_np(a.dtype), kind="ExternalInput").ap()
    for name, shape in _OUTS:
        A["out_" + name] = nc.dram_tensor(f"out_{name}", shape, F32, kind="ExternalOutput").ap()
    program(nc, A)
    r = run_bass_kernel_spmd(nc, [arrays], core_ids=[0])
    o = r.results[0]
    return (o["out_y_prompt"].reshape(1, SEQ, D), o["out_y_sample"].reshape(NSEQ, SDEC, D),
            o["out_new_lat_prompt"].reshape(1, 1, TP, KVL), o["out_new_kpe_prompt"].reshape(1, 1, TP, ROPE),
            o["out_new_conv_prompt"].reshape(1, 1, 2, CW), o["out_new_lat_sample"].reshape(1, NSEQ, SDEC, KVL),
            o["out_new_kpe_sample"].reshape(1, NSEQ, SDEC, ROPE), o["out_new_conv_sample"].reshape(1, NSEQ, 2, CW))
```
